# Optimizing a Trainium2 kernel written in Bass

```python
import jax, jax.numpy as jnp
from jax import lax
import numpy as np

D_MODEL = 1024
BATCH = 1
SEQ = 2048
DEPTH = 1
DEC_BATCH = 1
DEC_SEQ = 32
PAST_LEN = 1024

CHUNK = 64
MIX_WIDTH = D_MODEL
SB_WIDTH = MIX_WIDTH // 2
SB_HEAD_DIM = 64
SB_HEADS = SB_WIDTH // SB_HEAD_DIM
POOL_WIDTH = MIX_WIDTH - SB_WIDTH
POOL_WINDOWS = (2, 4, 8, 16)
POOL_GROUPS = len(POOL_WINDOWS)
POOL_GC = POOL_WIDTH // POOL_GROUPS
POOL_HIST = max(POOL_WINDOWS) - 1
IN_WIDTH = 3 * SB_WIDTH + POOL_WIDTH
D_FF = -(-8 * D_MODEL // (3 * 256)) * 256
Q_BLOCK = 128
ALPHA = (2 * DEPTH) ** 0.25
BETA = (8 * DEPTH) ** -0.25
LN_EPS = 1e-5

kernel_name = "stickbreak_pool_hybrid_stream_step"

def _layer_norm(x, g, b):
    xf = x.astype(jnp.float32)
    mu = jnp.mean(xf, axis=-1, keepdims=True)
    var = jnp.mean(jnp.square(xf - mu), axis=-1, keepdims=True)
    return ((xf - mu) * lax.rsqrt(var + LN_EPS) * g.astype(jnp.float32) + b.astype(jnp.float32)).astype(x.dtype)

def _sb_block(qb, qpos, k, v, kpos):
    z = jnp.einsum('bqhd,bkhd->bhqk', qb.astype(jnp.float32), k.astype(jnp.float32)) * (SB_HEAD_DIM ** -0.5)
    mask = kpos[None, :] < qpos[:, None]
    log_beta = jax.nn.log_sigmoid(z)
    log_1m = jnp.where(mask, log_beta - z, 0.0)
    after = lax.cumsum(log_1m, axis=3, reverse=True) - log_1m
    a = jnp.where(mask, jnp.exp(log_beta + after), 0.0)
    return jnp.einsum('bhqk,bkhd->bqhd', a, v.astype(jnp.float32))

def _stick_breaking(q, k, v, q_start):
    B, T, H, dh = q.shape
    qbs = min(Q_BLOCK, T)
    nblk = T // qbs
    qpos = q_start + jnp.arange(T, dtype=jnp.int32)
    kpos = jnp.arange(k.shape[1], dtype=jnp.int32)
    qs = q.reshape(B, nblk, qbs, H, dh).transpose(1, 0, 2, 3, 4)
    ps = qpos.reshape(nblk, qbs)
    out = lax.map(lambda a: _sb_block(a[0], a[1], k, v, kpos), (qs, ps))
    return out.transpose(1, 0, 2, 3, 4).reshape(B, T, H * dh)

def _pool_mix(u, hist, start_pos, pool_w, pool_scale):
    B, T, C = u.shape
    ue = jnp.concatenate([hist.astype(jnp.float32), u.astype(jnp.float32)], axis=1)
    csum = jnp.concatenate([jnp.zeros((B, 1, C), jnp.float32), jnp.cumsum(ue, axis=1)], axis=1)
    pos = start_pos + jnp.arange(T, dtype=jnp.int32)
    P = POOL_HIST
    diffs = []
    for g, w in enumerate(POOL_WINDOWS):
        lo_c, hi_c = g * POOL_GC, (g + 1) * POOL_GC
        hi = csum[:, P + 1:P + 1 + T, lo_c:hi_c]
        lo = csum[:, P + 1 - w:P + 1 - w + T, lo_c:hi_c]
        cnt = jnp.minimum(w, pos + 1).astype(jnp.float32)[None, :, None]
        diffs.append((hi - lo) / cnt - ue[:, P:, lo_c:hi_c])
    d = jnp.stack(diffs, axis=2)
    y = jnp.einsum('btgc,gcd->btgd', d, pool_w.astype(jnp.float32)).reshape(B, T, C)
    y = y * pool_scale.astype(jnp.float32)
    return y.astype(u.dtype), ue[:, -P:].astype(u.dtype)

def _layer(x, k_hist, v_hist, pool_hist, start_pos, w_in, pool_w, pool_scale, w_out,
           ln1_g, ln1_b, w_gate, w_up, w_down, ln2_g, ln2_b):
    B, T, _ = x.shape
    h = x @ w_in
    q = h[..., :SB_WIDTH].reshape(B, T, SB_HEADS, SB_HEAD_DIM)
    k = h[..., SB_WIDTH:2 * SB_WIDTH].reshape(B, T, SB_HEADS, SB_HEAD_DIM)
    v = h[..., 2 * SB_WIDTH:3 * SB_WIDTH].reshape(B, T, SB_HEADS, SB_HEAD_DIM)
    u = h[..., 3 * SB_WIDTH:]
    k_all = jnp.concatenate([k_hist.astype(k.dtype), k], axis=1)
    v_all = jnp.concatenate([v_hist.astype(v.dtype), v], axis=1)
    a_out = _stick_breaking(q, k_all, v_all, start_pos).astype(x.dtype)
    p_out, new_pool = _pool_mix(u, pool_hist, start_pos, pool_w, pool_scale)
    mix = jnp.concatenate([a_out, p_out], axis=-1) @ w_out
    x1 = _layer_norm(ALPHA * x + mix, ln1_g, ln1_b)
    ffn = (jax.nn.silu(x1 @ w_gate) * (x1 @ w_up)) @ w_down
    y = _layer_norm(ALPHA * x1 + ffn, ln2_g, ln2_b)
    return y, k, v, new_pool

def setup_inputs(seed: int = 0) -> dict:
    key = jax.random.key(seed)
    ks = jax.random.split(key, 16)
    f32 = jnp.float32
    nrm = lambda k_, s: jax.random.normal(k_, s, f32)
    col_scale = jnp.concatenate([jnp.ones((2 * SB_WIDTH,), f32), jnp.full((SB_WIDTH,), BETA, f32),
                                 jnp.ones((POOL_WIDTH,), f32)])
    return {
        "x_prompt": nrm(ks[0], (BATCH, SEQ, D_MODEL)),
        "x_sample": nrm(ks[1], (DEC_BATCH, DEC_SEQ, D_MODEL)),
        "cache_k": nrm(ks[2], (DEC_BATCH, PAST_LEN, SB_HEADS, SB_HEAD_DIM)),
        "cache_v": nrm(ks[3], (DEC_BATCH, PAST_LEN, SB_HEADS, SB_HEAD_DIM)) * BETA,
        "state_pool": nrm(ks[4], (DEC_BATCH, POOL_HIST, POOL_WIDTH)),
        "w_in": nrm(ks[5], (D_MODEL, IN_WIDTH)) * (D_MODEL ** -0.5) * col_scale[None, :],
        "pool_w": nrm(ks[6], (POOL_GROUPS, POOL_GC, POOL_GC)) * (POOL_GC ** -0.5),
        "pool_scale": 1.0 + 0.02 * nrm(ks[7], (POOL_WIDTH,)),
        "w_out": nrm(ks[8], (MIX_WIDTH, D_MODEL)) * (MIX_WIDTH ** -0.5) * BETA,
        "ln1_g": 1.0 + 0.02 * nrm(ks[9], (D_MODEL,)),
        "ln1_b": 0.02 * nrm(ks[10], (D_MODEL,)),
        "w_gate": nrm(ks[11], (D_MODEL, D_FF)) * (D_MODEL ** -0.5),
        "w_up": nrm(ks[12], (D_MODEL, D_FF)) * (D_MODEL ** -0.5) * BETA,
        "w_down": nrm(ks[13], (D_FF, D_MODEL)) * (D_FF ** -0.5) * BETA,
        "ln2_g": 1.0 + 0.02 * nrm(ks[14], (D_MODEL,)),
        "ln2_b": 0.02 * nrm(ks[15], (D_MODEL,)),
    }

def reference(x_prompt, x_sample, cache_k, cache_v, state_pool, w_in, pool_w, pool_scale, w_out,
              ln1_g, ln1_b, w_gate, w_up, w_down, ln2_g, ln2_b):
    Bp = x_prompt.shape[0]
    yp = x_prompt
    ys = x_sample
    for _ in range(DEPTH):
        k_hist0 = jnp.zeros((Bp, 0, SB_HEADS, SB_HEAD_DIM), x_prompt.dtype)
        pool_hist0 = jnp.zeros((Bp, POOL_HIST, POOL_WIDTH), x_prompt.dtype)
        yp, k_p, v_p, pool_p = _layer(yp, k_hist0, k_hist0, pool_hist0, 0, w_in, pool_w, pool_scale, w_out,
                                      ln1_g, ln1_b, w_gate, w_up, w_down, ln2_g, ln2_b)
        ys, k_s, v_s, pool_s = _layer(ys, cache_k, cache_v, state_pool, cache_k.shape[1], w_in, pool_w,
                                      pool_scale, w_out, ln1_g, ln1_b, w_gate, w_up, w_down, ln2_g, ln2_b)
    return (yp, ys, k_p, v_p, pool_p, k_s, v_s, pool_s)


_drawn_inputs = setup_inputs


def setup_inputs(seed=0):
    import zlib

    import numpy as np

    out = dict(_drawn_inputs(seed))
    spreads = {}
    factors = {'cache_k': 20.968,
     'pool_scale': 22.05,
     'ln1_g': 2.813,
     'ln1_b': 2.873,
     'ln2_g': 8.238,
     'ln2_b': 8.231,
     'cache_v': 4.312}
    for name, (base, spread) in spreads.items():
        noise = np.random.default_rng([zlib.crc32(name.encode()), seed]).standard_normal(out[name].shape)
        drawn = base * np.exp(spread * noise) if base else spread * noise
        out[name] = __import__('jax').numpy.asarray(drawn.astype(out[name].dtype))
    for name, factor in factors.items():
        out[name] = (out[name] * factor).astype(out[name].dtype)
    return out
```

```python
from contextlib import ExitStack, contextmanager

import concourse.bass as bass
from concourse import mybir

F32 = mybir.dt.float32
F32R = mybir.dt.float32r
I32 = mybir.dt.int32
ALU = mybir.AluOpType
ACT = mybir.ActivationFunctionType

P = 128
D = 1024
KD = D // P
SEQ = 2048
DEC = 32
TOK = SEQ + DEC
PT = SEQ // P
PAST = 1024
CT = PAST // P
SBW = 512
HEADS = 8
HD = 64
HC = SBW // P
WINDOWS = (2, 4, 8, 16)
HIST = 15
FF = 2816
FC = FF // P
ALPHA = 2.0 ** 0.25
EPS = 1e-5
PRIME = 96
NEG = -(2.0 ** 100)
TB = 416
NB = TOK // TB

ITEMS = [(q, c, 512 if c < q // 4 else (q % 4 + 1) * P) for q in range(PT) for c in range(q // 4, -1, -1)]
NI = len(ITEMS)


def r32(ap):
    return ap.bitcast(F32)


def build(nc, x_prompt, x_sample, cache_k, cache_v, state_pool, w_in, pool_w, pool_scale, w_out,
          ln1_g, ln1_b, w_gate, w_up, w_down, ln2_g, ln2_b,
          y_prompt, y_sample, k_prompt, v_prompt, pool_prompt, k_sample, v_sample, pool_sample):
    xp = x_prompt.rearrange("a t d -> (a t) d")
    xs = x_sample.rearrange("a t d -> (a t) d")
    ck = cache_k.rearrange("a t h d -> (a t) (h d)")
    cv = cache_v.rearrange("a t h d -> (a t) (h d)")
    sp = state_pool.rearrange("a t c -> (a t) c")
    yp = y_prompt.rearrange("a t d -> (a t) d")
    ys = y_sample.rearrange("a t d -> (a t) d")
    kp_out = k_prompt.rearrange("a t h d -> (a t) (h d)")
    vp_out = v_prompt.rearrange("a t h d -> (a t) (h d)")
    ks_out = k_sample.rearrange("a t h d -> (a t) (h d)")
    vs_out = v_sample.rearrange("a t h d -> (a t) (h d)")
    pp_out = pool_prompt.rearrange("a t c -> (a t) c")
    ps_out = pool_sample.rearrange("a t c -> (a t) c")

    qT_d = nc.dram_tensor("qT_scratch", [2, SBW, TOK], F32R).ap()
    kT_d = nc.dram_tensor("kT_scratch", [2, SBW, TOK], F32R).ap()
    kcT_d = nc.dram_tensor("kcT_scratch", [2, SBW, PAST], F32R).ap()
    v_d = nc.dram_tensor("v_scratch", [TOK, HEADS, 2, HD], F32R).ap()
    vc_d = nc.dram_tensor("vc_scratch", [PAST, HEADS, 2, HD], F32R).ap()
    mixT_d = nc.dram_tensor("mixT_scratch", [2, D, TOK], F32R).ap()

    top = ExitStack()
    used = []

    def sem(n):
        used.append(nc.alloc_semaphore(name=n))
        return used[-1]

    @contextmanager
    def phase():
        with ExitStack() as ctx:
            yield ctx
            with nc.Block() as block:
                @block.sync
                def _(sp):
                    for x in used:
                        sp.sem_clear(x)
            for x in used:
                nc.release_semaphore(x)
            used.clear()

    def sb(ctx, n, shape, dt=F32):
        return ctx.enter_context(nc.sbuf_tensor(n, shape, dt))

    with top:
        passed = nc.alloc_semaphore(name="passed")
        bank = [top.enter_context(nc.psum_tensor(f"bank{i}", [P, 512], F32)) for i in range(8)]
        ident = sb(top, "ident", [P, P])
        ident_r = sb(top, "ident_r", [P, P], F32R)
        mask = sb(top, "mask", [P, P])
        mask_r = sb(top, "mask_r", [P, P], F32R)
        maskd_r = sb(top, "maskd_r", [P, P], F32R)
        eps_t = sb(top, "eps_t", [P, 1])

        constants(nc, sem, ident, ident_r, mask, mask_r, maskd_r, eps_t)
        with phase() as ctx:
            xT = [sb(ctx, f"xT{j}", [P, KD, TOK], F32R) for j in range(2)]
            transpose_x(nc, ctx, sem, sb, passed, bank, ident, xp, xs, xT)
            project(nc, ctx, sem, sb, passed, bank, ident, xT, w_in, sp, pool_w, pool_scale,
                    qT_d, kT_d, v_d, mixT_d, kp_out, vp_out, ks_out, vs_out, pp_out, ps_out)
        with phase() as ctx:
            split_cache(nc, ctx, sem, sb, passed, bank, ident, ck, cv, kcT_d, vc_d)
        with phase() as ctx:
            attend_prompt(nc, ctx, sem, sb, passed, bank, ident, ident_r, mask_r, qT_d, kT_d, v_d, mixT_d)
        with phase() as ctx:
            attend_sample(nc, ctx, sem, sb, passed, bank, ident, ident_r, maskd_r,
                          qT_d, kT_d, kcT_d, v_d, vc_d, mixT_d)
        for blk in range(2):
            tiles = 8 + blk
            width = 1024 + DEC * blk
            with ExitStack() as ctx:
                x1T = [sb(ctx, f"x1T{j}_{blk}", [P, KD, width], F32R) for j in range(2)]
                acc = sb(ctx, f"acc_{blk}", [P, tiles, D])
                with phase() as inner:
                    mix_norm(nc, inner, sem, sb, passed, bank, ident, eps_t, blk, xp, xs, mixT_d, w_out,
                             ln1_g, ln1_b, x1T, acc)
                with phase() as inner:
                    ffn(nc, inner, sem, sb, passed, bank, blk, width, tiles, w_gate, w_up, w_down, x1T, acc)
                with phase() as inner:
                    final_norm(nc, inner, sem, sb, passed, eps_t, blk, acc, ln2_g, ln2_b, yp, ys)


def constants(nc, sem, ident, ident_r, mask, mask_r, maskd_r, eps_t):
    filled, made, cast = sem("c_filled"), sem("c_made"), sem("c_cast")
    with nc.Block() as block:
        @block.scalar
        def _(act):
            act.preload_act_table_set("natural_log_exp_and_others")

        @block.gpsimd
        def _(pool):
            pool.memset(ident[:], 0.0).then_inc(filled, 1)
            pool.memset(mask[:], 0.0).then_inc(filled, 1)
            pool.wait_ge(filled, 2)
            pool.affine_select(out=ident[:], in_=ident[:], compare_op=ALU.not_equal, fill=1.0, base=0,
                               pattern=[[-1, P]], channel_multiplier=1).then_inc(made, 1)
            pool.affine_select(out=mask[:], in_=mask[:], compare_op=ALU.is_gt, fill=NEG, base=0,
                               pattern=[[-1, P]], channel_multiplier=1).then_inc(made, 1)

        @block.vector
        def _(dve):
            dve.memset(eps_t[:], EPS)
            dve.memset(r32(maskd_r[:]), NEG).then_inc(cast, 1)
            dve.wait_ge(made, 2)
            dve.wait_ge(cast, 1)
            dve.tensor_copy(ident_r[:], ident[:])
            dve.tensor_copy(mask_r[:], mask[:])
            for h in range(4):
                s = slice(DEC * h, DEC * h + DEC)
                dve.tensor_copy(maskd_r[s, 0:DEC], mask[s, s])


def transpose_x(nc, ctx, sem, sb, passed, bank, ident, xp, xs, xT):
    with ExitStack() as mem:
        xin = [sb(mem, f"xin{u}", [P, D]) for u in range(2)]
        loaded = [sem(f"x_loaded{u}") for u in range(2)]
        turned, hi_done, lo_done = sem("x_turned"), sem("x_hi"), sem("x_lo")

        def ps(u):
            return bank[2 * u], bank[2 * u + 1]

        with nc.Block() as block:
            @block.sync
            def _(sp):
                with sp.Fori(0, PT // 2) as i:
                    for u in range(2):
                        sp.wait_ge(turned, 2 * i + u - 1 + PRIME)
                        sp.sem_inc(passed, 1)
                        sp.dma_start(xin[u][:], xp[bass.ds((2 * i + u) * P, P), :]).then_inc(loaded[u], 16)
                sp.wait_ge(turned, PT - 1 + PRIME)
                sp.dma_start(xin[0][0:DEC, :], xs).then_inc(loaded[0], 16)

            @block.tensor
            def _(pe):
                pe.sem_inc(turned, PRIME)

                def turn(t, u, rows, times):
                    pe.wait_ge(loaded[u], 16 * times)
                    pe.wait_ge(lo_done, t - 1 + PRIME)
                    for k in range(KD):
                        m = pe.transpose(ps(u)[k // 4][:, (k % 4) * P:(k % 4) * P + rows],
                                         xin[u][0:rows, k * P:(k + 1) * P], ident[0:rows, 0:rows])
                    m.then_inc(turned, 1)

                with pe.Fori(0, PT // 2) as i:
                    for u in range(2):
                        turn(2 * i + u, u, P, i + 1)
                turn(PT, 0, DEC, PT // 2 + 1)

            def halves(t, u, rows):
                for b in range(2):
                    yield b, ps(u)[b][:, :].rearrange("p (k n) -> p k n", k=4)[:, :, 0:rows], \
                        (slice(None), slice(4 * b, 4 * b + 4), bass.ds(t * P, rows))

            @block.scalar
            def _(act):
                act.sem_inc(hi_done, PRIME)

                def hi(t, u, rows):
                    act.wait_ge(turned, t + 1 + PRIME)
                    for _, src, at in halves(t, u, rows):
                        m = act.activation(xT[0][at], src, ACT.Copy)
                    m.then_inc(hi_done, 1)

                with act.Fori(0, PT // 2) as i:
                    for u in range(2):
                        hi(2 * i + u, u, P)
                hi(PT, 0, DEC)

            @block.vector
            def _(dve):
                dve.sem_inc(lo_done, PRIME)

                def lo(t, u, rows):
                    dve.wait_ge(hi_done, t + 1 + PRIME)
                    for _, src, at in halves(t, u, rows):
                        m = dve.tensor_tensor(xT[1][at], src, r32(xT[0][at]), ALU.subtract)
                    m.then_inc(lo_done, 1)

                with dve.Fori(0, PT // 2) as i:
                    for u in range(2):
                        lo(2 * i + u, u, P)
                lo(PT, 0, DEC)


def project(nc, ctx, sem, sb, passed, bank, ident, xT, w_in, sp_in, pool_w, pool_scale,
            qT_d, kT_d, v_d, mixT_d, kp_out, vp_out, ks_out, vs_out, pp_out, ps_out):
    CH = 16
    PAD = 16
    UW = PAD + SEQ + PAD + DEC
    S0 = PAD + SEQ + PAD
    wraw = [sb(ctx, f"wraw{u}", [P, KD, P]) for u in range(2)]
    whi = [sb(ctx, f"whi{u}", [P, KD, P], F32R) for u in range(2)]
    wlo = [sb(ctx, f"wlo{u}", [P, KD, P], F32R) for u in range(2)]
    col = [sb(ctx, f"col{u}", [P, UW]) for u in range(2)]
    parts = sb(ctx, "parts", [P, 2, 17 * P], F32R)
    vparts = parts[:, :, :].rearrange("p a (b c) -> p (a b c)", c=P).rearrange(
        "p (t h j d) -> p t h j d", t=17, h=2, j=2)
    nat = sb(ctx, "nat", [P, 17 * P])
    nat3 = nat[:, :].rearrange("p (t c) -> p t c", c=P)
    pw_raw = sb(ctx, "pw_raw", [P, 4, P])
    pw = [sb(ctx, f"pw_{n}", [P, P], F32R) for n in ("hi", "lo")]
    tails = [sb(ctx, f"tails{u}", [P, 2, P]) for u in range(2)]
    pscale = sb(ctx, "pscale", [P, 4])
    hist_in = sb(ctx, "hist_in", [DEC, SBW])
    hist = sb(ctx, "hist", [P, 4, PAD])
    rcount = sb(ctx, "rcount", [P, PAD])

    w_loaded = [sem(f"w_loaded{u}") for u in range(2)]
    w_hi, w_lo = sem("w_hi"), sem("w_lo")
    mm_done, col_done = sem("mm_done"), sem("col_done")
    parts_hi, parts_lo = sem("parts_hi"), sem("parts_lo")
    nat_turned, nat_done = sem("nat_turned"), sem("nat_done")
    stored = sem("p_stored")
    pre_loaded, pre_done = sem("pre_loaded"), sem("pre_done")
    hist_turned, hist_done = sem("hist_turned"), sem("hist_done")
    pooled_done, pooled_out = sem("pooled_done"), sem("pooled_out")
    d_done = sem("d_done")
    dve_chain = sem("p_dve_chain")

    wv = w_in.rearrange("(k p) n -> p k n", p=P)
    kinds = "qkv"
    N_ST = {"q": 2, "k": 4, "v": 4, "u": 4}

    def st_before(kind, c):
        return 16 * (sum(N_ST[k] * 4 for k in "qkvu"[:"qkvu".index(kind)]) + N_ST[kind] * c)

    NBT = 5

    def ladder(level):
        return (col[1], nat)[level % 2]

    def diff(c):
        return ladder(c + 1)

    def tok_cols(b):
        lo, hi = b * TB, (b + 1) * TB
        if hi <= SEQ:
            return [(0, TB, PAD + lo)]
        return [(0, SEQ - lo, PAD + lo), (SEQ - lo, hi - SEQ, S0)]

    with nc.Block() as block:
        @block.sync
        def _(sp):
            def load(n, u):
                sp.wait_ge(w_lo, n - 1 + PRIME)
                sp.sem_inc(passed, 1)
                sp.dma_start(wraw[u][:], wv[:, :, bass.ds(n * P, P)]).then_inc(w_loaded[u], 16)

            sp.wait_ge(pre_done, 1)
            sp.dma_start(hist_in[1:1 + HIST, :], sp_in).then_inc(pre_loaded, 16)
            sp.dma_start(pw_raw[:], pool_w.rearrange("g c d -> c g d")).then_inc(pre_loaded, 16)
            with nc.allow_non_contiguous_dma(reason="512 scales, one a partition"):
                sp.dma_start(pscale[:], pool_scale.rearrange("(g p) -> p g", p=P)).then_inc(pre_loaded, 16)
            load(0, 0)
            load(1, 1)

            def store_parts(n, dst, row, width):
                sp.wait_ge(parts_lo, n + 1 + PRIME)
                sp.sem_inc(passed, 1)
                for j in range(2):
                    sp.dma_start(r32(dst[j, bass.ds(row, P), :]), r32(parts[:, j, 0:width])).then_inc(stored, 16)

            with sp.Fori(0, 2) as i:
                for u in range(2):
                    load(2 * i + u + 2, u)
                    store_parts(2 * i + u, qT_d, (2 * i + u) * P, TOK)
            with sp.Fori(0, 2) as i:
                for u in range(2):
                    c = 2 * i + u
                    load(c + 6, u)
                    store_parts(c + 4, kT_d, c * P, TOK)
                    sp.wait_ge(nat_done, NBT * (c + 1) + PRIME)
                    sp.sem_inc(passed, 1)
                    sp.dma_start(kp_out.rearrange("(t p) c -> p t c", p=P)[:, :, bass.ds(c * P, P)],
                                 nat3[:, 0:PT, :]).then_inc(stored, 16)
                    sp.dma_start(ks_out[:, bass.ds(c * P, P)], nat3[0:DEC, PT, :]).then_inc(stored, 16)
            with sp.Fori(0, 2) as i:
                for u in range(2):
                    c = 2 * i + u
                    load(c + 10, u)
                    sp.wait_ge(parts_lo, c + 9 + PRIME)
                    sp.sem_inc(passed, 1)
                    sp.dma_start(vp_out.rearrange("(t p) c -> p t c", p=P)[:, :, bass.ds(c * P, P)],
                                 nat3[:, 0:PT, :]).then_inc(stored, 16)
                    sp.dma_start(vs_out[:, bass.ds(c * P, P)], nat3[0:DEC, PT, :]).then_inc(stored, 16)
                    vrow = v_d.rearrange("t h j d -> t (h j d)")
                    vflat = parts[:, :, :].rearrange("p a b -> p (a b)").rearrange("p (t n) -> p t n", t=17)
                    sp.dma_start(r32(vrow[0:SEQ, bass.ds(c * 2 * P, 2 * P)].rearrange("(t p) n -> p t n", p=P)),
                                 r32(vflat[:, 0:PT, :])).then_inc(stored, 16)
                    sp.dma_start(r32(vrow[SEQ:TOK, bass.ds(c * 2 * P, 2 * P)]),
                                 r32(vflat[0:DEC, PT, :])).then_inc(stored, 16)
            for c in range(4):
                if c < 2:
                    load(c + 14, c % 2)
                sp.wait_ge(hist_done, 2 + 2 * (c + 1))
                sp.sem_inc(passed, 1)
                sp.dma_start(pp_out[:, c * P:(c + 1) * P], tails[c % 2][P - HIST:P, 0, :]).then_inc(stored, 16)
                sp.dma_start(ps_out[:, c * P:(c + 1) * P], tails[c % 2][DEC - HIST:DEC, 1, :]).then_inc(stored, 16)
                sp.wait_ge(parts_lo, 12 + 2 * c + 2 + PRIME)
                sp.sem_inc(passed, 1)
                for j in range(2):
                    sp.dma_start(r32(mixT_d[j, SBW + c * P:SBW + (c + 1) * P, :]),
                                 r32(parts[:, j, 0:TOK])).then_inc(stored, 16)
            sp.wait_ge(stored, st_before("u", 4))
            sp.sem_inc(passed, 1)

        @block.scalar
        def _(act):
            for x in (w_hi, col_done, pooled_out):
                act.sem_inc(x, PRIME)

            def split_w(n, u, times):
                act.wait_ge(w_loaded[u], 16 * times)
                act.wait_ge(mm_done, NB * (n - 1) + PRIME)
                act.activation(whi[u][:], wraw[u][:], ACT.Copy).then_inc(w_hi, 1)

            def columns(n, u, scale):
                for b in range(NB):
                    act.wait_ge(mm_done, NB * n + b + 1 + PRIME)
                    act.activation(col[u][:, b * TB:(b + 1) * TB], bank[(NB * u + b) % 2][:, 0:TB],
                                   ACT.Copy, scale=scale).then_inc(col_done, 1)

            split_w(0, 0, 1)
            with act.Fori(0, 2) as i:
                for u in range(2):
                    n = 2 * i + u
                    split_w(n + 1, 1 - u, i + 1 + u)
                    act.wait_ge(parts_lo, n - 1 + PRIME)
                    columns(n, u, HD ** -0.5)
            with act.Fori(0, 2) as i:
                for u in range(2):
                    n = 2 * i + u + 4
                    split_w(n + 1, 1 - u, i + 3 + u)
                    act.wait_ge(parts_lo, n - 1 + PRIME)
                    act.wait_ge(nat_turned, NBT * (n - 5) + PRIME)
                    columns(n, u, 1.0)
            with act.Fori(0, 2) as i:
                for u in range(2):
                    n = 2 * i + u + 8
                    split_w(n + 1, 1 - u, i + 5 + u)
                    act.wait_ge(parts_lo, n - 1 + PRIME)
                    act.wait_ge(nat_turned, NBT * (n - 5) + PRIME)
                    columns(n, u, 1.0)
            act.wait_ge(pre_loaded, 48)
            for c in range(4):
                n = 12 + c
                if c < 3:
                    split_w(n + 1, (n + 1) % 2, (n + 1) // 2 + 1)
                act.wait_ge(parts_lo, 12 + 2 * c + PRIME)
                act.wait_ge(hist_done, 2 + 2 * c)
                if c == 0:
                    act.wait_ge(nat_turned, NBT * 8 + PRIME)
                for b in range(NB):
                    act.wait_ge(mm_done, NB * n + b + 1 + PRIME)
                    for s, w, at in tok_cols(b):
                        m = act.activation(col[0][:, at:at + w], bank[(NB * n + b) % 2][:, s:s + w], ACT.Copy)
                    m.then_inc(col_done, 1)
                for b in range(5):
                    w = 512 if b < 4 else DEC
                    act.wait_ge(pooled_done, 5 * c + b + 1 + PRIME)
                    m = act.activation(col[1][:, 512 * b:512 * b + w], bank[4 + b % 2][:, 0:w], ACT.Copy,
                                       scale=pscale[:, c:c + 1])
                    m.then_inc(pooled_out, 1)

        @block.tensor
        def _(pe):
            pe.sem_inc(mm_done, PRIME)
            pe.sem_inc(nat_turned, PRIME)
            pe.sem_inc(pooled_done, PRIME)
            pe.wait_ge(pre_loaded, 48)
            for g in range(4):
                m = pe.transpose(bank[6][:, g * DEC:(g + 1) * DEC], hist_in[:, g * P:(g + 1) * P],
                                 ident[0:DEC, 0:DEC])
            m.then_inc(hist_turned, 1)

            def products(n, u, par):
                pe.wait_ge(w_lo, n + 1 + PRIME)
                for b in range(NB):
                    pe.wait_ge(col_done, NB * n + b - 1 + PRIME)
                    ps = bank[(par + b) % 2][:, 0:TB]
                    for k in range(KD):
                        for j, (w, x) in enumerate(((whi, 0), (whi, 1), (wlo, 0))):
                            m = pe.matmul(ps, w[u][:, k, :], xT[x][:, k, b * TB:(b + 1) * TB],
                                          start=(k == 0 and j == 0), stop=(k == KD - 1 and j == 2))
                    m.then_inc(mm_done, 1)

            def to_natural(m0, n, u, par):
                for b in range(NBT):
                    last_tile = min(4 * b + 4, 17)
                    pe.wait_ge(col_done, NB * n + min(NB, last_tile * P // TB + 1) + PRIME)
                    pe.wait_ge(nat_done, m0 + b - 1 + PRIME)
                    for t in range(4 * b, last_tile):
                        w = P if t < PT else DEC
                        m = pe.transpose(bank[2 + (par + b) % 2][0:w, (t % 4) * P:(t % 4 + 1) * P],
                                         col[u][:, t * P:t * P + w], ident[:, :])
                    m.then_inc(nat_turned, 1)

            with pe.Fori(0, 2) as i:
                for u in range(2):
                    products(2 * i + u, u, NB * u)
            for base in (4, 8):
                with pe.Fori(0, 2) as i:
                    for u in range(2):
                        n = 2 * i + u + base
                        products(n, u, NB * u)
                        to_natural(NBT * (n - 4), n, u, NBT * u)
            for c in range(4):
                n = 12 + c
                products(n, n % 2, NB * n)
                pe.wait_ge(col_done, NB * (n + 1) + PRIME)
                pe.wait_ge(hist_done, 2 + 2 * c)
                pe.transpose(bank[6][:, 0:P], col[0][:, PAD + SEQ - P:PAD + SEQ], ident[:, :])
                pe.transpose(bank[6][0:DEC, P:2 * P], col[0][:, S0:S0 + DEC], ident[:, :]).then_inc(hist_turned, 1)
                pe.wait_ge(parts_lo, 12 + 2 * c + 1 + PRIME)
                for b in range(5):
                    w = 512 if b < 4 else DEC
                    at = PAD + 512 * b if b < 4 else S0
                    pe.wait_ge(pooled_out, 5 * c + max(b - 1, 0) + PRIME)
                    for j, (a, d) in enumerate(((0, 0), (0, 1), (1, 0))):
                        m = pe.matmul(bank[4 + b % 2][:, 0:w], pw[a][:], parts[:, d, at:at + w],
                                      start=j == 0, stop=j == 2)
                    m.then_inc(pooled_done, 1)

        @block.gpsimd
        def _(pool):
            pool.sem_inc(parts_hi, PRIME)
            pool.memset(hist_in[:], 0.0).then_inc(pre_done, 1)

            def hi_parts(n, u, base_st, c):
                pool.wait_ge(col_done, NB * (n + 1) + PRIME)
                pool.sem_inc(passed, 1)
                pool.wait_ge(stored, base_st)
                pool.sem_inc(passed, 1)
                pool.tensor_copy(parts[:, 0, 0:TOK], col[u][:, 0:TOK]).then_inc(parts_hi, 1)

            with pool.Fori(0, 2) as i:
                for u in range(2):
                    c = 2 * i + u
                    hi_parts(c, u, 32 * c, c)
            with pool.Fori(0, 2) as i:
                for u in range(2):
                    c = 2 * i + u
                    hi_parts(c + 4, u, 64 * c + st_before("k", 0), c)
            with pool.Fori(0, 2) as i:
                for u in range(2):
                    c = 2 * i + u
                    pool.wait_ge(nat_done, NBT * (c + 5) + PRIME)
                    pool.sem_inc(passed, 1)
                    pool.wait_ge(stored, 64 * c + st_before("v", 0))
                    pool.sem_inc(passed, 1)
                    pool.tensor_copy(vparts[:, 0:PT, :, 0, :],
                                     nat3[:, 0:PT, :].rearrange("p t (h d) -> p t h d", h=2))
                    pool.tensor_copy(vparts[0:DEC, PT, :, 0, :],
                                     nat3[0:DEC, PT, :].rearrange("p (h d) -> p h d", h=2)).then_inc(parts_hi, 1)
            for c in range(4):
                pool.wait_ge(d_done, c + 1 + PRIME)
                pool.sem_inc(passed, 1)
                pool.wait_ge(stored, st_before("u", c))
                pool.sem_inc(passed, 1)
                pool.tensor_copy(parts[:, 0, PAD:UW], diff(c)[:, PAD:UW]).then_inc(parts_hi, 1)
                pool.wait_ge(pooled_out, 5 * (c + 1) + PRIME)
                pool.sem_inc(passed, 1)
                pool.tensor_copy(parts[:, 0, 0:TOK], col[1][:, 0:TOK]).then_inc(parts_hi, 1)

        @block.vector
        def _(dve):
            for x in (w_lo, parts_lo, nat_done, d_done):
                dve.sem_inc(x, PRIME)
            chain = [0]

            def link(m):
                chain[0] += 1
                m.then_inc(dve_chain, 1)
                dve.wait_ge(dve_chain, chain[0])

            def split_w(n, u):
                dve.wait_ge(w_hi, n + 1 + PRIME)
                dve.tensor_tensor(wlo[u][:], wraw[u][:], r32(whi[u][:]), ALU.subtract).then_inc(w_lo, 1)

            def lo_parts(n, u):
                dve.wait_ge(parts_hi, n + 1 + PRIME)
                dve.tensor_tensor(parts[:, 1, 0:TOK], col[u][:, 0:TOK], r32(parts[:, 0, 0:TOK]),
                                  ALU.subtract).then_inc(parts_lo, 1)

            def natural(m0, par, base_st):
                dve.wait_ge(stored, base_st)
                for b in range(NBT):
                    dve.wait_ge(nat_turned, m0 + b + 1 + PRIME)
                    if b < 4:
                        m = dve.tensor_copy(nat[:, 512 * b:512 * b + 512], bank[2 + (par + b) % 2][:])
                    else:
                        m = dve.tensor_copy(nat[0:DEC, PT * P:17 * P], bank[2 + (par + b) % 2][0:DEC, 0:P])
                    m.then_inc(nat_done, 1)

            for t in range(PAD):
                dve.memset(rcount[:, t:t + 1], 1.0 / (t + 1))
            dve.wait_ge(pre_loaded, 48)
            dve.wait_ge(hist_turned, 1)
            dve.tensor_copy(hist[:], bank[6][:, 0:4 * DEC].rearrange("p (g n) -> p g n", g=4)[:, :, 0:PAD])\
               .then_inc(hist_done, 2)
            split_w(0, 0)
            with dve.Fori(0, 2) as i:
                for u in range(2):
                    n = 2 * i + u
                    split_w(n + 1, 1 - u)
                    lo_parts(n, u)
            with dve.Fori(0, 2) as i:
                for u in range(2):
                    c = 2 * i + u
                    split_w(c + 5, 1 - u)
                    natural(NBT * c, NBT * u, 64 * c + st_before("k", 0))
                    lo_parts(c + 4, u)
            with dve.Fori(0, 2) as i:
                for u in range(2):
                    c = 2 * i + u
                    split_w(c + 9, 1 - u)
                    natural(NBT * (c + 4), NBT * u, 64 * c + st_before("v", 0))
                    dve.wait_ge(parts_hi, c + 9 + PRIME)
                    for rows, t in ((P, slice(0, PT)), (DEC, slice(PT, PT + 1))):
                        m = dve.tensor_tensor(vparts[0:rows, t, :, 1, :],
                                              nat3[0:rows, t, :].rearrange("p t (h d) -> p t h d", h=2),
                                              r32(vparts[0:rows, t, :, 0, :]), ALU.subtract)
                    m.then_inc(parts_lo, 1)
            for c in range(4):
                n = 12 + c
                if c < 3:
                    split_w(n + 1, (n + 1) % 2)
                dve.wait_ge(parts_lo, 12 + 2 * c + PRIME)
                link(dve.tensor_copy(pw[0][:], pw_raw[:, c, :]))
                dve.tensor_tensor(pw[1][:], pw_raw[:, c, :], r32(pw[0][:]), ALU.subtract)
                if c == 0:
                    dve.wait_ge(stored, st_before("u", 0))
                dve.memset(col[0][:, 0:PAD], 0.0)
                link(dve.tensor_copy(col[0][:, S0 - PAD:S0], hist[:, c, :]))
                dve.wait_ge(col_done, NB * (n + 1) + PRIME)
                src = col[0]
                for lv in range(c + 1):
                    back, dst = 1 << lv, ladder(lv)
                    link(dve.tensor_tensor(dst[:, 2 * back - 1:UW], src[:, 2 * back - 1:UW],
                                           src[:, back - 1:UW - back], ALU.add))
                    src = dst
                w = WINDOWS[c]
                out = diff(c)
                link(dve.scalar_tensor_tensor(out[:, PAD:UW], src[:, PAD:UW], 1.0 / w, col[0][:, PAD:UW],
                                              ALU.mult, ALU.subtract))
                link(dve.tensor_tensor(out[:, PAD:PAD + w - 1], src[:, PAD:PAD + w - 1], rcount[:, 0:w - 1], ALU.mult))
                dve.tensor_tensor(out[:, PAD:PAD + w - 1], out[:, PAD:PAD + w - 1], col[0][:, PAD:PAD + w - 1],
                                  ALU.subtract).then_inc(d_done, 1)
                dve.wait_ge(parts_hi, 12 + 2 * c + 1 + PRIME)
                dve.tensor_tensor(parts[:, 1, PAD:UW], out[:, PAD:UW], r32(parts[:, 0, PAD:UW]),
                                  ALU.subtract).then_inc(parts_lo, 1)
                dve.wait_ge(hist_turned, c + 2)
                if c >= 2:
                    dve.wait_ge(stored, st_before("u", c - 1))
                dve.tensor_copy(tails[c % 2][:, 0, :], bank[6][:, 0:P]).then_inc(hist_done, 1)
                dve.tensor_copy(tails[c % 2][0:DEC, 1, :], bank[6][0:DEC, P:2 * P]).then_inc(hist_done, 1)
                dve.wait_ge(parts_hi, 12 + 2 * c + 2 + PRIME)
                dve.tensor_tensor(parts[:, 1, 0:TOK], col[1][:, 0:TOK], r32(parts[:, 0, 0:TOK]),
                                  ALU.subtract).then_inc(parts_lo, 1)


def split_cache(nc, ctx, sem, sb, passed, bank, ident, ck, cv, kcT_d, vc_d):
    kin = [sb(ctx, f"kin{u}", [P, SBW]) for u in range(2)]
    vin = [sb(ctx, f"vin{u}", [P, SBW]) for u in range(2)]
    kparts = [sb(ctx, f"kparts{u}", [P, 2, HC, P], F32R) for u in range(2)]
    vparts = [sb(ctx, f"vcparts{u}", [P, HEADS, 2, HD], F32R) for u in range(2)]
    k_loaded = [sem(f"kc_loaded{u}") for u in range(2)]
    v_loaded = [sem(f"vc_loaded{u}") for u in range(2)]
    stored = [sem(f"c_stored{u}") for u in range(2)]
    turned, k_hi, k_lo, v_hi, v_lo = (sem(n) for n in ("kc_turned", "kc_hi", "kc_lo", "vc_hi", "vc_lo"))
    N_ST = 16 * (2 * HC + 1)

    with nc.Block() as block:
        @block.sync
        def _(sp):
            with sp.Fori(0, CT // 2) as i:
                for u in range(2):
                    sp.wait_ge(turned, 2 * i + u - 1 + PRIME)
                    sp.sem_inc(passed, 1)
                    sp.dma_start(kin[u][:], ck[bass.ds((2 * i + u) * P, P), :]).then_inc(k_loaded[u], 16)
                    sp.wait_ge(v_lo, 2 * i + u - 1 + PRIME)
                    sp.sem_inc(passed, 1)
                    sp.dma_start(vin[u][:], cv[bass.ds((2 * i + u) * P, P), :]).then_inc(v_loaded[u], 16)

        @block.tensor
        def _(pe):
            pe.sem_inc(turned, PRIME)
            with pe.Fori(0, CT // 2) as i:
                for u in range(2):
                    pe.wait_ge(k_loaded[u], 16 * i + 16)
                    pe.wait_ge(k_lo, 2 * i + u - 1 + PRIME)
                    for c in range(HC):
                        m = pe.transpose(bank[u][:, c * P:(c + 1) * P], kin[u][:, c * P:(c + 1) * P], ident[:, :])
                    m.then_inc(turned, 1)

        @block.scalar
        def _(act):
            act.sem_inc(k_hi, PRIME)
            with act.Fori(0, CT // 2) as i:
                for u in range(2):
                    act.wait_ge(turned, 2 * i + u + 1 + PRIME)
                    act.wait_ge(stored[u], N_ST * i)
                    act.activation(kparts[u][:, 0, :, :].rearrange("p c n -> p (c n)"), bank[u][:], ACT.Copy)\
                       .then_inc(k_hi, 1)

        @block.vector
        def _(dve):
            dve.sem_inc(k_lo, PRIME)
            dve.sem_inc(v_lo, PRIME)
            with dve.Fori(0, CT // 2) as i:
                for u in range(2):
                    dve.wait_ge(k_hi, 2 * i + u + 1 + PRIME)
                    dve.tensor_tensor(kparts[u][:, 1, :, :].rearrange("p c n -> p (c n)"), bank[u][:],
                                      r32(kparts[u][:, 0, :, :].rearrange("p c n -> p (c n)")), ALU.subtract)\
                       .then_inc(k_lo, 1)
                    dve.wait_ge(v_hi, 2 * i + u + 1 + PRIME)
                    dve.tensor_tensor(vparts[u][:, :, 1, :], vin[u][:].rearrange("p (h d) -> p h d", h=HEADS),
                                      r32(vparts[u][:, :, 0, :]), ALU.subtract).then_inc(v_lo, 1)

        @block.gpsimd
        def _(pool):
            pool.sem_inc(v_hi, PRIME)
            with pool.Fori(0, CT // 2) as i:
                for u in range(2):
                    pool.wait_ge(v_loaded[u], 16 * i + 16)
                    pool.sem_inc(passed, 1)
                    pool.wait_ge(stored[u], N_ST * i)
                    pool.sem_inc(passed, 1)
                    pool.tensor_copy(vparts[u][:, :, 0, :], vin[u][:].rearrange("p (h d) -> p h d", h=HEADS))\
                        .then_inc(v_hi, 1)
                    pool.wait_ge(k_lo, 2 * i + u + 1 + PRIME)
                    pool.sem_inc(passed, 1)
                    for j in range(2):
                        for c in range(HC):
                            pool.dma_start(r32(kcT_d[j, c * P:(c + 1) * P, bass.ds((2 * i + u) * P, P)]),
                                           r32(kparts[u][:, j, c, :])).then_inc(stored[u], 16)
                    pool.wait_ge(v_lo, 2 * i + u + 1 + PRIME)
                    pool.sem_inc(passed, 1)
                    pool.dma_start(r32(vc_d[bass.ds((2 * i + u) * P, P)].rearrange("t h j d -> t (h j d)")),
                                   r32(vparts[u][:].rearrange("p h j d -> p (h j d)"))).then_inc(stored[u], 16)
            for u in range(2):
                pool.wait_ge(stored[u], N_ST * (CT // 2))
                pool.sem_inc(passed, 1)


def attend_prompt(nc, ctx, sem, sb, passed, bank, ident, ident_r, mask_r, qT_d, kT_d, v_d, mixT_d):
    NBUF = 4
    G = PT // 4
    k_st = [[sb(ctx, f"k_st{u}{j}", [P, SEQ], F32R) for j in range(2)] for u in range(2)]
    q_st = [sb(ctx, f"q_st{u}", [P, SEQ], F32R) for u in range(2)]
    v_st = [sb(ctx, f"v_st{u}", [P, PT, P], F32R) for u in range(2)]
    e_t = [sb(ctx, f"e_t{b}", [P, 512]) for b in range(4)]
    l_t = [sb(ctx, f"l_t{b}", [P, 512]) for b in range(2)]
    sp_t = [sb(ctx, f"sp_t{b}", [P, 512]) for b in range(2)]
    c_t = [sb(ctx, f"c_t{b}", [P, 512]) for b in range(2)]
    t_t = [sb(ctx, f"t_t{b}", [P, 512]) for b in range(2)]
    a_t = [sb(ctx, f"a_t{b}", [P, 512]) for b in range(2)]
    ahi = [sb(ctx, f"ahi{b}", [P, 512], F32R) for b in range(2)]
    alo = [sb(ctx, f"alo{b}", [P, 512], F32R) for b in range(2)]
    low_half = [sb(ctx, f"low_half{b}", [HD, 512]) for b in range(2)]
    o_t = [sb(ctx, f"o_t{b}", [HD, 512]) for b in range(2)]
    oparts = [sb(ctx, f"oparts{b}", [HD, 2, 512], F32R) for b in range(2)]

    loaded = [sem(f"a_loaded{u}") for u in range(2)]
    z_done, e_done, l_done, sp_done, c_done, t_done, a_done, turn_done, hi_done, lo_done, av_done = (
        sem(f"a_{n}") for n in ("z", "e", "l", "sp", "c", "t", "a", "turn", "hi", "lo", "av"))
    abs_done = sem("a_abs_even"), sem("a_abs_odd")
    half_out, o_done, opart_done = sem("a_half"), sem("a_o"), sem("a_opart")
    stored = [sem(f"a_stored{b}") for b in range(2)]

    all_items = [(u, q, c, w) for u in range(2) for q, c, w in ITEMS]
    N = len(all_items)
    Z_BANK, T_BANK, O_BANK = 0, 4, 6
    last_of_group = {n: (4 * u + q // 4) for n, (u, q, c, w) in enumerate(all_items) if q % 4 == 3 and c == 0}
    group_before = {n: (4 * u + q // 4) for n, (u, q, c, w) in enumerate(all_items) if q % 4 == 0 and c == q // 4}

    with nc.Block() as block:
        @block.sync
        def _(sp):
            with sp.Fori(0, HEADS // 2) as i:
                for u in range(2):
                    sp.wait_ge(av_done, N * (i - 1) + NI * (u + 1) + PRIME)
                    sp.sem_inc(passed, 1)
                    row = (2 * i + u) * HD
                    for half in range(2):
                        s = slice(half * HD, half * HD + HD)
                        for j in range(2):
                            sp.dma_start(r32(k_st[u][j][s, :]), r32(kT_d[j, bass.ds(row, HD), 0:SEQ]))\
                              .then_inc(loaded[u], 16)
                        sp.dma_start(r32(q_st[u][s, :]), r32(qT_d[half, bass.ds(row, HD), 0:SEQ]))\
                          .then_inc(loaded[u], 16)
                    sp.dma_start(r32(v_st[u][:]),
                                 r32(v_d[0:SEQ].rearrange("(t p) h j d -> h p t (j d)", p=P)[2 * i + u]))\
                      .then_inc(loaded[u], 16)

        @block.tensor
        def _(pe):
            for x in (z_done, turn_done, av_done):
                pe.sem_inc(x, PRIME)
            with pe.Fori(0, HEADS // 2) as i:
                def scores(n):
                    u, q, c, w = all_items[n]
                    if n % NI == 0:
                        pe.wait_ge(loaded[u], 16 * 7 * (i + 1))
                    pe.wait_ge(t_done, N * i + n - NBUF + 1 + PRIME)
                    z = bank[Z_BANK + n % NBUF][:, 0:w]
                    diagonal = c == q // 4
                    for j in range(2):
                        if diagonal and j == 1:
                            pe.matmul(bank[Z_BANK + n % NBUF][:, w - P:w], ident_r[:], mask_r[:],
                                      start=False, stop=False, skip_group_check=True)
                        m = pe.matmul(z, q_st[u][:, q * P:(q + 1) * P], k_st[u][j][:, c * 512:c * 512 + w],
                                      start=j == 0, stop=j == 1)
                    m.then_inc(z_done, 1)

                def turn(n):
                    u, q, c, w = all_items[n]
                    pe.wait_ge(a_done, N * i + n + 1 + PRIME)
                    pe.wait_ge(lo_done, N * i + n - 1 + PRIME)
                    for b in range(w // P):
                        m = pe.transpose(bank[T_BANK + n % 2][:, b * P:(b + 1) * P],
                                         a_t[n % 2][:, b * P:(b + 1) * P], ident[:, :])
                    m.then_inc(turn_done, 1)

                def values(n):
                    u, q, c, w = all_items[n]
                    pe.wait_ge(lo_done, N * i + n + 1 + PRIME)
                    if n in group_before:
                        pe.wait_ge(o_done, 2 * G * i + group_before[n] - 1 + PRIME)
                    out = bank[O_BANK + (q // 4) % 2][:, (q % 4) * P:(q % 4 + 1) * P]
                    for b in range(w // P):
                        for j, a in enumerate((ahi, alo)):
                            m = pe.matmul(out, v_st[u][:, 4 * c + b, :], a[n % 2][:, b * P:(b + 1) * P],
                                          start=(c == q // 4 and b == 0 and j == 0),
                                          stop=(c == 0 and b == w // P - 1 and j == 1))
                    m.then_inc(av_done, 1)

                for s in range(N + 4):
                    if s < N:
                        scores(s)
                    if 0 <= s - 3 < N:
                        turn(s - 3)
                    if 0 <= s - 4 < N:
                        values(s - 4)

        @block.scalar
        def _(act):
            for x in (e_done, l_done, a_done, hi_done, half_out, abs_done[0]):
                act.sem_inc(x, PRIME)
            with act.Fori(0, HEADS // 2) as i:
                def absolute(n):
                    w = all_items[n][3]
                    act.wait_ge(z_done, N * i + n + 1 + PRIME)
                    act.wait_ge(l_done, N * i + n - 3 + PRIME)
                    act.activation(e_t[n % 4][:, 0:w], bank[Z_BANK + n % NBUF][:, 0:w], ACT.Abs)\
                       .then_inc(abs_done[0], 1)

                for s in range(N + 6):
                    if s == 0:
                        absolute(0)
                    if s < N:
                        n, w = s, all_items[s][3]
                        act.wait_ge(abs_done[n % 2], N // 2 * i + n // 2 + 1 + PRIME)
                        act.activation(e_t[n % 4][:, 0:w], e_t[n % 4][:, 0:w], ACT.Exp, scale=-1.0)\
                           .then_inc(e_done, 1)
                    if 0 <= s - 1 < N:
                        n, w = s - 1, all_items[s - 1][3]
                        act.wait_ge(e_done, N * i + n + 1 + PRIME)
                        act.wait_ge(sp_done, N * i + n - 1 + PRIME)
                        act.activation(l_t[n % 2][:, 0:w], e_t[n % 4][:, 0:w], ACT.Ln, bias=1.0)\
                           .then_inc(l_done, 1)
                    if 0 <= s - 2 < N:
                        n, w = s - 2, all_items[s - 2][3]
                        act.wait_ge(t_done, N * i + n + 1 + PRIME)
                        act.wait_ge(turn_done, N * i + n - 1 + PRIME)
                        act.activation(a_t[n % 2][:, 0:w], t_t[n % 2][:, 0:w], ACT.Exp).then_inc(a_done, 1)
                    if 0 <= s - 3 < N:
                        n, w = s - 3, all_items[s - 3][3]
                        act.wait_ge(turn_done, N * i + n + 1 + PRIME)
                        act.wait_ge(av_done, N * i + n - 1 + PRIME)
                        act.activation(ahi[n % 2][:, 0:w], bank[T_BANK + n % 2][:, 0:w], ACT.Copy)\
                           .then_inc(hi_done, 1)
                    if s + 1 < N and (s + 1) % 2 == 0:
                        absolute(s + 1)
                    if s - 5 in last_of_group:
                        g = last_of_group[s - 5]
                        act.wait_ge(av_done, N * i + s - 5 + 1 + PRIME)
                        act.wait_ge(o_done, 2 * G * i + g - 1 + PRIME)
                        act.activation(low_half[g % 2][:], bank[O_BANK + g % 2][HD:P, :], ACT.Copy)\
                           .then_inc(half_out, 1)

        @block.gpsimd
        def _(pool):
            pool.sem_inc(opart_done, PRIME)
            with pool.Fori(0, HEADS // 2) as i:
                for s in range(N + 7):
                    if s - 6 in last_of_group:
                        g = last_of_group[s - 6]
                        pool.wait_ge(o_done, 2 * G * i + g + 1 + PRIME)
                        pool.sem_inc(passed, 1)
                        pool.wait_ge(stored[g % 2], 32 * (G * i + g // 2))
                        pool.sem_inc(passed, 1)
                        pool.tensor_copy(oparts[g % 2][:, 0, :], o_t[g % 2][:]).then_inc(opart_done, 1)
                        pool.wait_ge(opart_done, 4 * G * i + 2 * g + 1 + PRIME)
                        pool.sem_inc(passed, 1)
                        pool.tensor_tensor(oparts[g % 2][:, 1, :], o_t[g % 2][:], r32(oparts[g % 2][:, 0, :]),
                                           ALU.subtract).then_inc(opart_done, 1)
                        pool.wait_ge(opart_done, 4 * G * i + 2 * g + 2 + PRIME)
                        pool.sem_inc(passed, 1)
                        for j in range(2):
                            pool.dma_start(r32(mixT_d[j, bass.ds((2 * i + g // 4) * HD, HD),
                                                      (g % 4) * 512:(g % 4 + 1) * 512]),
                                           r32(oparts[g % 2][:, j, :])).then_inc(stored[g % 2], 16)
            for b in range(2):
                pool.wait_ge(stored[b], 32 * G * HEADS // 2)

        @block.vector
        def _(dve):
            for x in (sp_done, c_done, t_done, lo_done, o_done, abs_done[1]):
                dve.sem_inc(x, PRIME)
            with dve.Fori(0, HEADS // 2) as i:
                for s in range(N + 6):
                    if 0 <= s - 1 < N:
                        n, (u, q, c, w) = s - 1, all_items[s - 1]
                        z = bank[Z_BANK + n % NBUF][:, 0:w]
                        dve.wait_ge(l_done, N * i + n + 1 + PRIME)
                        dve.wait_ge(c_done, N * i + n - 1 + PRIME)
                        dve.scalar_tensor_tensor(sp_t[n % 2][:, 0:w], z, 0.0, l_t[n % 2][:, 0:w], ALU.max, ALU.add)\
                           .then_inc(sp_done, 1)
                        dve.wait_ge(sp_done, N * i + n + 1 + PRIME)
                        dve.wait_ge(t_done, N * i + n - 1 + PRIME)
                        first = c == q // 4
                        dve.tensor_tensor_scan(c_t[n % 2][:, 0:w][:, ::-1], sp_t[n % 2][:, 0:w][:, ::-1],
                                               sp_t[n % 2][:, 0:w][:, ::-1],
                                               0.0 if first else c_t[(n - 1) % 2][:, 0:1],
                                               ALU.add, ALU.max).then_inc(c_done, 1)
                        dve.wait_ge(c_done, N * i + n + 1 + PRIME)
                        dve.wait_ge(a_done, N * i + n - 1 + PRIME)
                        dve.tensor_tensor(t_t[n % 2][:, 0:w], z, c_t[n % 2][:, 0:w], ALU.subtract)\
                           .then_inc(t_done, 1)
                    if 0 <= s - 3 < N:
                        n, w = s - 3, all_items[s - 3][3]
                        dve.wait_ge(hi_done, N * i + n + 1 + PRIME)
                        dve.tensor_tensor(alo[n % 2][:, 0:w], bank[T_BANK + n % 2][:, 0:w], r32(ahi[n % 2][:, 0:w]),
                                          ALU.subtract).then_inc(lo_done, 1)
                    if s + 1 < N and (s + 1) % 2 == 1:
                        n, w = s + 1, all_items[s + 1][3]
                        dve.wait_ge(z_done, N * i + n + 1 + PRIME)
                        dve.wait_ge(l_done, N * i + n - 3 + PRIME)
                        dve.tensor_scalar(e_t[n % 4][:, 0:w].bitcast(I32), bank[Z_BANK + n % NBUF][:, 0:w].bitcast(I32),
                                          0x7FFFFFFF, None, ALU.bitwise_and).then_inc(abs_done[1], 1)
                    if s - 5 in last_of_group:
                        g = last_of_group[s - 5]
                        dve.wait_ge(half_out, 2 * G * i + g + 1 + PRIME)
                        dve.wait_ge(opart_done, 4 * G * i + 2 * g - 2 + PRIME)
                        dve.tensor_tensor(o_t[g % 2][:], bank[O_BANK + g % 2][0:HD, :], low_half[g % 2][:], ALU.add)\
                           .then_inc(o_done, 1)


def attend_sample(nc, ctx, sem, sb, passed, bank, ident, ident_r, maskd_r, qT_d, kT_d, kcT_d, v_d, vc_d, mixT_d):
    HG = 4
    KW = PAST + P
    NT = KW // P
    ks = [sb(ctx, f"ds_k{j}", [P, HG, KW], F32R) for j in range(2)]
    qz = sb(ctx, "ds_q", [P, HG, P], F32R)
    vs = sb(ctx, "ds_v", [P, HG, NT, P], F32R)
    e_t, l_t, sp_t, c_t, t_t, a_t = (sb(ctx, f"ds_{n}", [P, KW]) for n in "elsctA")
    at = [sb(ctx, f"ds_at{j}", [P, KW], F32R) for j in range(2)]
    low_half = sb(ctx, "ds_half", [HD, P])
    o_t = sb(ctx, "ds_o", [HD, P])
    oparts = sb(ctx, "ds_oparts", [HD, 2, P], F32R)
    zeroed, loaded, stored = sem("ds_zeroed"), sem("ds_loaded"), sem("ds_stored")
    N_LD = HG * 12
    z_done, abs_done, e_done, l_done, sp_done, c_done, t_done, a_done, turn_done, hi_done, lo_done, av_done = (
        sem(f"ds_{n}") for n in ("z", "abs", "e", "l", "sp", "c", "t", "a", "turn", "hi", "lo", "av"))
    half_out, o_done, opart_done = sem("ds_halfout"), sem("ds_osum"), sem("ds_opart")
    parts = ((PAST, P), (512, 512), (0, 512))

    with nc.Block() as block:
        @block.sync
        def _(sp):
            sp.wait_ge(zeroed, 4)
            with sp.Fori(0, HEADS // HG) as i:
                sp.wait_ge(av_done, i + PRIME)
                sp.sem_inc(passed, 1)
                for h in range(HG):
                    row = (HG * i + h) * HD
                    for half in range(2):
                        s = slice(half * HD, half * HD + HD)
                        for j in range(2):
                            sp.dma_start(r32(ks[j][s, h, 0:PAST]), r32(kcT_d[j, bass.ds(row, HD), :])).then_inc(loaded, 16)
                            sp.dma_start(r32(ks[j][s, h, PAST:PAST + DEC]), r32(kT_d[j, bass.ds(row, HD), SEQ:TOK]))\
                              .then_inc(loaded, 16)
                        sp.dma_start(r32(qz[s, h, h * DEC:(h + 1) * DEC]), r32(qT_d[half, bass.ds(row, HD), SEQ:TOK]))\
                          .then_inc(loaded, 16)
                    sp.dma_start(r32(vs[:, h, 0:CT, :]),
                                 r32(vc_d.rearrange("(t p) h j d -> h p t (j d)", p=P)[HG * i + h])).then_inc(loaded, 16)
                    sp.dma_start(r32(vs[0:DEC, h, CT, :]),
                                 r32(v_d[SEQ:TOK].rearrange("t h j d -> h t (j d)")[HG * i + h])).then_inc(loaded, 16)

        @block.tensor
        def _(pe):
            for x in (z_done, turn_done, av_done):
                pe.sem_inc(x, PRIME)
            with pe.Fori(0, HEADS // HG) as i:
                pe.wait_ge(loaded, 16 * N_LD * (i + 1))
                pe.wait_ge(t_done, 3 * i + PRIME)
                for n, (k0, w) in enumerate(parts):
                    for h in range(HG):
                        for j in range(2):
                            m = pe.matmul(bank[n][:, 0:w], qz[:, h, :], ks[j][:, h, k0:k0 + w],
                                          start=h == 0 and j == 0, stop=h == HG - 1 and j == 1 and n > 0)
                    if n == 0:
                        m = pe.matmul(bank[n][:, 0:w], ident_r[:], maskd_r[:], start=False, stop=True)
                    m.then_inc(z_done, 1)
                for n, (k0, w) in enumerate(parts):
                    pe.wait_ge(a_done, 3 * i + n + 1 + PRIME)
                    pe.wait_ge(lo_done, 3 * i + PRIME)
                    for b in range(w // P):
                        m = pe.transpose(bank[3 + n][:, b * P:(b + 1) * P], a_t[:, k0 + b * P:k0 + (b + 1) * P],
                                         ident[:, :])
                    m.then_inc(turn_done, 1)
                pe.wait_ge(lo_done, 3 * i + 3 + PRIME)
                pe.wait_ge(o_done, i + PRIME)
                for h in range(HG):
                    q = slice(h * DEC, (h + 1) * DEC)
                    for t in range(NT):
                        for j in range(2):
                            m = pe.matmul(bank[6][:, q], vs[:, h, t, :], at[j][:, t * P + h * DEC:t * P + (h + 1) * DEC],
                                          start=t == 0 and j == 0, stop=t == NT - 1 and j == 1)
                m.then_inc(av_done, 1)

        @block.scalar
        def _(act):
            for x in (abs_done, e_done, l_done, a_done, hi_done, half_out):
                act.sem_inc(x, PRIME)
            with act.Fori(0, HEADS // HG) as i:
                for n, (k0, w) in enumerate(parts):
                    act.wait_ge(z_done, 3 * i + n + 1 + PRIME)
                    act.activation(e_t[:, k0:k0 + w], bank[n][:, 0:w], ACT.Abs).then_inc(abs_done, 1)
                for n, (k0, w) in enumerate(parts):
                    act.wait_ge(abs_done, 3 * i + n + 1 + PRIME)
                    act.activation(e_t[:, k0:k0 + w], e_t[:, k0:k0 + w], ACT.Exp, scale=-1.0).then_inc(e_done, 1)
                for n, (k0, w) in enumerate(parts):
                    act.wait_ge(e_done, 3 * i + n + 1 + PRIME)
                    act.activation(l_t[:, k0:k0 + w], e_t[:, k0:k0 + w], ACT.Ln, bias=1.0).then_inc(l_done, 1)
                for n, (k0, w) in enumerate(parts):
                    act.wait_ge(t_done, 3 * i + n + 1 + PRIME)
                    act.activation(a_t[:, k0:k0 + w], t_t[:, k0:k0 + w], ACT.Exp).then_inc(a_done, 1)
                for n, (k0, w) in enumerate(parts):
                    act.wait_ge(turn_done, 3 * i + n + 1 + PRIME)
                    act.activation(at[0][:, k0:k0 + w], bank[3 + n][:, 0:w], ACT.Copy).then_inc(hi_done, 1)
                act.wait_ge(av_done, i + 1 + PRIME)
                act.activation(low_half[:], bank[6][HD:P, 0:P], ACT.Copy).then_inc(half_out, 1)

        @block.vector
        def _(dve):
            for x in (sp_done, c_done, t_done, lo_done, o_done):
                dve.sem_inc(x, PRIME)
            dve.memset(r32(qz[:]), 0.0).then_inc(zeroed, 1)
            dve.memset(r32(vs[:, :, CT, :]), 0.0).then_inc(zeroed, 1)
            for j in range(2):
                dve.memset(r32(ks[j][:, :, PAST:KW]), 0.0).then_inc(zeroed, 1)
            with dve.Fori(0, HEADS // HG) as i:
                for n, (k0, w) in enumerate(parts):
                    dve.wait_ge(l_done, 3 * i + n + 1 + PRIME)
                    dve.scalar_tensor_tensor(sp_t[:, k0:k0 + w], bank[n][:, 0:w], 0.0, l_t[:, k0:k0 + w],
                                             ALU.max, ALU.add).then_inc(sp_done, 1)
                    dve.wait_ge(sp_done, 3 * i + n + 1 + PRIME)
                    dve.wait_ge(c_done, 3 * i + n + PRIME)
                    back = sp_t[:, k0:k0 + w][:, ::-1]
                    dve.tensor_tensor_scan(c_t[:, k0:k0 + w][:, ::-1], back, back,
                                           0.0 if n == 0 else c_t[:, k0 + w:k0 + w + 1],
                                           ALU.add, ALU.max).then_inc(c_done, 1)
                    dve.wait_ge(c_done, 3 * i + n + 1 + PRIME)
                    dve.tensor_tensor(t_t[:, k0:k0 + w], bank[n][:, 0:w], c_t[:, k0:k0 + w], ALU.subtract)\
                       .then_inc(t_done, 1)
                for n, (k0, w) in enumerate(parts):
                    dve.wait_ge(hi_done, 3 * i + n + 1 + PRIME)
                    dve.tensor_tensor(at[1][:, k0:k0 + w], bank[3 + n][:, 0:w], r32(at[0][:, k0:k0 + w]), ALU.subtract)\
                       .then_inc(lo_done, 1)
                dve.wait_ge(half_out, i + 1 + PRIME)
                dve.wait_ge(opart_done, 2 * i + PRIME)
                dve.tensor_tensor(o_t[:], bank[6][0:HD, 0:P], low_half[:], ALU.add).then_inc(o_done, 1)

        @block.gpsimd
        def _(pool):
            pool.sem_inc(opart_done, PRIME)
            with pool.Fori(0, HEADS // HG) as i:
                pool.wait_ge(o_done, i + 1 + PRIME)
                pool.sem_inc(passed, 1)
                pool.wait_ge(stored, 16 * 2 * i)
                pool.sem_inc(passed, 1)
                pool.tensor_copy(oparts[:, 0, :], o_t[:]).then_inc(opart_done, 1)
                pool.wait_ge(opart_done, 2 * i + 1 + PRIME)
                pool.sem_inc(passed, 1)
                pool.tensor_tensor(oparts[:, 1, :], o_t[:], r32(oparts[:, 0, :]), ALU.subtract).then_inc(opart_done, 1)
                pool.wait_ge(opart_done, 2 * i + 2 + PRIME)
                pool.sem_inc(passed, 1)
                for j in range(2):
                    pool.dma_start(r32(mixT_d[j, bass.ds(HG * HD * i, HG * HD), SEQ:TOK].rearrange("(h d) t -> d h t", h=HG)),
                                   r32(oparts[:, j, :].rearrange("d (h t) -> d h t", h=HG))).then_inc(stored, 16)
            pool.wait_ge(stored, 16 * 2 * (HEADS // HG))


def mix_norm(nc, ctx, sem, sb, passed, bank, ident, eps_t, blk, xp, xs, mixT_d, w_out, ln_g, ln_b, x1T, acc):
    wo = [sb(ctx, f"wo{j}_{blk}", [P, KD, D], F32R) for j in range(2)]
    xin = [sb(ctx, f"mx{u}_{blk}", [P, D]) for u in range(2)]
    mixT = [sb(ctx, f"mixT{u}_{blk}", [P, 2, KD, P], F32R) for u in range(2)]
    x1n = xin
    gain, bias = sb(ctx, f"g1_{blk}", [P, D]), sb(ctx, f"b1_{blk}", [P, D])
    stats = sb(ctx, f"st1_{blk}", [P, 2, 6])
    mv = sb(ctx, f"mv1_{blk}", [P, 2])
    lnv, rstd = sb(ctx, f"lnv1_{blk}", [P, 1]), sb(ctx, f"rs1_{blk}", [P, 1])

    def c(n):
        return sem(f"m{blk}_{n}")

    wo_loaded = [sem(f"m{blk}_wo_loaded{u}") for u in range(2)]
    x_loaded = [sem(f"m{blk}_x_loaded{u}") for u in range(2)]
    mixT_loaded = [sem(f"m{blk}_mixT_loaded{u}") for u in range(2)]
    par_loaded = sem(f"m{blk}_par_loaded")
    wo_hi, wo_lo, sums, added, bn, var, lnd, rs, normed, scaled, shifted, turned, hi, lo, kept = (
        c(n) for n in ("wo_hi", "wo_lo", "sums", "added", "bn", "var", "ln", "rs", "normed", "scaled", "shifted",
                       "turned", "hi", "lo", "kept"))
    t0 = 8 * blk

    with nc.Block() as block:
        def tiles(eng, f):
            with eng.Fori(0, 4) as i:
                for u in range(2):
                    f(2 * i + u, u, i + 1, P)
            if blk == 1:
                f(8, 0, 5, DEC)

        @block.sync
        def _(sp):
            sp.dma_start(gain[:], ln_g.rearrange("(a n) -> a n", a=1).broadcast_to([P, D])).then_inc(par_loaded, 16)
            sp.dma_start(bias[:], ln_b.rearrange("(a n) -> a n", a=1).broadcast_to([P, D])).then_inc(par_loaded, 16)
            with sp.Fori(0, KD // 2) as i:
                for u in range(2):
                    sp.wait_ge(wo_lo, 2 * i + u - 1 + PRIME)
                    sp.sem_inc(passed, 1)
                    sp.dma_start(xin[u][:], w_out[bass.ds((2 * i + u) * P, P), :]).then_inc(wo_loaded[u], 16)
            sp.wait_ge(wo_lo, KD + PRIME)

            def load(t, u, times, rows):
                sp.wait_ge(kept, t - 1 + PRIME)
                sp.sem_inc(passed, 1)
                sp.wait_ge(turned, t - 1 + PRIME)
                sp.sem_inc(passed, 1)
                if rows == P:
                    sp.dma_start(xin[u][:], xp[bass.ds((t + t0) * P, P), :]).then_inc(x_loaded[u], 16)
                else:
                    sp.dma_start(xin[u][0:DEC, :], xs).then_inc(x_loaded[u], 16)
                sp.wait_ge(sums, 2 * (t - 1) + PRIME)
                sp.sem_inc(passed, 1)
                for j in range(2):
                    sp.dma_start(r32(mixT[u][:, j, :, 0:rows]),
                                 r32(mixT_d[j].rearrange("(k p) t -> p k t", p=P)[:, :, bass.ds((t + t0) * P, rows)]))\
                      .then_inc(mixT_loaded[u], 16)

            tiles(sp, load)

        @block.tensor
        def _(pe):
            pe.sem_inc(sums, PRIME)
            pe.sem_inc(turned, PRIME)
            pe.wait_ge(wo_lo, KD + PRIME)

            def project(t, u, times, rows):
                pe.wait_ge(mixT_loaded[u], 32 * times)
                for half in range(2):
                    pe.wait_ge(added, 2 * (t - 1) + half + PRIME)
                    for k in range(KD):
                        for n, (a, w) in enumerate(((0, 0), (0, 1), (1, 0))):
                            m = pe.matmul(bank[2 * u + half][:], mixT[u][:, a, k, :], wo[w][:, k, half * 512:half * 512 + 512],
                                          start=k == 0 and n == 0, stop=k == KD - 1 and n == 2)
                    m.then_inc(sums, 1)

            def turn(t, u, times, rows):
                pe.wait_ge(shifted, t + 1 + PRIME)
                pe.wait_ge(lo, t - 1 + PRIME)
                for k in range(KD):
                    m = pe.transpose(bank[4 + 2 * u + k // 4][:, (k % 4) * P:(k % 4) * P + rows],
                                     x1n[u][0:rows, k * P:(k + 1) * P], ident[0:rows, 0:rows])
                m.then_inc(turned, 1)

            project(0, 0, 1, P)
            with pe.Fori(0, 3) as i:
                for u in range(2):
                    project(2 * i + u + 1, 1 - u, i + 1 + u, P)
                    turn(2 * i + u, u, i + 1, P)
            project(7, 1, 4, P)
            turn(6, 0, 4, P)
            if blk == 1:
                project(8, 0, 5, DEC)
            turn(7, 1, 4, P)
            if blk == 1:
                turn(8, 0, 5, DEC)

        @block.scalar
        def _(act):
            for x in (wo_hi, lnd, rs, hi, kept):
                act.sem_inc(x, PRIME)
            with act.Fori(0, KD // 2) as i:
                for u in range(2):
                    act.wait_ge(wo_loaded[u], 16 * i + 16)
                    act.activation(wo[0][:, bass.ds(2 * i + u, 1), :].rearrange("p a n -> p (a n)"), xin[u][:], ACT.Copy)\
                       .then_inc(wo_hi, 1)

            def norm(t, u, times, rows):
                act.wait_ge(var, t + 1 + PRIME)
                act.activation(lnv[:], mv[:, 1:2], ACT.Ln, bias=eps_t[:]).then_inc(lnd, 1)
                act.wait_ge(lnd, t + 1 + PRIME)
                act.activation(rstd[:], lnv[:], ACT.Exp, scale=-0.5).then_inc(rs, 1)
                act.wait_ge(shifted, t + 1 + PRIME)
                act.activation(acc[:, bass.ds(t, 1), :].rearrange("p a n -> p (a n)"), x1n[u][:], ACT.Copy, scale=ALPHA)\
                   .then_inc(kept, 1)
                act.wait_ge(turned, t + 1 + PRIME)
                for b in range(2):
                    m = act.activation(x1T[0][:, 4 * b:4 * b + 4, bass.ds(t * P, rows)],
                                       bank[4 + 2 * u + b][:, :].rearrange("p (k n) -> p k n", k=4)[:, :, 0:rows],
                                       ACT.Copy)
                m.then_inc(hi, 1)

            tiles(act, norm)

        @block.vector
        def _(dve):
            for x in (wo_lo, added, bn, var, normed, lo):
                dve.sem_inc(x, PRIME)
            with dve.Fori(0, KD // 2) as i:
                for u in range(2):
                    dve.wait_ge(wo_hi, 2 * i + u + 1 + PRIME)
                    s = (slice(None), bass.ds(2 * i + u, 1), slice(None))
                    dve.tensor_tensor(wo[1][s].rearrange("p a n -> p (a n)"), xin[u][:],
                                      r32(wo[0][s]).rearrange("p a n -> p (a n)"), ALU.subtract).then_inc(wo_lo, 1)

            def norm(t, u, times, rows):
                dve.wait_ge(x_loaded[u], 16 * times)
                for half in range(2):
                    dve.wait_ge(sums, 2 * t + half + 1 + PRIME)
                    s = slice(half * 512, half * 512 + 512)
                    dve.scalar_tensor_tensor(x1n[u][:, s], xin[u][:, s], ALPHA, bank[2 * u + half][:],
                                             ALU.mult, ALU.add).then_inc(added, 1)
                for half in range(2):
                    dve.wait_ge(added, 2 * t + half + 1 + PRIME)
                    dve.bn_stats(stats[:, half, :], x1n[u][:, half * 512:half * 512 + 512]).then_inc(bn, 1)
                dve.wait_ge(bn, 2 * t + 2 + PRIME)
                dve.wait_ge(rs, t + PRIME)
                dve.sem_inc(passed, 1)
                dve.bn_aggr(mv[:], stats[:].rearrange("p a b -> p (a b)")).then_inc(var, 1)
                dve.wait_ge(rs, t + 1 + PRIME)
                dve.tensor_scalar(x1n[u][:], x1n[u][:], mv[:, 0:1], rstd[:, 0:1], ALU.subtract, ALU.mult)\
                   .then_inc(normed, 1)

            def low(t, u, times, rows):
                dve.wait_ge(hi, t + 1 + PRIME)
                for b in range(2):
                    s = (slice(None), slice(4 * b, 4 * b + 4), bass.ds(t * P, rows))
                    m = dve.tensor_tensor(x1T[1][s], bank[4 + 2 * u + b][:, :].rearrange("p (k n) -> p k n", k=4)[:, :, 0:rows],
                                          r32(x1T[0][s]), ALU.subtract)
                m.then_inc(lo, 1)

            def both(t, u, times, rows):
                norm(t, u, times, rows)
                low(t, u, times, rows)

            tiles(dve, both)

        @block.gpsimd
        def _(pool):
            pool.sem_inc(scaled, PRIME)
            pool.sem_inc(shifted, PRIME)
            pool.wait_ge(par_loaded, 32)

            def affine(t, u, times, rows):
                pool.wait_ge(normed, t + 1 + PRIME)
                pool.sem_inc(passed, 1)
                pool.tensor_tensor(x1n[u][:], x1n[u][:], gain[:], ALU.mult).then_inc(scaled, 1)
                pool.wait_ge(scaled, t + 1 + PRIME)
                pool.sem_inc(passed, 1)
                pool.tensor_tensor(x1n[u][:], x1n[u][:], bias[:], ALU.add).then_inc(shifted, 1)

            tiles(pool, affine)


def ffn(nc, ctx, sem, sb, passed, bank, blk, width, tiles, w_gate, w_up, w_down, x1T, acc):
    NT = 3 if blk else 2
    TW = width // NT
    graw = [sb(ctx, f"graw{j}_{blk}", [P, KD, P]) for j in range(2)]
    gw = [[[sb(ctx, f"gw{u}{g}{j}_{blk}", [P, KD, P], F32R) for j in range(2)] for g in range(2)] for u in range(2)]
    draw = sb(ctx, f"draw_{blk}", [P, D])
    dw = [[sb(ctx, f"dw{u}{j}_{blk}", [P, D], F32R) for j in range(2)] for u in range(2)]
    hT = [[sb(ctx, f"hT{u}{j}_{blk}", [P, tiles * P], F32R) for j in range(2)] for u in range(2)]
    e_t = [sb(ctx, f"fe{b}_{blk}", [P, TW]) for b in range(2)]
    h_t = [sb(ctx, f"fh{b}_{blk}", [P, TW]) for b in range(2)]

    def c(n):
        return sem(f"f{blk}_{n}")

    g_loaded, d_loaded = sem(f"f{blk}_g_loaded"), sem(f"f{blk}_d_loaded")
    pad = sem(f"f{blk}_pad")
    g_hi, g_lo, d_hi, d_lo = c("g_hi"), c("g_lo"), c("d_hi"), c("d_lo")
    gate_up, absd, exped, logd, logsig, sig, silu, prod, h_hi, h_lo = (
        c(n) for n in ("gate_up", "abs", "exp", "log", "logsig", "sig", "silu", "prod", "h_hi", "h_lo"))
    down, summed = c("down"), c("summed")
    ND = 2 * tiles

    def pipeline(eng, first, second):
        first(0, 0)
        with eng.Fori(0, FC // 2 - 1) as i:
            first(2 * i + 1, 1)
            second(2 * i, 0)
            first(2 * i + 2, 0)
            second(2 * i + 1, 1)
        first(FC - 1, 1)
        second(FC - 2, 0)
        second(FC - 1, 1)

    with nc.Block() as block:
        @block.sync
        def _(sp):
            with sp.Fori(0, FC) as f:
                sp.wait_ge(g_lo, f + PRIME)
                sp.sem_inc(passed, 1)
                for j, w in enumerate((w_gate, w_up)):
                    sp.dma_start(graw[j][:], w.rearrange("(k p) f -> p k f", p=P)[:, :, bass.ds(f * P, P)])\
                      .then_inc(g_loaded, 16)
                sp.wait_ge(d_lo, f + PRIME)
                sp.sem_inc(passed, 1)
                sp.dma_start(draw[:], w_down[bass.ds(f * P, P), :]).then_inc(d_loaded, 16)

        @block.tensor
        def _(pe):
            pe.sem_inc(gate_up, PRIME)
            pe.sem_inc(down, PRIME)
            if blk:
                pe.wait_ge(pad, 4)

            def gates(f, u):
                pe.wait_ge(g_lo, f + 1 + PRIME)
                for n in range(NT):
                    pe.wait_ge(prod, NT * f + n - 1 + PRIME)
                    b = (NT * u + n) % 2
                    for g in range(2):
                        for k in range(KD):
                            for s, (w, x) in enumerate(((0, 0), (0, 1), (1, 0))):
                                m = pe.matmul(bank[2 * b + g][:, 0:TW], gw[u][g][w][:, k, :],
                                              x1T[x][:, k, n * TW:(n + 1) * TW],
                                              start=k == 0 and s == 0, stop=k == KD - 1 and s == 2)
                    m.then_inc(gate_up, 1)

            def downs(f, u):
                pe.wait_ge(d_lo, f + 1 + PRIME)
                for t in range(tiles):
                    pe.wait_ge(h_lo, NT * f + min(NT, ((t + 1) * P - 1) // TW + 1) + PRIME)
                    for half in range(2):
                        n = 2 * t + half
                        pe.wait_ge(summed, ND * f + n - 3 + PRIME)
                        for s, (a, w) in enumerate(((0, 0), (0, 1), (1, 0))):
                            m = pe.matmul(bank[4 + (ND * u + n) % 4][:], hT[u][a][:, t * P:(t + 1) * P],
                                          dw[u][w][:, half * 512:half * 512 + 512], start=s == 0, stop=s == 2)
                        m.then_inc(down, 1)

            pipeline(pe, gates, downs)

        @block.scalar
        def _(act):
            for x in (g_hi, d_hi, absd, exped, logd, sig, h_hi):
                act.sem_inc(x, PRIME)

            def split_gate(f, u):
                act.wait_ge(g_loaded, 32 * f + 32)
                act.wait_ge(gate_up, NT * (f - 1) + PRIME)
                act.activation(gw[u][0][0][:], graw[0][:], ACT.Copy)
                act.activation(gw[u][1][0][:], graw[1][:], ACT.Copy).then_inc(g_hi, 1)

            def split_down(f, u):
                act.wait_ge(d_loaded, 16 * f + 16)
                act.wait_ge(down, ND * (f - 1) + PRIME)
                act.activation(dw[u][0][:], draw[:], ACT.Copy).then_inc(d_hi, 1)

            def hidden(f, u):
                for n in range(NT + 1):
                    if n < NT:
                        b = (NT * u + n) % 2
                        act.wait_ge(gate_up, NT * f + n + 1 + PRIME)
                        act.wait_ge(silu, NT * f + n - 1 + PRIME)
                        act.activation(e_t[b][:], bank[2 * b][:, 0:TW], ACT.Abs).then_inc(absd, 1)
                        act.wait_ge(absd, NT * f + n + 1 + PRIME)
                        act.activation(e_t[b][:], e_t[b][:], ACT.Exp, scale=-1.0).then_inc(exped, 1)
                        act.wait_ge(exped, NT * f + n + 1 + PRIME)
                        act.activation(e_t[b][:], e_t[b][:], ACT.Ln, bias=1.0).then_inc(logd, 1)
                    if n:
                        m = n - 1
                        b = (NT * u + m) % 2
                        act.wait_ge(prod, NT * f + m + 1 + PRIME)
                        act.wait_ge(down, ND * (f - 1) + PRIME)
                        act.activation(hT[u][0][:, m * TW:(m + 1) * TW], h_t[b][:], ACT.Copy).then_inc(h_hi, 1)
                    if n < NT:
                        b = (NT * u + n) % 2
                        act.wait_ge(logsig, NT * f + n + 1 + PRIME)
                        act.activation(e_t[b][:], e_t[b][:], ACT.Exp).then_inc(sig, 1)

            split_gate(0, 0)
            with act.Fori(0, FC // 2 - 1) as i:
                split_gate(2 * i + 1, 1)
                hidden(2 * i, 0)
                split_down(2 * i, 0)
                split_gate(2 * i + 2, 0)
                hidden(2 * i + 1, 1)
                split_down(2 * i + 1, 1)
            split_gate(FC - 1, 1)
            hidden(FC - 2, 0)
            split_down(FC - 2, 0)
            hidden(FC - 1, 1)
            split_down(FC - 1, 1)

        @block.vector
        def _(dve):
            for x in (g_lo, d_lo, logsig, silu, prod, h_lo, summed):
                dve.sem_inc(x, PRIME)
            if blk:
                for u in range(2):
                    for j in range(2):
                        dve.memset(r32(hT[u][j][:, width:tiles * P]), 0.0).then_inc(pad, 1)

            def split_gate(f, u):
                dve.wait_ge(g_hi, f + 1 + PRIME)
                dve.tensor_tensor(gw[u][0][1][:], graw[0][:], r32(gw[u][0][0][:]), ALU.subtract)
                dve.tensor_tensor(gw[u][1][1][:], graw[1][:], r32(gw[u][1][0][:]), ALU.subtract).then_inc(g_lo, 1)

            def split_down(f, u):
                dve.wait_ge(d_hi, f + 1 + PRIME)
                dve.tensor_tensor(dw[u][1][:], draw[:], r32(dw[u][0][:]), ALU.subtract).then_inc(d_lo, 1)

            def hidden(f, u):
                for n in range(NT):
                    b = (NT * u + n) % 2
                    dve.wait_ge(logd, NT * f + n + 1 + PRIME)
                    dve.scalar_tensor_tensor(e_t[b][:], bank[2 * b][:, 0:TW], 0.0, e_t[b][:],
                                             ALU.min, ALU.subtract).then_inc(logsig, 1)
                    dve.wait_ge(sig, NT * f + n + 1 + PRIME)
                    dve.wait_ge(h_hi, NT * f + n - 1 + PRIME)
                    dve.wait_ge(h_lo, NT * f + n - 1 + PRIME)
                    dve.tensor_tensor(h_t[b][:], bank[2 * b][:, 0:TW], e_t[b][:], ALU.mult).then_inc(silu, 1)
                    dve.wait_ge(silu, NT * f + n + 1 + PRIME)
                    dve.tensor_tensor(h_t[b][:], bank[2 * b + 1][:, 0:TW], h_t[b][:], ALU.mult).then_inc(prod, 1)
                    dve.wait_ge(h_hi, NT * f + n + 1 + PRIME)
                    dve.tensor_tensor(hT[u][1][:, n * TW:(n + 1) * TW], h_t[b][:],
                                      r32(hT[u][0][:, n * TW:(n + 1) * TW]), ALU.subtract).then_inc(h_lo, 1)

            def sums(f, u):
                for n in range(ND):
                    dve.wait_ge(down, ND * f + n + 1 + PRIME)
                    dve.wait_ge(summed, ND * (f - 1) + n + 1 + PRIME)
                    s = acc[:, n // 2, (n % 2) * 512:(n % 2) * 512 + 512]
                    dve.tensor_tensor(s, bank[4 + (ND * u + n) % 4][:], s, ALU.add).then_inc(summed, 1)

            split_gate(0, 0)
            split_gate(1, 1)
            hidden(0, 0)
            split_down(0, 0)
            with dve.Fori(0, FC // 2 - 1) as i:
                split_gate(2 * i + 2, 0)
                hidden(2 * i + 1, 1)
                split_down(2 * i + 1, 1)
                sums(2 * i, 0)
                split_gate(2 * i + 3, 1)
                hidden(2 * i + 2, 0)
                split_down(2 * i + 2, 0)
                sums(2 * i + 1, 1)
            hidden(FC - 1, 1)
            split_down(FC - 1, 1)
            sums(FC - 2, 0)
            sums(FC - 1, 1)


def final_norm(nc, ctx, sem, sb, passed, eps_t, blk, acc, ln_g, ln_b, yp, ys):
    y = [sb(ctx, f"y{u}_{blk}", [P, D]) for u in range(2)]
    gain, bias = sb(ctx, f"g2_{blk}", [P, D]), sb(ctx, f"b2_{blk}", [P, D])
    stats = [sb(ctx, f"st2{u}_{blk}", [P, 2, 6]) for u in range(2)]
    mv = [sb(ctx, f"mv2{u}_{blk}", [P, 2]) for u in range(2)]
    lnv, rstd = sb(ctx, f"lnv2_{blk}", [P, 1]), [sb(ctx, f"rs2{u}_{blk}", [P, 1]) for u in range(2)]
    par_loaded = sem(f"n{blk}_par_loaded")
    stored = [sem(f"n{blk}_stored{u}") for u in range(2)]
    bn, var, lnd, rs, normed, scaled, shifted = (
        sem(f"n{blk}_{n}") for n in ("bn", "var", "ln", "rs", "normed", "scaled", "shifted"))
    t0 = 8 * blk

    with nc.Block() as block:
        def tiles(eng, f):
            with eng.Fori(0, 4) as i:
                for u in range(2):
                    f(2 * i + u, u, i, P)
            if blk == 1:
                f(8, 0, 4, DEC)

        @block.sync
        def _(sp):
            sp.dma_start(gain[:], ln_g.rearrange("(a n) -> a n", a=1).broadcast_to([P, D])).then_inc(par_loaded, 16)
            sp.dma_start(bias[:], ln_b.rearrange("(a n) -> a n", a=1).broadcast_to([P, D])).then_inc(par_loaded, 16)

            def store(t, u, times, rows):
                sp.wait_ge(shifted, t + 1 + PRIME)
                sp.sem_inc(passed, 1)
                if rows == P:
                    sp.dma_start(yp[bass.ds((t + t0) * P, P), :], y[u][:]).then_inc(stored[u], 16)
                else:
                    sp.dma_start(ys, y[u][0:DEC, :]).then_inc(stored[u], 16)

            tiles(sp, store)
            sp.wait_ge(stored[0], 16 * (4 + blk))
            sp.sem_inc(passed, 1)
            sp.wait_ge(stored[1], 16 * 4)

        @block.scalar
        def _(act):
            act.sem_inc(lnd, PRIME)
            act.sem_inc(rs, PRIME)

            def dev(t, u, times, rows):
                act.wait_ge(var, t + 1 + PRIME)
                act.activation(lnv[:], mv[u][:, 1:2], ACT.Ln, bias=eps_t[:]).then_inc(lnd, 1)
                act.wait_ge(lnd, t + 1 + PRIME)
                act.wait_ge(normed, t - 1 + PRIME)
                act.activation(rstd[u][:], lnv[:], ACT.Exp, scale=-0.5).then_inc(rs, 1)

            tiles(act, dev)

        @block.vector
        def _(dve):
            for x in (bn, var, normed):
                dve.sem_inc(x, PRIME)

            def norm(t, u, times, rows):
                row = acc[:, bass.ds(t, 1), :].rearrange("p a n -> p (a n)")
                for half in range(2):
                    m = dve.bn_stats(stats[u][:, half, :], row[:, half * 512:half * 512 + 512])
                m.then_inc(bn, 1)
                dve.wait_ge(bn, t + 1 + PRIME)
                dve.wait_ge(rs, t - 1 + PRIME)
                dve.sem_inc(passed, 1)
                dve.bn_aggr(mv[u][:], stats[u][:].rearrange("p a b -> p (a b)")).then_inc(var, 1)
                dve.wait_ge(rs, t + 1 + PRIME)
                dve.wait_ge(stored[u], 16 * times)
                dve.tensor_scalar(y[u][:], row, mv[u][:, 0:1], rstd[u][:, 0:1], ALU.subtract, ALU.mult)\
                   .then_inc(normed, 1)

            tiles(dve, norm)

        @block.gpsimd
        def _(pool):
            pool.sem_inc(scaled, PRIME)
            pool.sem_inc(shifted, PRIME)
            pool.wait_ge(par_loaded, 32)

            def affine(t, u, times, rows):
                pool.wait_ge(normed, t + 1 + PRIME)
                pool.sem_inc(passed, 1)
                pool.tensor_tensor(y[u][:], y[u][:], gain[:], ALU.mult).then_inc(scaled, 1)
                pool.wait_ge(scaled, t + 1 + PRIME)
                pool.sem_inc(passed, 1)
                pool.tensor_tensor(y[u][:], y[u][:], bias[:], ALU.add).then_inc(shifted, 1)

            tiles(pool, affine)


_INS = ["x_prompt", "x_sample", "cache_k", "cache_v", "state_pool", "w_in", "pool_w", "pool_scale", "w_out",
        "ln1_g", "ln1_b", "w_gate", "w_up", "w_down", "ln2_g", "ln2_b"]
_OUTS = [(1, SEQ, D), (1, DEC, D), (1, SEQ, HEADS, HD), (1, SEQ, HEADS, HD), (1, HIST, SBW),
         (1, DEC, HEADS, HD), (1, DEC, HEADS, HD), (1, HIST, SBW)]


def kernel(**inputs):
    import numpy as _np
    import concourse.bacc as _bacc
    from concourse import mybir as _mybir
    from concourse.bass_utils import run_bass_kernel_spmd as _run

    nc = _bacc.Bacc("TRN2", target_bir_lowering=False, num_devices=1)
    arrays, args = {}, []
    for name in _INS:
        a = _np.ascontiguousarray(inputs[name])
        arrays[f"in_{name}_dram"] = a
        args.append(nc.dram_tensor(f"in_{name}_dram", a.shape, _mybir.dt.from_np(a.dtype), kind="ExternalInput").ap())
    for i, shape in enumerate(_OUTS):
        args.append(nc.dram_tensor(f"out_{i}_dram", shape, _mybir.dt.float32, kind="ExternalOutput").ap())
    build(nc, *args)
    r = _run(nc, [arrays], core_ids=[0])
    return tuple(r.results[0][f"out_{i}_dram"] for i in range(len(_OUTS)))
```

```python
from collections import namedtuple
from contextlib import ExitStack, contextmanager

import concourse.bass as bass
from concourse import mybir

F32 = mybir.dt.float32
F32R = mybir.dt.float32r
ALU = mybir.AluOpType
ACT = mybir.ActivationFunctionType

P = 128
D = 1024
KD = D // P
SEQ = 2048
DEC = 32
TOK = SEQ + DEC
PT = SEQ // P
PAST = 1024
CT = PAST // P
SBW = 512
HEADS = 8
HD = 64
HC = SBW // P
WINDOWS = (2, 4, 8, 16)
HIST = 15
FF = 2816
FC = FF // P
ALPHA = 2.0 ** 0.25
EPS = 1e-5
PRIME = 96
NEG = -(2.0 ** 100)
TB = 416
NB = TOK // TB

Item = namedtuple("Item", "head tile key0 width first last group starts_group ends_group")
ITEMS = [Item(u, q, 512 * c, 512 if c < q // 4 else (q % 4 + 1) * P, c == q // 4, c == 0,
              PT // 4 * u + q // 4, q % 4 == 0 and c == q // 4, q % 4 == 3 and c == 0)
         for u in range(2) for q in range(PT) for c in range(q // 4, -1, -1)]
NI = len(ITEMS) // 2
ITEMS += [Item(2, 0, k0, w, k0 == PAST, k0 == 0, PT // 2, k0 == PAST, k0 == 0)
          for k0, w in ((PAST, P), (5 * P, 3 * P), (2 * P, 3 * P), (0, 2 * P))]


def r32(ap):
    return ap.bitcast(F32)


def build(nc, x_prompt, x_sample, cache_k, cache_v, state_pool, w_in, pool_w, pool_scale, w_out,
          ln1_g, ln1_b, w_gate, w_up, w_down, ln2_g, ln2_b,
          y_prompt, y_sample, k_prompt, v_prompt, pool_prompt, k_sample, v_sample, pool_sample):
    xp = x_prompt.rearrange("a t d -> (a t) d")
    xs = x_sample.rearrange("a t d -> (a t) d")
    ck = cache_k.rearrange("a t h d -> (a t) (h d)")
    cv = cache_v.rearrange("a t h d -> (a t) (h d)")
    sp = state_pool.rearrange("a t c -> (a t) c")
    yp = y_prompt.rearrange("a t d -> (a t) d")
    ys = y_sample.rearrange("a t d -> (a t) d")
    kp_out = k_prompt.rearrange("a t h d -> (a t) (h d)")
    vp_out = v_prompt.rearrange("a t h d -> (a t) (h d)")
    ks_out = k_sample.rearrange("a t h d -> (a t) (h d)")
    vs_out = v_sample.rearrange("a t h d -> (a t) (h d)")
    pp_out = pool_prompt.rearrange("a t c -> (a t) c")
    ps_out = pool_sample.rearrange("a t c -> (a t) c")

    qT_d = nc.dram_tensor("qT_scratch", [2, SBW, TOK], F32R).ap()
    kT_d = nc.dram_tensor("kT_scratch", [2, SBW, TOK], F32R).ap()
    kcT_d = nc.dram_tensor("kcT_scratch", [2, SBW, PAST], F32R).ap()
    v_d = nc.dram_tensor("v_scratch", [TOK, HEADS, 2, HD], F32R).ap()
    vc_d = nc.dram_tensor("vc_scratch", [PAST, HEADS, 2, HD], F32R).ap()
    mixT_d = nc.dram_tensor("mixT_scratch", [2, D, TOK], F32R).ap()

    top = ExitStack()
    used = []

    def sem(n):
        used.append(nc.alloc_semaphore(name=n))
        return used[-1]

    @contextmanager
    def phase():
        with ExitStack() as ctx:
            yield ctx
            with nc.Block() as block:
                @block.sync
                def _(sp):
                    for x in used:
                        sp.sem_clear(x)
            for x in used:
                nc.release_semaphore(x)
            used.clear()

    def sb(ctx, n, shape, dt=F32):
        return ctx.enter_context(nc.sbuf_tensor(n, shape, dt))

    with top:
        passed = nc.alloc_semaphore(name="passed")
        bank = [top.enter_context(nc.psum_tensor(f"bank{i}", [P, 512], F32)) for i in range(8)]
        ident = sb(top, "ident", [P, P])
        ident_r = sb(top, "ident_r", [P, P], F32R)
        mask = sb(top, "mask", [P, P])
        mask_r = sb(top, "mask_r", [P, P], F32R)
        maskd_r = sb(top, "maskd_r", [P, P], F32R)
        eps_t = sb(top, "eps_t", [P, 1])

        constants(nc, sem, ident, ident_r, mask, mask_r, maskd_r, eps_t)
        with phase() as ctx:
            xT = [sb(ctx, f"xT{j}", [P, KD, TOK], F32R) for j in range(2)]
            transpose_x(nc, ctx, sem, sb, passed, bank, ident, xp, xs, xT)
            project(nc, ctx, sem, sb, passed, bank, ident, xT, w_in, sp, pool_w, pool_scale,
                    qT_d, kT_d, v_d, mixT_d, kp_out, vp_out, ks_out, vs_out, pp_out, ps_out)
        with phase() as ctx:
            split_cache(nc, ctx, sem, sb, passed, bank, ident, ck, cv, kcT_d, vc_d)
        with phase() as ctx:
            attend(nc, ctx, sem, sb, passed, bank, ident, ident_r, mask_r, maskd_r, cv, qT_d, kT_d, kcT_d,
                   vp_out, vs_out, mixT_d)
        for blk in range(2):
            tiles = 8 + blk
            width = 1024 + DEC * blk
            with ExitStack() as ctx:
                x1T = [sb(ctx, f"x1T{j}_{blk}", [P, KD, width], F32R) for j in range(2)]
                acc = sb(ctx, f"acc_{blk}", [P, tiles, D])
                with phase() as inner:
                    mix_norm(nc, inner, sem, sb, passed, bank, ident, eps_t, blk, xp, xs, mixT_d, w_out,
                             ln1_g, ln1_b, x1T, acc)
                with phase() as inner:
                    ffn(nc, inner, sem, sb, passed, bank, blk, width, tiles, w_gate, w_up, w_down, x1T, acc)
                with phase() as inner:
                    final_norm(nc, inner, sem, sb, passed, eps_t, blk, acc, ln2_g, ln2_b, yp, ys)


def constants(nc, sem, ident, ident_r, mask, mask_r, maskd_r, eps_t):
    filled, made, cast = sem("c_filled"), sem("c_made"), sem("c_cast")
    with nc.Block() as block:
        @block.scalar
        def _(act):
            act.preload_act_table_set("natural_log_exp_and_others")

        @block.gpsimd
        def _(pool):
            pool.memset(ident[:], 0.0).then_inc(filled, 1)
            pool.memset(mask[:], 0.0).then_inc(filled, 1)
            pool.wait_ge(filled, 2)
            pool.affine_select(out=ident[:], in_=ident[:], compare_op=ALU.not_equal, fill=1.0, base=0,
                               pattern=[[-1, P]], channel_multiplier=1).then_inc(made, 1)
            pool.affine_select(out=mask[:], in_=mask[:], compare_op=ALU.is_gt, fill=NEG, base=0,
                               pattern=[[-1, P]], channel_multiplier=1).then_inc(made, 1)

        @block.vector
        def _(dve):
            dve.memset(eps_t[:], EPS)
            dve.memset(r32(maskd_r[:]), NEG).then_inc(cast, 1)
            dve.wait_ge(made, 2)
            dve.wait_ge(cast, 1)
            dve.tensor_copy(ident_r[:], ident[:])
            dve.tensor_copy(mask_r[:], mask[:])
            for h in range(4):
                s = slice(DEC * h, DEC * h + DEC)
                dve.tensor_copy(maskd_r[s, 0:DEC], mask[s, s])


def transpose_x(nc, ctx, sem, sb, passed, bank, ident, xp, xs, xT):
    with ExitStack() as mem:
        xin = [sb(mem, f"xin{u}", [P, D]) for u in range(2)]
        loaded = [sem(f"x_loaded{u}") for u in range(2)]
        turned, hi_done, lo_done = sem("x_turned"), sem("x_hi"), sem("x_lo")

        def ps(u):
            return bank[2 * u], bank[2 * u + 1]

        with nc.Block() as block:
            @block.sync
            def _(sp):
                with sp.Fori(0, PT // 2) as i:
                    for u in range(2):
                        sp.wait_ge(turned, 2 * i + u - 1 + PRIME)
                        sp.sem_inc(passed, 1)
                        sp.dma_start(xin[u][:], xp[bass.ds((2 * i + u) * P, P), :]).then_inc(loaded[u], 16)
                sp.wait_ge(turned, PT - 1 + PRIME)
                sp.dma_start(xin[0][0:DEC, :], xs).then_inc(loaded[0], 16)

            @block.tensor
            def _(pe):
                pe.sem_inc(turned, PRIME)

                def turn(t, u, rows, times):
                    pe.wait_ge(loaded[u], 16 * times)
                    pe.wait_ge(lo_done, t - 1 + PRIME)
                    for k in range(KD):
                        m = pe.transpose(ps(u)[k // 4][:, (k % 4) * P:(k % 4) * P + rows],
                                         xin[u][0:rows, k * P:(k + 1) * P], ident[0:rows, 0:rows])
                    m.then_inc(turned, 1)

                with pe.Fori(0, PT // 2) as i:
                    for u in range(2):
                        turn(2 * i + u, u, P, i + 1)
                turn(PT, 0, DEC, PT // 2 + 1)

            def halves(t, u, rows):
                for b in range(2):
                    yield b, ps(u)[b][:, :].rearrange("p (k n) -> p k n", k=4)[:, :, 0:rows], \
                        (slice(None), slice(4 * b, 4 * b + 4), bass.ds(t * P, rows))

            @block.scalar
            def _(act):
                act.sem_inc(hi_done, PRIME)

                def hi(t, u, rows):
                    act.wait_ge(turned, t + 1 + PRIME)
                    for _, src, at in halves(t, u, rows):
                        m = act.activation(xT[0][at], src, ACT.Copy)
                    m.then_inc(hi_done, 1)

                with act.Fori(0, PT // 2) as i:
                    for u in range(2):
                        hi(2 * i + u, u, P)
                hi(PT, 0, DEC)

            @block.vector
            def _(dve):
                dve.sem_inc(lo_done, PRIME)

                def lo(t, u, rows):
                    dve.wait_ge(hi_done, t + 1 + PRIME)
                    for _, src, at in halves(t, u, rows):
                        m = dve.tensor_tensor(xT[1][at], src, r32(xT[0][at]), ALU.subtract)
                    m.then_inc(lo_done, 1)

                with dve.Fori(0, PT // 2) as i:
                    for u in range(2):
                        lo(2 * i + u, u, P)
                lo(PT, 0, DEC)


def project(nc, ctx, sem, sb, passed, bank, ident, xT, w_in, sp_in, pool_w, pool_scale,
            qT_d, kT_d, v_d, mixT_d, kp_out, vp_out, ks_out, vs_out, pp_out, ps_out):
    CH = 16
    PAD = 16
    UW = PAD + SEQ + PAD + DEC
    S0 = PAD + SEQ + PAD
    wraw = [sb(ctx, f"wraw{u}", [P, KD, P]) for u in range(2)]
    whi = [sb(ctx, f"whi{u}", [P, KD, P], F32R) for u in range(2)]
    wlo = [sb(ctx, f"wlo{u}", [P, KD, P], F32R) for u in range(2)]
    col = [sb(ctx, f"col{u}", [P, UW]) for u in range(2)]
    parts = sb(ctx, "parts", [P, 2, 17 * P], F32R)
    vparts = parts[:, :, :].rearrange("p a (b c) -> p (a b c)", c=P).rearrange(
        "p (t h j d) -> p t h j d", t=17, h=2, j=2)
    nat = sb(ctx, "nat", [P, 17 * P])
    nat3 = nat[:, :].rearrange("p (t c) -> p t c", c=P)
    pw_raw = sb(ctx, "pw_raw", [P, 4, P])
    pw = [sb(ctx, f"pw_{n}", [P, P], F32R) for n in ("hi", "lo")]
    tails = [sb(ctx, f"tails{u}", [P, 2, P]) for u in range(2)]
    pscale = sb(ctx, "pscale", [P, 4])
    hist_in = sb(ctx, "hist_in", [DEC, SBW])
    hist = sb(ctx, "hist", [P, 4, PAD])
    rcount = sb(ctx, "rcount", [P, PAD])

    w_loaded = [sem(f"w_loaded{u}") for u in range(2)]
    w_hi, w_lo = sem("w_hi"), sem("w_lo")
    mm_done, col_done = sem("mm_done"), sem("col_done")
    parts_hi, parts_lo = sem("parts_hi"), sem("parts_lo")
    nat_turned, nat_done = sem("nat_turned"), sem("nat_done")
    stored = sem("p_stored")
    pre_loaded, pre_done = sem("pre_loaded"), sem("pre_done")
    hist_turned, hist_done = sem("hist_turned"), sem("hist_done")
    pooled_done, pooled_out = sem("pooled_done"), sem("pooled_out")
    d_done = sem("d_done")
    dve_chain = sem("p_dve_chain")

    wv = w_in.rearrange("(k p) n -> p k n", p=P)
    kinds = "qkv"
    N_ST = {"q": 2, "k": 4, "v": 4, "u": 4}

    def st_before(kind, c):
        return 16 * (sum(N_ST[k] * 4 for k in "qkvu"[:"qkvu".index(kind)]) + N_ST[kind] * c)

    NBT = 5

    def ladder(level):
        return (col[1], nat)[level % 2]

    def diff(c):
        return ladder(c + 1)

    def tok_cols(b):
        lo, hi = b * TB, (b + 1) * TB
        if hi <= SEQ:
            return [(0, TB, PAD + lo)]
        return [(0, SEQ - lo, PAD + lo), (SEQ - lo, hi - SEQ, S0)]

    with nc.Block() as block:
        @block.sync
        def _(sp):
            def load(n, u):
                sp.wait_ge(w_lo, n - 1 + PRIME)
                sp.sem_inc(passed, 1)
                sp.dma_start(wraw[u][:], wv[:, :, bass.ds(n * P, P)]).then_inc(w_loaded[u], 16)

            sp.wait_ge(pre_done, 1)
            sp.dma_start(hist_in[1:1 + HIST, :], sp_in).then_inc(pre_loaded, 16)
            sp.dma_start(pw_raw[:], pool_w.rearrange("g c d -> c g d")).then_inc(pre_loaded, 16)
            with nc.allow_non_contiguous_dma(reason="512 scales, one a partition"):
                sp.dma_start(pscale[:], pool_scale.rearrange("(g p) -> p g", p=P)).then_inc(pre_loaded, 16)
            load(0, 0)
            load(1, 1)

            def store_parts(n, dst, row, width):
                sp.wait_ge(parts_lo, n + 1 + PRIME)
                sp.sem_inc(passed, 1)
                for j in range(2):
                    sp.dma_start(r32(dst[j, bass.ds(row, P), :]), r32(parts[:, j, 0:width])).then_inc(stored, 16)

            with sp.Fori(0, 2) as i:
                for u in range(2):
                    load(2 * i + u + 2, u)
                    store_parts(2 * i + u, qT_d, (2 * i + u) * P, TOK)
            with sp.Fori(0, 2) as i:
                for u in range(2):
                    c = 2 * i + u
                    load(c + 6, u)
                    store_parts(c + 4, kT_d, c * P, TOK)
                    sp.wait_ge(nat_done, NBT * (c + 1) + PRIME)
                    sp.sem_inc(passed, 1)
                    sp.dma_start(kp_out.rearrange("(t p) c -> p t c", p=P)[:, :, bass.ds(c * P, P)],
                                 nat3[:, 0:PT, :]).then_inc(stored, 16)
                    sp.dma_start(ks_out[:, bass.ds(c * P, P)], nat3[0:DEC, PT, :]).then_inc(stored, 16)
            with sp.Fori(0, 2) as i:
                for u in range(2):
                    c = 2 * i + u
                    load(c + 10, u)
                    sp.wait_ge(parts_lo, c + 9 + PRIME)
                    sp.sem_inc(passed, 1)
                    sp.dma_start(vp_out.rearrange("(t p) c -> p t c", p=P)[:, :, bass.ds(c * P, P)],
                                 nat3[:, 0:PT, :]).then_inc(stored, 16)
                    sp.dma_start(vs_out[:, bass.ds(c * P, P)], nat3[0:DEC, PT, :]).then_inc(stored, 16)
                    vrow = v_d.rearrange("t h j d -> t (h j d)")
                    vflat = parts[:, :, :].rearrange("p a b -> p (a b)").rearrange("p (t n) -> p t n", t=17)
                    sp.dma_start(r32(vrow[0:SEQ, bass.ds(c * 2 * P, 2 * P)].rearrange("(t p) n -> p t n", p=P)),
                                 r32(vflat[:, 0:PT, :])).then_inc(stored, 16)
                    sp.dma_start(r32(vrow[SEQ:TOK, bass.ds(c * 2 * P, 2 * P)]),
                                 r32(vflat[0:DEC, PT, :])).then_inc(stored, 16)
            for c in range(4):
                if c < 2:
                    load(c + 14, c % 2)
                sp.wait_ge(hist_done, 2 + 2 * (c + 1))
                sp.sem_inc(passed, 1)
                sp.dma_start(pp_out[:, c * P:(c + 1) * P], tails[c % 2][P - HIST:P, 0, :]).then_inc(stored, 16)
                sp.dma_start(ps_out[:, c * P:(c + 1) * P], tails[c % 2][DEC - HIST:DEC, 1, :]).then_inc(stored, 16)
                sp.wait_ge(parts_lo, 12 + 2 * c + 2 + PRIME)
                sp.sem_inc(passed, 1)
                for j in range(2):
                    sp.dma_start(r32(mixT_d[j, SBW + c * P:SBW + (c + 1) * P, :]),
                                 r32(parts[:, j, 0:TOK])).then_inc(stored, 16)
            sp.wait_ge(stored, st_before("u", 4))
            sp.sem_inc(passed, 1)

        @block.scalar
        def _(act):
            for x in (w_hi, col_done, pooled_out):
                act.sem_inc(x, PRIME)

            def split_w(n, u, times):
                act.wait_ge(w_loaded[u], 16 * times)
                act.wait_ge(mm_done, NB * (n - 1) + PRIME)
                act.activation(whi[u][:], wraw[u][:], ACT.Copy).then_inc(w_hi, 1)

            def columns(n, u, scale):
                for b in range(NB):
                    act.wait_ge(mm_done, NB * n + b + 1 + PRIME)
                    act.activation(col[u][:, b * TB:(b + 1) * TB], bank[(NB * u + b) % 2][:, 0:TB],
                                   ACT.Copy, scale=scale).then_inc(col_done, 1)

            split_w(0, 0, 1)
            with act.Fori(0, 2) as i:
                for u in range(2):
                    n = 2 * i + u
                    split_w(n + 1, 1 - u, i + 1 + u)
                    act.wait_ge(parts_lo, n - 1 + PRIME)
                    columns(n, u, HD ** -0.5)
            with act.Fori(0, 2) as i:
                for u in range(2):
                    n = 2 * i + u + 4
                    split_w(n + 1, 1 - u, i + 3 + u)
                    act.wait_ge(parts_lo, n - 1 + PRIME)
                    act.wait_ge(nat_turned, NBT * (n - 5) + PRIME)
                    columns(n, u, 1.0)
            with act.Fori(0, 2) as i:
                for u in range(2):
                    n = 2 * i + u + 8
                    split_w(n + 1, 1 - u, i + 5 + u)
                    act.wait_ge(parts_lo, n - 1 + PRIME)
                    act.wait_ge(nat_turned, NBT * (n - 5) + PRIME)
                    columns(n, u, 1.0)
            act.wait_ge(pre_loaded, 48)
            for c in range(4):
                n = 12 + c
                if c < 3:
                    split_w(n + 1, (n + 1) % 2, (n + 1) // 2 + 1)
                act.wait_ge(parts_lo, 12 + 2 * c + PRIME)
                act.wait_ge(hist_done, 2 + 2 * c)
                if c == 0:
                    act.wait_ge(nat_turned, NBT * 8 + PRIME)
                for b in range(NB):
                    act.wait_ge(mm_done, NB * n + b + 1 + PRIME)
                    for s, w, at in tok_cols(b):
                        m = act.activation(col[0][:, at:at + w], bank[(NB * n + b) % 2][:, s:s + w], ACT.Copy)
                    m.then_inc(col_done, 1)
                for b in range(5):
                    w = 512 if b < 4 else DEC
                    act.wait_ge(pooled_done, 5 * c + b + 1 + PRIME)
                    m = act.activation(col[1][:, 512 * b:512 * b + w], bank[4 + b % 2][:, 0:w], ACT.Copy,
                                       scale=pscale[:, c:c + 1])
                    m.then_inc(pooled_out, 1)

        @block.tensor
        def _(pe):
            pe.sem_inc(mm_done, PRIME)
            pe.sem_inc(nat_turned, PRIME)
            pe.sem_inc(pooled_done, PRIME)
            pe.wait_ge(pre_loaded, 48)
            for g in range(4):
                m = pe.transpose(bank[6][:, g * DEC:(g + 1) * DEC], hist_in[:, g * P:(g + 1) * P],
                                 ident[0:DEC, 0:DEC])
            m.then_inc(hist_turned, 1)

            def products(n, u, par):
                pe.wait_ge(w_lo, n + 1 + PRIME)
                for b in range(NB):
                    pe.wait_ge(col_done, NB * n + b - 1 + PRIME)
                    ps = bank[(par + b) % 2][:, 0:TB]
                    for k in range(KD):
                        for j, (w, x) in enumerate(((whi, 0), (whi, 1), (wlo, 0))):
                            m = pe.matmul(ps, w[u][:, k, :], xT[x][:, k, b * TB:(b + 1) * TB],
                                          start=(k == 0 and j == 0), stop=(k == KD - 1 and j == 2))
                    m.then_inc(mm_done, 1)

            def to_natural(m0, n, u, par):
                for b in range(NBT):
                    last_tile = min(4 * b + 4, 17)
                    pe.wait_ge(col_done, NB * n + min(NB, last_tile * P // TB + 1) + PRIME)
                    pe.wait_ge(nat_done, m0 + b - 1 + PRIME)
                    for t in range(4 * b, last_tile):
                        w = P if t < PT else DEC
                        m = pe.transpose(bank[2 + (par + b) % 2][0:w, (t % 4) * P:(t % 4 + 1) * P],
                                         col[u][:, t * P:t * P + w], ident[:, :])
                    m.then_inc(nat_turned, 1)

            with pe.Fori(0, 2) as i:
                for u in range(2):
                    products(2 * i + u, u, NB * u)
            for base in (4, 8):
                with pe.Fori(0, 2) as i:
                    for u in range(2):
                        n = 2 * i + u + base
                        products(n, u, NB * u)
                        to_natural(NBT * (n - 4), n, u, NBT * u)
            for c in range(4):
                n = 12 + c
                products(n, n % 2, NB * n)
                pe.wait_ge(col_done, NB * (n + 1) + PRIME)
                pe.wait_ge(hist_done, 2 + 2 * c)
                pe.transpose(bank[6][:, 0:P], col[0][:, PAD + SEQ - P:PAD + SEQ], ident[:, :])
                pe.transpose(bank[6][0:DEC, P:2 * P], col[0][:, S0:S0 + DEC], ident[:, :]).then_inc(hist_turned, 1)
                pe.wait_ge(parts_lo, 12 + 2 * c + 1 + PRIME)
                for b in range(5):
                    w = 512 if b < 4 else DEC
                    at = PAD + 512 * b if b < 4 else S0
                    pe.wait_ge(pooled_out, 5 * c + max(b - 1, 0) + PRIME)
                    for j, (a, d) in enumerate(((0, 0), (0, 1), (1, 0))):
                        m = pe.matmul(bank[4 + b % 2][:, 0:w], pw[a][:], parts[:, d, at:at + w],
                                      start=j == 0, stop=j == 2)
                    m.then_inc(pooled_done, 1)

        @block.gpsimd
        def _(pool):
            pool.sem_inc(parts_hi, PRIME)
            pool.memset(hist_in[:], 0.0).then_inc(pre_done, 1)

            def hi_parts(n, u, base_st, c):
                pool.wait_ge(col_done, NB * (n + 1) + PRIME)
                pool.sem_inc(passed, 1)
                pool.wait_ge(stored, base_st)
                pool.sem_inc(passed, 1)
                pool.tensor_copy(parts[:, 0, 0:TOK], col[u][:, 0:TOK]).then_inc(parts_hi, 1)

            with pool.Fori(0, 2) as i:
                for u in range(2):
                    c = 2 * i + u
                    hi_parts(c, u, 32 * c, c)
            with pool.Fori(0, 2) as i:
                for u in range(2):
                    c = 2 * i + u
                    hi_parts(c + 4, u, 64 * c + st_before("k", 0), c)
            with pool.Fori(0, 2) as i:
                for u in range(2):
                    c = 2 * i + u
                    pool.wait_ge(nat_done, NBT * (c + 5) + PRIME)
                    pool.sem_inc(passed, 1)
                    pool.wait_ge(stored, 64 * c + st_before("v", 0))
                    pool.sem_inc(passed, 1)
                    pool.tensor_copy(vparts[:, 0:PT, :, 0, :],
                                     nat3[:, 0:PT, :].rearrange("p t (h d) -> p t h d", h=2))
                    pool.tensor_copy(vparts[0:DEC, PT, :, 0, :],
                                     nat3[0:DEC, PT, :].rearrange("p (h d) -> p h d", h=2)).then_inc(parts_hi, 1)
            for c in range(4):
                pool.wait_ge(d_done, c + 1 + PRIME)
                pool.sem_inc(passed, 1)
                pool.wait_ge(stored, st_before("u", c))
                pool.sem_inc(passed, 1)
                pool.tensor_copy(parts[:, 0, PAD:UW], diff(c)[:, PAD:UW]).then_inc(parts_hi, 1)
                pool.wait_ge(pooled_out, 5 * (c + 1) + PRIME)
                pool.sem_inc(passed, 1)
                pool.tensor_copy(parts[:, 0, 0:TOK], col[1][:, 0:TOK]).then_inc(parts_hi, 1)

        @block.vector
        def _(dve):
            for x in (w_lo, parts_lo, nat_done, d_done):
                dve.sem_inc(x, PRIME)
            chain = [0]

            def link(m):
                chain[0] += 1
                m.then_inc(dve_chain, 1)
                dve.wait_ge(dve_chain, chain[0])

            def split_w(n, u):
                dve.wait_ge(w_hi, n + 1 + PRIME)
                dve.tensor_tensor(wlo[u][:], wraw[u][:], r32(whi[u][:]), ALU.subtract).then_inc(w_lo, 1)

            def lo_parts(n, u):
                dve.wait_ge(parts_hi, n + 1 + PRIME)
                dve.tensor_tensor(parts[:, 1, 0:TOK], col[u][:, 0:TOK], r32(parts[:, 0, 0:TOK]),
                                  ALU.subtract).then_inc(parts_lo, 1)

            def natural(m0, par, base_st):
                dve.wait_ge(stored, base_st)
                for b in range(NBT):
                    dve.wait_ge(nat_turned, m0 + b + 1 + PRIME)
                    if b < 4:
                        m = dve.tensor_copy(nat[:, 512 * b:512 * b + 512], bank[2 + (par + b) % 2][:])
                    else:
                        m = dve.tensor_copy(nat[0:DEC, PT * P:17 * P], bank[2 + (par + b) % 2][0:DEC, 0:P])
                    m.then_inc(nat_done, 1)

            for t in range(PAD):
                dve.memset(rcount[:, t:t + 1], 1.0 / (t + 1))
            dve.wait_ge(pre_loaded, 48)
            dve.wait_ge(hist_turned, 1)
            dve.tensor_copy(hist[:], bank[6][:, 0:4 * DEC].rearrange("p (g n) -> p g n", g=4)[:, :, 0:PAD])\
               .then_inc(hist_done, 2)
            split_w(0, 0)
            with dve.Fori(0, 2) as i:
                for u in range(2):
                    n = 2 * i + u
                    split_w(n + 1, 1 - u)
                    lo_parts(n, u)
            with dve.Fori(0, 2) as i:
                for u in range(2):
                    c = 2 * i + u
                    split_w(c + 5, 1 - u)
                    natural(NBT * c, NBT * u, 64 * c + st_before("k", 0))
                    lo_parts(c + 4, u)
            with dve.Fori(0, 2) as i:
                for u in range(2):
                    c = 2 * i + u
                    split_w(c + 9, 1 - u)
                    natural(NBT * (c + 4), NBT * u, 64 * c + st_before("v", 0))
                    dve.wait_ge(parts_hi, c + 9 + PRIME)
                    for rows, t in ((P, slice(0, PT)), (DEC, slice(PT, PT + 1))):
                        m = dve.tensor_tensor(vparts[0:rows, t, :, 1, :],
                                              nat3[0:rows, t, :].rearrange("p t (h d) -> p t h d", h=2),
                                              r32(vparts[0:rows, t, :, 0, :]), ALU.subtract)
                    m.then_inc(parts_lo, 1)
            for c in range(4):
                n = 12 + c
                if c < 3:
                    split_w(n + 1, (n + 1) % 2)
                dve.wait_ge(parts_lo, 12 + 2 * c + PRIME)
                link(dve.tensor_copy(pw[0][:], pw_raw[:, c, :]))
                dve.tensor_tensor(pw[1][:], pw_raw[:, c, :], r32(pw[0][:]), ALU.subtract)
                if c == 0:
                    dve.wait_ge(stored, st_before("u", 0))
                dve.memset(col[0][:, 0:PAD], 0.0)
                link(dve.tensor_copy(col[0][:, S0 - PAD:S0], hist[:, c, :]))
                dve.wait_ge(col_done, NB * (n + 1) + PRIME)
                src = col[0]
                for lv in range(c + 1):
                    back, dst = 1 << lv, ladder(lv)
                    link(dve.tensor_tensor(dst[:, 2 * back - 1:UW], src[:, 2 * back - 1:UW],
                                           src[:, back - 1:UW - back], ALU.add))
                    src = dst
                w = WINDOWS[c]
                out = diff(c)
                link(dve.scalar_tensor_tensor(out[:, PAD:UW], src[:, PAD:UW], 1.0 / w, col[0][:, PAD:UW],
                                              ALU.mult, ALU.subtract))
                link(dve.tensor_tensor(out[:, PAD:PAD + w - 1], src[:, PAD:PAD + w - 1], rcount[:, 0:w - 1], ALU.mult))
                dve.tensor_tensor(out[:, PAD:PAD + w - 1], out[:, PAD:PAD + w - 1], col[0][:, PAD:PAD + w - 1],
                                  ALU.subtract).then_inc(d_done, 1)
                dve.wait_ge(parts_hi, 12 + 2 * c + 1 + PRIME)
                dve.tensor_tensor(parts[:, 1, PAD:UW], out[:, PAD:UW], r32(parts[:, 0, PAD:UW]),
                                  ALU.subtract).then_inc(parts_lo, 1)
                dve.wait_ge(hist_turned, c + 2)
                if c >= 2:
                    dve.wait_ge(stored, st_before("u", c - 1))
                dve.tensor_copy(tails[c % 2][:, 0, :], bank[6][:, 0:P]).then_inc(hist_done, 1)
                dve.tensor_copy(tails[c % 2][0:DEC, 1, :], bank[6][0:DEC, P:2 * P]).then_inc(hist_done, 1)
                dve.wait_ge(parts_hi, 12 + 2 * c + 2 + PRIME)
                dve.tensor_tensor(parts[:, 1, 0:TOK], col[1][:, 0:TOK], r32(parts[:, 0, 0:TOK]),
                                  ALU.subtract).then_inc(parts_lo, 1)


def split_cache(nc, ctx, sem, sb, passed, bank, ident, ck, cv, kcT_d, vc_d):
    kin = [sb(ctx, f"kin{u}", [P, SBW]) for u in range(2)]
    vin = [sb(ctx, f"vin{u}", [P, SBW]) for u in range(2)]
    kparts = [sb(ctx, f"kparts{u}", [P, 2, HC, P], F32R) for u in range(2)]
    vparts = [sb(ctx, f"vcparts{u}", [P, HEADS, 2, HD], F32R) for u in range(2)]
    k_loaded = [sem(f"kc_loaded{u}") for u in range(2)]
    v_loaded = [sem(f"vc_loaded{u}") for u in range(2)]
    stored = [sem(f"c_stored{u}") for u in range(2)]
    turned, k_hi, k_lo, v_hi, v_lo = (sem(n) for n in ("kc_turned", "kc_hi", "kc_lo", "vc_hi", "vc_lo"))
    N_ST = 16 * (2 * HC + 1)

    with nc.Block() as block:
        @block.sync
        def _(sp):
            with sp.Fori(0, CT // 2) as i:
                for u in range(2):
                    sp.wait_ge(turned, 2 * i + u - 1 + PRIME)
                    sp.sem_inc(passed, 1)
                    sp.dma_start(kin[u][:], ck[bass.ds((2 * i + u) * P, P), :]).then_inc(k_loaded[u], 16)
                    sp.wait_ge(v_lo, 2 * i + u - 1 + PRIME)
                    sp.sem_inc(passed, 1)
                    sp.dma_start(vin[u][:], cv[bass.ds((2 * i + u) * P, P), :]).then_inc(v_loaded[u], 16)

        @block.tensor
        def _(pe):
            pe.sem_inc(turned, PRIME)
            with pe.Fori(0, CT // 2) as i:
                for u in range(2):
                    pe.wait_ge(k_loaded[u], 16 * i + 16)
                    pe.wait_ge(k_lo, 2 * i + u - 1 + PRIME)
                    for c in range(HC):
                        m = pe.transpose(bank[u][:, c * P:(c + 1) * P], kin[u][:, c * P:(c + 1) * P], ident[:, :])
                    m.then_inc(turned, 1)

        @block.scalar
        def _(act):
            act.sem_inc(k_hi, PRIME)
            with act.Fori(0, CT // 2) as i:
                for u in range(2):
                    act.wait_ge(turned, 2 * i + u + 1 + PRIME)
                    act.wait_ge(stored[u], N_ST * i)
                    act.activation(kparts[u][:, 0, :, :].rearrange("p c n -> p (c n)"), bank[u][:], ACT.Copy)\
                       .then_inc(k_hi, 1)

        @block.vector
        def _(dve):
            dve.sem_inc(k_lo, PRIME)
            dve.sem_inc(v_lo, PRIME)
            with dve.Fori(0, CT // 2) as i:
                for u in range(2):
                    dve.wait_ge(k_hi, 2 * i + u + 1 + PRIME)
                    dve.tensor_tensor(kparts[u][:, 1, :, :].rearrange("p c n -> p (c n)"), bank[u][:],
                                      r32(kparts[u][:, 0, :, :].rearrange("p c n -> p (c n)")), ALU.subtract)\
                       .then_inc(k_lo, 1)
                    dve.wait_ge(v_hi, 2 * i + u + 1 + PRIME)
                    dve.tensor_tensor(vparts[u][:, :, 1, :], vin[u][:].rearrange("p (h d) -> p h d", h=HEADS),
                                      r32(vparts[u][:, :, 0, :]), ALU.subtract).then_inc(v_lo, 1)

        @block.gpsimd
        def _(pool):
            pool.sem_inc(v_hi, PRIME)
            with pool.Fori(0, CT // 2) as i:
                for u in range(2):
                    pool.wait_ge(v_loaded[u], 16 * i + 16)
                    pool.sem_inc(passed, 1)
                    pool.wait_ge(stored[u], N_ST * i)
                    pool.sem_inc(passed, 1)
                    pool.tensor_copy(vparts[u][:, :, 0, :], vin[u][:].rearrange("p (h d) -> p h d", h=HEADS))\
                        .then_inc(v_hi, 1)
                    pool.wait_ge(k_lo, 2 * i + u + 1 + PRIME)
                    pool.sem_inc(passed, 1)
                    for j in range(2):
                        for c in range(HC):
                            pool.dma_start(r32(kcT_d[j, c * P:(c + 1) * P, bass.ds((2 * i + u) * P, P)]),
                                           r32(kparts[u][:, j, c, :])).then_inc(stored[u], 16)
                    pool.wait_ge(v_lo, 2 * i + u + 1 + PRIME)
                    pool.sem_inc(passed, 1)
                    pool.dma_start(r32(vc_d[bass.ds((2 * i + u) * P, P)].rearrange("t h j d -> t (h j d)")),
                                   r32(vparts[u][:].rearrange("p h j d -> p (h j d)"))).then_inc(stored[u], 16)
            for u in range(2):
                pool.wait_ge(stored[u], N_ST * (CT // 2))
                pool.sem_inc(passed, 1)


def attend(nc, ctx, sem, sb, passed, bank, ident, ident_r, mask_r, maskd_r, cv, qT_d, kT_d, kcT_d, vp_out, vs_out,
           mixT_d):
    N = len(ITEMS)
    G = 2 * PT // 4 + 1
    OB = 3
    assert N % 4 == 0 and G % OB == 0
    KW = PAST + P
    k_st = [[sb(ctx, f"k_st{u}{j}", [P, SEQ], F32R) for j in range(2)] for u in range(2)]
    q_st = [sb(ctx, f"q_st{u}", [P, SEQ], F32R) for u in range(2)]
    v_st = [sb(ctx, f"v_st{u}", [P, PT, HD]) for u in range(2)]
    ks = [sb(ctx, f"ks{j}", [P, 2, KW], F32R) for j in range(2)]
    qs = sb(ctx, "qs", [P, 2, P], F32R)
    vs = sb(ctx, "vs", [P, 2, KW // P, HD])
    e_t = [sb(ctx, f"e_t{b}", [P, 512]) for b in range(4)]
    l_t, sp_t, c_t, t_t, a_t, aT = ([sb(ctx, f"{n}_t{b}", [P, 512]) for b in range(2)]
                                    for n in ("l", "sp", "c", "t", "a", "aT"))
    o_t = [sb(ctx, f"o_t{b}", [HD, 512]) for b in range(OB)]
    oparts = [sb(ctx, f"oparts{b}", [HD, 2, 512], F32R) for b in range(OB)]

    loaded = [sem(f"a_loaded{u}") for u in range(2)]
    sample_loaded, zeroed = sem("a_sample_loaded"), sem("a_zeroed")
    z_done, abs_done, e_done, l_done, sp_done, c_done, t_done, a_done, turn_done, av_done = (
        sem(f"a_{n}") for n in ("z", "abs", "e", "l", "sp", "c", "t", "a", "turn", "av"))
    aT_done = [sem("a_aT_even"), sem("a_aT_odd")]
    o_done, opart_done = sem("a_o"), sem("a_opart")
    stored = [sem(f"a_stored{b}") for b in range(OB)]
    Z_BANK, T_BANK, O_BANK = 0, 4, 6
    NZ = 4

    AT_ABS, AT_EXP, AT_LN, AT_SUMS, AT_A, AT_OUT, AT_V, AT_O = 1, 2, 3, 4, 5, 6, 7, 8
    STEPS = N + AT_O

    def z_bank(n):
        return bank[Z_BANK + n % NZ][:, 0:ITEMS[n].width]

    def before(n, b):
        return N // 2 * b + n // 2

    def group_end(n):
        return n >= 0 and n < N and ITEMS[n].ends_group

    with nc.Block() as block:
        @block.sync
        def _(sp):
            with sp.Fori(0, HEADS // 2) as i:
                for u in range(2):
                    sp.wait_ge(av_done, N * (i - 1) + NI * (u + 1) + PRIME)
                    sp.sem_inc(passed, 1)
                    row = (2 * i + u) * HD
                    for half in range(2):
                        s = slice(half * HD, half * HD + HD)
                        for j in range(2):
                            sp.dma_start(r32(k_st[u][j][s, :]), r32(kT_d[j, bass.ds(row, HD), 0:SEQ]))\
                              .then_inc(loaded[u], 16)
                        sp.dma_start(r32(q_st[u][s, :]), r32(qT_d[half, bass.ds(row, HD), 0:SEQ]))\
                          .then_inc(loaded[u], 16)
                    sp.dma_start(v_st[u][:], vp_out.rearrange("(t p) c -> p t c", p=P)[:, :, bass.ds(row, HD)])\
                      .then_inc(loaded[u], 16)
                sp.wait_ge(zeroed, 4)
                sp.wait_ge(av_done, N * i + PRIME)
                sp.sem_inc(passed, 1)
                for h in range(2):
                    row = (2 * i + h) * HD
                    for half in range(2):
                        s = slice(half * HD, half * HD + HD)
                        for j in range(2):
                            sp.dma_start(r32(ks[j][s, h, 0:PAST]), r32(kcT_d[j, bass.ds(row, HD), :]))\
                              .then_inc(sample_loaded, 16)
                            sp.dma_start(r32(ks[j][s, h, PAST:PAST + DEC]), r32(kT_d[j, bass.ds(row, HD), SEQ:TOK]))\
                              .then_inc(sample_loaded, 16)
                        sp.dma_start(r32(qs[s, h, h * DEC:(h + 1) * DEC]), r32(qT_d[half, bass.ds(row, HD), SEQ:TOK]))\
                          .then_inc(sample_loaded, 16)
                    sp.dma_start(vs[:, h, 0:CT, :], cv.rearrange("(t p) c -> p t c", p=P)[:, :, bass.ds(row, HD)])\
                      .then_inc(sample_loaded, 16)
                    sp.dma_start(vs[0:DEC, h, CT, :], vs_out[:, bass.ds(row, HD)]).then_inc(sample_loaded, 16)

        @block.tensor
        def _(pe):
            for x in (z_done, turn_done, av_done):
                pe.sem_inc(x, PRIME)
            with pe.Fori(0, HEADS // 2) as i:
                def scores(n):
                    it, z = ITEMS[n], z_bank(n)
                    if n % NI == 0 and it.head < 2:
                        pe.wait_ge(loaded[it.head], 16 * 7 * (i + 1))
                    if it.head == 2 and it.first:
                        pe.wait_ge(sample_loaded, 16 * 24 * (i + 1))
                    pe.wait_ge(t_done, N * i + n - NZ + 1 + PRIME)
                    keys = slice(it.key0, it.key0 + it.width)
                    if it.head < 2:
                        left = q_st[it.head][:, it.tile * P:(it.tile + 1) * P]
                        terms = [(left, k_st[it.head][j][:, keys]) for j in range(2)]
                    else:
                        terms = [(qs[:, h, :], ks[j][:, h, keys]) for h in range(2) for j in range(2)]
                    for k, (left, right) in enumerate(terms):
                        if it.first and k == len(terms) - 1:
                            pe.matmul(z[:, it.width - P:it.width], ident_r[:], (mask_r if it.head < 2 else maskd_r)[:],
                                      start=False, stop=False, skip_group_check=True)
                        m = pe.matmul(z, left, right, start=k == 0, stop=k == len(terms) - 1)
                    m.then_inc(z_done, 1)

                def turn(n):
                    pe.wait_ge(a_done, N * i + n + 1 + PRIME)
                    pe.wait_ge(aT_done[n % 2], before(n, i) + PRIME)
                    for b in range(ITEMS[n].width // P):
                        m = pe.transpose(bank[T_BANK + n % 2][:, b * P:(b + 1) * P],
                                         a_t[n % 2][:, b * P:(b + 1) * P], ident[:, :])
                    m.then_inc(turn_done, 1)

                def values(n):
                    it = ITEMS[n]
                    pe.wait_ge(aT_done[n % 2], before(n, i) + 1 + PRIME)
                    g = it.group
                    if it.starts_group:
                        pe.wait_ge(o_done, G * i + (g if g in (0, G - 1) else g - 1) + PRIME)
                    for b in range(it.width // P):
                        start, stop = it.first and b == 0, it.last and b == it.width // P - 1
                        t = it.key0 // P + b
                        if it.head < 2:
                            m = pe.matmul(bank[O_BANK + g % 2][0:HD, (it.tile % 4) * P:(it.tile % 4 + 1) * P],
                                          v_st[it.head][:, t, :], aT[n % 2][:, b * P:(b + 1) * P],
                                          start=start, stop=stop)
                        else:
                            for h in range(2):
                                m = pe.matmul(bank[O_BANK + h][0:HD, 0:DEC], vs[:, h, t, :],
                                              aT[n % 2][:, b * P + h * DEC:b * P + (h + 1) * DEC],
                                              start=start, stop=stop)
                    m.then_inc(av_done, 1)

                for s in range(STEPS):
                    if 0 <= s - AT_V < N:
                        values(s - AT_V)
                    if 0 <= s - AT_A < N:
                        turn(s - AT_A)
                    if s < N:
                        scores(s)

        @block.scalar
        def _(act):
            for x in (abs_done, e_done, l_done, a_done, o_done, aT_done[0]):
                act.sem_inc(x, PRIME)
            with act.Fori(0, HEADS // 2) as i:
                for s in range(STEPS + 1):
                    n = s - AT_LN
                    if 0 <= n < N:
                        w = ITEMS[n].width
                        act.wait_ge(e_done, N * i + n + 1 + PRIME)
                        act.wait_ge(sp_done, N * i + n - 1 + PRIME)
                        act.activation(l_t[n % 2][:, 0:w], e_t[n % 4][:, 0:w], ACT.Ln, bias=1.0).then_inc(l_done, 1)
                    n = s - AT_A
                    if 0 <= n < N:
                        w = ITEMS[n].width
                        act.wait_ge(t_done, N * i + n + 1 + PRIME)
                        act.wait_ge(turn_done, N * i + n - 1 + PRIME)
                        act.activation(a_t[n % 2][:, 0:w], t_t[n % 2][:, 0:w], ACT.Exp).then_inc(a_done, 1)
                    n = s - AT_EXP
                    if 0 <= n < N:
                        w = ITEMS[n].width
                        act.wait_ge(abs_done, N * i + n + 1 + PRIME)
                        act.activation(e_t[n % 4][:, 0:w], e_t[n % 4][:, 0:w], ACT.Exp, scale=-1.0)\
                           .then_inc(e_done, 1)
                    n = s - AT_OUT
                    if 0 <= n < N and n % 2 == 0:
                        w = ITEMS[n].width
                        act.wait_ge(turn_done, N * i + n + 1 + PRIME)
                        act.wait_ge(av_done, N * i + n - 1 + PRIME)
                        act.activation(aT[0][:, 0:w], bank[T_BANK][:, 0:w], ACT.Copy).then_inc(aT_done[0], 1)
                    n = s - AT_ABS
                    if 0 <= n < N:
                        w = ITEMS[n].width
                        act.wait_ge(z_done, N * i + n + 1 + PRIME)
                        act.wait_ge(l_done, N * i + n - 3 + PRIME)
                        act.activation(e_t[n % 4][:, 0:w], z_bank(n), ACT.Abs).then_inc(abs_done, 1)
                    n = s - AT_O
                    if group_end(n):
                        g = ITEMS[n].group
                        act.wait_ge(av_done, N * i + n + 1 + PRIME)
                        act.wait_ge(opart_done, 2 * (G * i + g - OB + 1) + PRIME)
                        if g < G - 1:
                            m = act.activation(o_t[g % OB][:], bank[O_BANK + g % 2][0:HD, :], ACT.Copy)
                        else:
                            for h in range(2):
                                m = act.activation(o_t[g % OB][:, h * DEC:(h + 1) * DEC],
                                                   bank[O_BANK + h][0:HD, 0:DEC], ACT.Copy)
                        m.then_inc(o_done, 1)

        @block.gpsimd
        def _(pool):
            pool.sem_inc(opart_done, PRIME)
            with pool.Fori(0, HEADS // 2) as i:
                for g in range(G):
                    w = 512 if g < G - 1 else 2 * DEC
                    out, parts = o_t[g % OB], oparts[g % OB]
                    pool.wait_ge(o_done, G * i + g + 1 + PRIME)
                    pool.sem_inc(passed, 1)
                    pool.wait_ge(stored[g % OB], 32 * (G // OB * i + g // OB))
                    pool.sem_inc(passed, 1)
                    pool.tensor_copy(parts[:, 0, 0:w], out[:, 0:w]).then_inc(opart_done, 1)
                    pool.wait_ge(opart_done, 2 * (G * i + g) + 1 + PRIME)
                    pool.sem_inc(passed, 1)
                    pool.tensor_tensor(parts[:, 1, 0:w], out[:, 0:w], r32(parts[:, 0, 0:w]), ALU.subtract)\
                        .then_inc(opart_done, 1)
                    pool.wait_ge(opart_done, 2 * (G * i + g) + 2 + PRIME)
                    pool.sem_inc(passed, 1)
                    for j in range(2):
                        if g < G - 1:
                            pool.dma_start(r32(mixT_d[j, bass.ds((2 * i + g // 4) * HD, HD),
                                                      (g % 4) * 512:(g % 4 + 1) * 512]),
                                           r32(parts[:, j, :])).then_inc(stored[g % OB], 16)
                        else:
                            pool.dma_start(r32(mixT_d[j, bass.ds(2 * i * HD, 2 * HD), SEQ:TOK]
                                               .rearrange("(h d) t -> d h t", h=2)),
                                           r32(parts[:, j, 0:w].rearrange("d (h t) -> d h t", h=2)))\
                                .then_inc(stored[g % OB], 16)
            for b in range(OB):
                pool.wait_ge(stored[b], 32 * G // OB * HEADS // 2)

        @block.vector
        def _(dve):
            for x in (sp_done, c_done, t_done, aT_done[1]):
                dve.sem_inc(x, PRIME)
            dve.memset(r32(qs[:]), 0.0).then_inc(zeroed, 1)
            dve.memset(vs[:, :, CT, :], 0.0).then_inc(zeroed, 1)
            for j in range(2):
                dve.memset(r32(ks[j][:, :, PAST:KW]), 0.0).then_inc(zeroed, 1)
            with dve.Fori(0, HEADS // 2) as i:
                for s in range(STEPS):
                    n = s - AT_SUMS
                    if 0 <= n < N:
                        w, z = ITEMS[n].width, z_bank(n)
                        dve.wait_ge(l_done, N * i + n + 1 + PRIME)
                        dve.wait_ge(c_done, N * i + n - 1 + PRIME)
                        dve.scalar_tensor_tensor(sp_t[n % 2][:, 0:w], z, 0.0, l_t[n % 2][:, 0:w], ALU.max, ALU.add)\
                           .then_inc(sp_done, 1)
                        dve.wait_ge(sp_done, N * i + n + 1 + PRIME)
                        dve.wait_ge(t_done, N * i + n - 1 + PRIME)
                        back = sp_t[n % 2][:, 0:w][:, ::-1]
                        dve.tensor_tensor_scan(c_t[n % 2][:, 0:w][:, ::-1], back, back,
                                               0.0 if ITEMS[n].first else c_t[(n - 1) % 2][:, 0:1],
                                               ALU.add, ALU.max).then_inc(c_done, 1)
                        dve.wait_ge(c_done, N * i + n + 1 + PRIME)
                        dve.wait_ge(a_done, N * i + n - 1 + PRIME)
                        dve.tensor_tensor(t_t[n % 2][:, 0:w], z, c_t[n % 2][:, 0:w], ALU.subtract)\
                           .then_inc(t_done, 1)
                    n = s - AT_OUT
                    if 0 <= n < N and n % 2 == 1:
                        w = ITEMS[n].width
                        dve.wait_ge(turn_done, N * i + n + 1 + PRIME)
                        dve.wait_ge(av_done, N * i + n - 1 + PRIME)
                        dve.tensor_copy(aT[1][:, 0:w], bank[T_BANK + 1][:, 0:w]).then_inc(aT_done[1], 1)


def mix_norm(nc, ctx, sem, sb, passed, bank, ident, eps_t, blk, xp, xs, mixT_d, w_out, ln_g, ln_b, x1T, acc):
    wo = [sb(ctx, f"wo{j}_{blk}", [P, KD, D], F32R) for j in range(2)]
    xin = [sb(ctx, f"mx{u}_{blk}", [P, D]) for u in range(2)]
    mixT = [sb(ctx, f"mixT{u}_{blk}", [P, 2, KD, P], F32R) for u in range(2)]
    x1n = xin
    gain, bias = sb(ctx, f"g1_{blk}", [P, D]), sb(ctx, f"b1_{blk}", [P, D])
    stats = sb(ctx, f"st1_{blk}", [P, 2, 6])
    mv = sb(ctx, f"mv1_{blk}", [P, 2])
    lnv, rstd = sb(ctx, f"lnv1_{blk}", [P, 1]), sb(ctx, f"rs1_{blk}", [P, 1])

    def c(n):
        return sem(f"m{blk}_{n}")

    wo_loaded = [sem(f"m{blk}_wo_loaded{u}") for u in range(2)]
    x_loaded = [sem(f"m{blk}_x_loaded{u}") for u in range(2)]
    mixT_loaded = [sem(f"m{blk}_mixT_loaded{u}") for u in range(2)]
    par_loaded = sem(f"m{blk}_par_loaded")
    wo_hi, wo_lo, sums, added, bn, var, lnd, rs, normed, scaled, shifted, turned, hi, lo, kept = (
        c(n) for n in ("wo_hi", "wo_lo", "sums", "added", "bn", "var", "ln", "rs", "normed", "scaled", "shifted",
                       "turned", "hi", "lo", "kept"))
    t0 = 8 * blk

    with nc.Block() as block:
        def tiles(eng, f):
            with eng.Fori(0, 4) as i:
                for u in range(2):
                    f(2 * i + u, u, i + 1, P)
            if blk == 1:
                f(8, 0, 5, DEC)

        @block.sync
        def _(sp):
            sp.dma_start(gain[:], ln_g.rearrange("(a n) -> a n", a=1).broadcast_to([P, D])).then_inc(par_loaded, 16)
            sp.dma_start(bias[:], ln_b.rearrange("(a n) -> a n", a=1).broadcast_to([P, D])).then_inc(par_loaded, 16)
            with sp.Fori(0, KD // 2) as i:
                for u in range(2):
                    sp.wait_ge(wo_lo, 2 * i + u - 1 + PRIME)
                    sp.sem_inc(passed, 1)
                    sp.dma_start(xin[u][:], w_out[bass.ds((2 * i + u) * P, P), :]).then_inc(wo_loaded[u], 16)
            sp.wait_ge(wo_lo, KD + PRIME)

            def load(t, u, times, rows):
                sp.wait_ge(kept, t - 1 + PRIME)
                sp.sem_inc(passed, 1)
                sp.wait_ge(turned, t - 1 + PRIME)
                sp.sem_inc(passed, 1)
                if rows == P:
                    sp.dma_start(xin[u][:], xp[bass.ds((t + t0) * P, P), :]).then_inc(x_loaded[u], 16)
                else:
                    sp.dma_start(xin[u][0:DEC, :], xs).then_inc(x_loaded[u], 16)
                sp.wait_ge(sums, 2 * (t - 1) + PRIME)
                sp.sem_inc(passed, 1)
                for j in range(2):
                    sp.dma_start(r32(mixT[u][:, j, :, 0:rows]),
                                 r32(mixT_d[j].rearrange("(k p) t -> p k t", p=P)[:, :, bass.ds((t + t0) * P, rows)]))\
                      .then_inc(mixT_loaded[u], 16)

            tiles(sp, load)

        @block.tensor
        def _(pe):
            pe.sem_inc(sums, PRIME)
            pe.sem_inc(turned, PRIME)
            pe.wait_ge(wo_lo, KD + PRIME)

            def project(t, u, times, rows):
                pe.wait_ge(mixT_loaded[u], 32 * times)
                for half in range(2):
                    pe.wait_ge(added, 2 * (t - 1) + half + PRIME)
                    for k in range(KD):
                        for n, (a, w) in enumerate(((0, 0), (0, 1), (1, 0))):
                            m = pe.matmul(bank[2 * u + half][:], mixT[u][:, a, k, :], wo[w][:, k, half * 512:half * 512 + 512],
                                          start=k == 0 and n == 0, stop=k == KD - 1 and n == 2)
                    m.then_inc(sums, 1)

            def turn(t, u, times, rows):
                pe.wait_ge(shifted, t + 1 + PRIME)
                pe.wait_ge(lo, t - 1 + PRIME)
                for k in range(KD):
                    m = pe.transpose(bank[4 + 2 * u + k // 4][:, (k % 4) * P:(k % 4) * P + rows],
                                     x1n[u][0:rows, k * P:(k + 1) * P], ident[0:rows, 0:rows])
                m.then_inc(turned, 1)

            project(0, 0, 1, P)
            with pe.Fori(0, 3) as i:
                for u in range(2):
                    project(2 * i + u + 1, 1 - u, i + 1 + u, P)
                    turn(2 * i + u, u, i + 1, P)
            project(7, 1, 4, P)
            turn(6, 0, 4, P)
            if blk == 1:
                project(8, 0, 5, DEC)
            turn(7, 1, 4, P)
            if blk == 1:
                turn(8, 0, 5, DEC)

        @block.scalar
        def _(act):
            for x in (wo_hi, lnd, rs, hi, kept):
                act.sem_inc(x, PRIME)
            with act.Fori(0, KD // 2) as i:
                for u in range(2):
                    act.wait_ge(wo_loaded[u], 16 * i + 16)
                    act.activation(wo[0][:, bass.ds(2 * i + u, 1), :].rearrange("p a n -> p (a n)"), xin[u][:], ACT.Copy)\
                       .then_inc(wo_hi, 1)

            def norm(t, u, times, rows):
                act.wait_ge(var, t + 1 + PRIME)
                act.activation(lnv[:], mv[:, 1:2], ACT.Ln, bias=eps_t[:]).then_inc(lnd, 1)
                act.wait_ge(lnd, t + 1 + PRIME)
                act.activation(rstd[:], lnv[:], ACT.Exp, scale=-0.5).then_inc(rs, 1)
                act.wait_ge(shifted, t + 1 + PRIME)
                act.activation(acc[:, bass.ds(t, 1), :].rearrange("p a n -> p (a n)"), x1n[u][:], ACT.Copy, scale=ALPHA)\
                   .then_inc(kept, 1)
                act.wait_ge(turned, t + 1 + PRIME)
                for b in range(2):
                    m = act.activation(x1T[0][:, 4 * b:4 * b + 4, bass.ds(t * P, rows)],
                                       bank[4 + 2 * u + b][:, :].rearrange("p (k n) -> p k n", k=4)[:, :, 0:rows],
                                       ACT.Copy)
                m.then_inc(hi, 1)

            tiles(act, norm)

        @block.vector
        def _(dve):
            for x in (wo_lo, added, bn, var, normed, lo):
                dve.sem_inc(x, PRIME)
            with dve.Fori(0, KD // 2) as i:
                for u in range(2):
                    dve.wait_ge(wo_hi, 2 * i + u + 1 + PRIME)
                    s = (slice(None), bass.ds(2 * i + u, 1), slice(None))
                    dve.tensor_tensor(wo[1][s].rearrange("p a n -> p (a n)"), xin[u][:],
                                      r32(wo[0][s]).rearrange("p a n -> p (a n)"), ALU.subtract).then_inc(wo_lo, 1)

            def norm(t, u, times, rows):
                dve.wait_ge(x_loaded[u], 16 * times)
                for half in range(2):
                    dve.wait_ge(sums, 2 * t + half + 1 + PRIME)
                    s = slice(half * 512, half * 512 + 512)
                    dve.scalar_tensor_tensor(x1n[u][:, s], xin[u][:, s], ALPHA, bank[2 * u + half][:],
                                             ALU.mult, ALU.add).then_inc(added, 1)
                for half in range(2):
                    dve.wait_ge(added, 2 * t + half + 1 + PRIME)
                    dve.bn_stats(stats[:, half, :], x1n[u][:, half * 512:half * 512 + 512]).then_inc(bn, 1)
                dve.wait_ge(bn, 2 * t + 2 + PRIME)
                dve.wait_ge(rs, t + PRIME)
                dve.sem_inc(passed, 1)
                dve.bn_aggr(mv[:], stats[:].rearrange("p a b -> p (a b)")).then_inc(var, 1)
                dve.wait_ge(rs, t + 1 + PRIME)
                dve.tensor_scalar(x1n[u][:], x1n[u][:], mv[:, 0:1], rstd[:, 0:1], ALU.subtract, ALU.mult)\
                   .then_inc(normed, 1)

            def low(t, u, times, rows):
                dve.wait_ge(hi, t + 1 + PRIME)
                for b in range(2):
                    s = (slice(None), slice(4 * b, 4 * b + 4), bass.ds(t * P, rows))
                    m = dve.tensor_tensor(x1T[1][s], bank[4 + 2 * u + b][:, :].rearrange("p (k n) -> p k n", k=4)[:, :, 0:rows],
                                          r32(x1T[0][s]), ALU.subtract)
                m.then_inc(lo, 1)

            def both(t, u, times, rows):
                norm(t, u, times, rows)
                low(t, u, times, rows)

            tiles(dve, both)

        @block.gpsimd
        def _(pool):
            pool.sem_inc(scaled, PRIME)
            pool.sem_inc(shifted, PRIME)
            pool.wait_ge(par_loaded, 32)

            def affine(t, u, times, rows):
                pool.wait_ge(normed, t + 1 + PRIME)
                pool.sem_inc(passed, 1)
                pool.tensor_tensor(x1n[u][:], x1n[u][:], gain[:], ALU.mult).then_inc(scaled, 1)
                pool.wait_ge(scaled, t + 1 + PRIME)
                pool.sem_inc(passed, 1)
                pool.tensor_tensor(x1n[u][:], x1n[u][:], bias[:], ALU.add).then_inc(shifted, 1)

            tiles(pool, affine)


def ffn(nc, ctx, sem, sb, passed, bank, blk, width, tiles, w_gate, w_up, w_down, x1T, acc):
    NT = 3 if blk else 2
    TW = width // NT
    graw = [sb(ctx, f"graw{j}_{blk}", [P, KD, P]) for j in range(2)]
    gw = [[[sb(ctx, f"gw{u}{g}{j}_{blk}", [P, KD, P], F32R) for j in range(2)] for g in range(2)] for u in range(2)]
    draw = sb(ctx, f"draw_{blk}", [P, D])
    dw = [[sb(ctx, f"dw{u}{j}_{blk}", [P, D], F32R) for j in range(2)] for u in range(2)]
    hT = [[sb(ctx, f"hT{u}{j}_{blk}", [P, tiles * P], F32R) for j in range(2)] for u in range(2)]
    e_t = [sb(ctx, f"fe{b}_{blk}", [P, TW]) for b in range(2)]
    h_t = [sb(ctx, f"fh{b}_{blk}", [P, TW]) for b in range(2)]

    def c(n):
        return sem(f"f{blk}_{n}")

    g_loaded, d_loaded = sem(f"f{blk}_g_loaded"), sem(f"f{blk}_d_loaded")
    pad = sem(f"f{blk}_pad")
    g_hi, g_lo, d_hi, d_lo = c("g_hi"), c("g_lo"), c("d_hi"), c("d_lo")
    gate_up, absd, exped, logd, logsig, sig, silu, prod, h_hi, h_lo = (
        c(n) for n in ("gate_up", "abs", "exp", "log", "logsig", "sig", "silu", "prod", "h_hi", "h_lo"))
    down, summed = c("down"), c("summed")
    ND = 2 * tiles

    SHARE = tiles // NT

    with nc.Block() as block:
        @block.sync
        def _(sp):
            with sp.Fori(0, FC) as f:
                sp.wait_ge(g_lo, f + PRIME)
                sp.sem_inc(passed, 1)
                for j, w in enumerate((w_gate, w_up)):
                    sp.dma_start(graw[j][:], w.rearrange("(k p) f -> p k f", p=P)[:, :, bass.ds(f * P, P)])\
                      .then_inc(g_loaded, 16)
                sp.wait_ge(d_lo, f + PRIME)
                sp.sem_inc(passed, 1)
                sp.dma_start(draw[:], w_down[bass.ds(f * P, P), :]).then_inc(d_loaded, 16)

        @block.tensor
        def _(pe):
            pe.sem_inc(gate_up, PRIME)
            pe.sem_inc(down, PRIME)
            if blk:
                pe.wait_ge(pad, 4)

            def gates(f, u, n):
                if n == 0:
                    pe.wait_ge(g_lo, f + 1 + PRIME)
                pe.wait_ge(prod, NT * f + n - 1 + PRIME)
                b = (NT * u + n) % 2
                for g in range(2):
                    for k in range(KD):
                        for s, (w, x) in enumerate(((0, 0), (0, 1), (1, 0))):
                            m = pe.matmul(bank[2 * b + g][:, 0:TW], gw[u][g][w][:, k, :],
                                          x1T[x][:, k, n * TW:(n + 1) * TW],
                                          start=k == 0 and s == 0, stop=k == KD - 1 and s == 2)
                m.then_inc(gate_up, 1)

            def downs(f, u, part):
                if part == 0:
                    pe.wait_ge(d_lo, f + 1 + PRIME)
                    pe.wait_ge(h_lo, NT * (f + 1) + PRIME)
                for t in range(part * SHARE, (part + 1) * SHARE):
                    for half in range(2):
                        n = 2 * t + half
                        pe.wait_ge(summed, ND * f + n - 3 + PRIME)
                        for s, (a, w) in enumerate(((0, 0), (0, 1), (1, 0))):
                            m = pe.matmul(bank[4 + (ND * u + n) % 4][:], hT[u][a][:, t * P:(t + 1) * P],
                                          dw[u][w][:, half * 512:half * 512 + 512], start=s == 0, stop=s == 2)
                        m.then_inc(down, 1)

            for n in range(NT):
                gates(0, 0, n)
            with pe.Fori(0, FC // 2 - 1) as i:
                for v in range(2):
                    for n in range(NT):
                        gates(2 * i + v + 1, 1 - v, n)
                        downs(2 * i + v, v, n)
            for n in range(NT):
                gates(FC - 1, 1, n)
                downs(FC - 2, 0, n)
            for n in range(NT):
                downs(FC - 1, 1, n)

        @block.scalar
        def _(act):
            for x in (g_hi, d_hi, absd, exped, logd, sig, h_hi):
                act.sem_inc(x, PRIME)

            def split_gate(f, u):
                act.wait_ge(g_loaded, 32 * f + 32)
                act.wait_ge(gate_up, NT * (f - 1) + PRIME)
                act.activation(gw[u][0][0][:], graw[0][:], ACT.Copy)
                act.activation(gw[u][1][0][:], graw[1][:], ACT.Copy).then_inc(g_hi, 1)

            def split_down(f, u):
                act.wait_ge(d_loaded, 16 * f + 16)
                act.wait_ge(down, ND * (f - 1) + PRIME)
                act.activation(dw[u][0][:], draw[:], ACT.Copy).then_inc(d_hi, 1)

            def log_of_gate(f, u, n):
                b = (NT * u + n) % 2
                act.wait_ge(gate_up, NT * f + n + 1 + PRIME)
                act.wait_ge(silu, NT * f + n - 1 + PRIME)
                act.activation(e_t[b][:], bank[2 * b][:, 0:TW], ACT.Abs).then_inc(absd, 1)
                act.wait_ge(absd, NT * f + n + 1 + PRIME)
                act.activation(e_t[b][:], e_t[b][:], ACT.Exp, scale=-1.0).then_inc(exped, 1)
                act.wait_ge(exped, NT * f + n + 1 + PRIME)
                act.activation(e_t[b][:], e_t[b][:], ACT.Ln, bias=1.0).then_inc(logd, 1)

            def hidden(f, u, n):
                b = (NT * u + n) % 2
                act.wait_ge(logsig, NT * f + n + 1 + PRIME)
                act.activation(e_t[b][:], e_t[b][:], ACT.Exp).then_inc(sig, 1)
                act.wait_ge(prod, NT * f + n + 1 + PRIME)
                act.wait_ge(down, ND * (f - 1) + PRIME)
                act.activation(hT[u][0][:, n * TW:(n + 1) * TW], h_t[b][:], ACT.Copy).then_inc(h_hi, 1)

            def chunk(f, u, more=True):
                for n in range(NT):
                    log_of_gate(f, u, n)
                    if n == 0:
                        split_down(f, u)
                    hidden(f, u, n)
                if more:
                    split_gate(f + 2, u)

            split_gate(0, 0)
            split_gate(1, 1)
            with act.Fori(0, FC // 2 - 1) as i:
                chunk(2 * i, 0)
                chunk(2 * i + 1, 1)
            chunk(FC - 2, 0, False)
            chunk(FC - 1, 1, False)

        @block.vector
        def _(dve):
            for x in (g_lo, d_lo, logsig, silu, prod, h_lo, summed):
                dve.sem_inc(x, PRIME)
            if blk:
                for u in range(2):
                    for j in range(2):
                        dve.memset(r32(hT[u][j][:, width:tiles * P]), 0.0).then_inc(pad, 1)

            def split_gate(f, u):
                dve.wait_ge(g_hi, f + 1 + PRIME)
                dve.tensor_tensor(gw[u][0][1][:], graw[0][:], r32(gw[u][0][0][:]), ALU.subtract)
                dve.tensor_tensor(gw[u][1][1][:], graw[1][:], r32(gw[u][1][0][:]), ALU.subtract).then_inc(g_lo, 1)

            def split_down(f, u):
                dve.wait_ge(d_hi, f + 1 + PRIME)
                dve.tensor_tensor(dw[u][1][:], draw[:], r32(dw[u][0][:]), ALU.subtract).then_inc(d_lo, 1)

            def hidden(f, u, n):
                b = (NT * u + n) % 2
                dve.wait_ge(logd, NT * f + n + 1 + PRIME)
                dve.scalar_tensor_tensor(e_t[b][:], bank[2 * b][:, 0:TW], 0.0, e_t[b][:],
                                         ALU.min, ALU.subtract).then_inc(logsig, 1)
                if n == 0:
                    split_down(f, u)
                dve.wait_ge(sig, NT * f + n + 1 + PRIME)
                dve.wait_ge(h_hi, NT * f + n - 1 + PRIME)
                dve.wait_ge(h_lo, NT * f + n - 1 + PRIME)
                dve.tensor_tensor(h_t[b][:], bank[2 * b][:, 0:TW], e_t[b][:], ALU.mult).then_inc(silu, 1)
                dve.wait_ge(silu, NT * f + n + 1 + PRIME)
                dve.tensor_tensor(h_t[b][:], bank[2 * b + 1][:, 0:TW], h_t[b][:], ALU.mult).then_inc(prod, 1)
                dve.wait_ge(h_hi, NT * f + n + 1 + PRIME)
                dve.tensor_tensor(hT[u][1][:, n * TW:(n + 1) * TW], h_t[b][:],
                                  r32(hT[u][0][:, n * TW:(n + 1) * TW]), ALU.subtract).then_inc(h_lo, 1)

            def sums(f, u, part):
                for n in range(2 * part * SHARE, 2 * (part + 1) * SHARE):
                    dve.wait_ge(down, ND * f + n + 1 + PRIME)
                    dve.wait_ge(summed, ND * (f - 1) + n + 1 + PRIME)
                    s = acc[:, n // 2, (n % 2) * 512:(n % 2) * 512 + 512]
                    dve.tensor_tensor(s, bank[4 + (ND * u + n) % 4][:], s, ALU.add).then_inc(summed, 1)

            split_gate(0, 0)
            split_gate(1, 1)
            for n in range(NT):
                hidden(0, 0, n)
            with dve.Fori(0, FC // 2 - 1) as i:
                for v in range(2):
                    split_gate(2 * i + v + 2, v)
                    for n in range(NT):
                        sums(2 * i + v, v, n)
                        hidden(2 * i + v + 1, 1 - v, n)
            for n in range(NT):
                sums(FC - 2, 0, n)
                hidden(FC - 1, 1, n)
            for n in range(NT):
                sums(FC - 1, 1, n)


def final_norm(nc, ctx, sem, sb, passed, eps_t, blk, acc, ln_g, ln_b, yp, ys):
    y = [sb(ctx, f"y{u}_{blk}", [P, D]) for u in range(2)]
    gain, bias = sb(ctx, f"g2_{blk}", [P, D]), sb(ctx, f"b2_{blk}", [P, D])
    stats = [sb(ctx, f"st2{u}_{blk}", [P, 2, 6]) for u in range(2)]
    mv = [sb(ctx, f"mv2{u}_{blk}", [P, 2]) for u in range(2)]
    lnv, rstd = sb(ctx, f"lnv2_{blk}", [P, 1]), [sb(ctx, f"rs2{u}_{blk}", [P, 1]) for u in range(2)]
    par_loaded = sem(f"n{blk}_par_loaded")
    stored = [sem(f"n{blk}_stored{u}") for u in range(2)]
    bn, var, lnd, rs, normed, scaled, shifted = (
        sem(f"n{blk}_{n}") for n in ("bn", "var", "ln", "rs", "normed", "scaled", "shifted"))
    t0 = 8 * blk

    with nc.Block() as block:
        def tiles(eng, f):
            with eng.Fori(0, 4) as i:
                for u in range(2):
                    f(2 * i + u, u, i, P)
            if blk == 1:
                f(8, 0, 4, DEC)

        @block.sync
        def _(sp):
            sp.dma_start(gain[:], ln_g.rearrange("(a n) -> a n", a=1).broadcast_to([P, D])).then_inc(par_loaded, 16)
            sp.dma_start(bias[:], ln_b.rearrange("(a n) -> a n", a=1).broadcast_to([P, D])).then_inc(par_loaded, 16)

            def store(t, u, times, rows):
                sp.wait_ge(shifted, t + 1 + PRIME)
                sp.sem_inc(passed, 1)
                if rows == P:
                    sp.dma_start(yp[bass.ds((t + t0) * P, P), :], y[u][:]).then_inc(stored[u], 16)
                else:
                    sp.dma_start(ys, y[u][0:DEC, :]).then_inc(stored[u], 16)

            tiles(sp, store)
            sp.wait_ge(stored[0], 16 * (4 + blk))
            sp.sem_inc(passed, 1)
            sp.wait_ge(stored[1], 16 * 4)

        @block.scalar
        def _(act):
            act.sem_inc(lnd, PRIME)
            act.sem_inc(rs, PRIME)

            def dev(t, u, times, rows):
                act.wait_ge(var, t + 1 + PRIME)
                act.activation(lnv[:], mv[u][:, 1:2], ACT.Ln, bias=eps_t[:]).then_inc(lnd, 1)
                act.wait_ge(lnd, t + 1 + PRIME)
                act.wait_ge(normed, t - 1 + PRIME)
                act.activation(rstd[u][:], lnv[:], ACT.Exp, scale=-0.5).then_inc(rs, 1)

            tiles(act, dev)

        @block.vector
        def _(dve):
            for x in (bn, var, normed):
                dve.sem_inc(x, PRIME)

            def norm(t, u, times, rows):
                row = acc[:, bass.ds(t, 1), :].rearrange("p a n -> p (a n)")
                for half in range(2):
                    m = dve.bn_stats(stats[u][:, half, :], row[:, half * 512:half * 512 + 512])
                m.then_inc(bn, 1)
                dve.wait_ge(bn, t + 1 + PRIME)
                dve.wait_ge(rs, t - 1 + PRIME)
                dve.sem_inc(passed, 1)
                dve.bn_aggr(mv[u][:], stats[u][:].rearrange("p a b -> p (a b)")).then_inc(var, 1)
                dve.wait_ge(rs, t + 1 + PRIME)
                dve.wait_ge(stored[u], 16 * times)
                dve.tensor_scalar(y[u][:], row, mv[u][:, 0:1], rstd[u][:, 0:1], ALU.subtract, ALU.mult)\
                   .then_inc(normed, 1)

            tiles(dve, norm)

        @block.gpsimd
        def _(pool):
            pool.sem_inc(scaled, PRIME)
            pool.sem_inc(shifted, PRIME)
            pool.wait_ge(par_loaded, 32)

            def affine(t, u, times, rows):
                pool.wait_ge(normed, t + 1 + PRIME)
                pool.sem_inc(passed, 1)
                pool.tensor_tensor(y[u][:], y[u][:], gain[:], ALU.mult).then_inc(scaled, 1)
                pool.wait_ge(scaled, t + 1 + PRIME)
                pool.sem_inc(passed, 1)
                pool.tensor_tensor(y[u][:], y[u][:], bias[:], ALU.add).then_inc(shifted, 1)

            tiles(pool, affine)


_INS = ["x_prompt", "x_sample", "cache_k", "cache_v", "state_pool", "w_in", "pool_w", "pool_scale", "w_out",
        "ln1_g", "ln1_b", "w_gate", "w_up", "w_down", "ln2_g", "ln2_b"]
_OUTS = [(1, SEQ, D), (1, DEC, D), (1, SEQ, HEADS, HD), (1, SEQ, HEADS, HD), (1, HIST, SBW),
         (1, DEC, HEADS, HD), (1, DEC, HEADS, HD), (1, HIST, SBW)]


def kernel(**inputs):
    import numpy as _np
    import concourse.bacc as _bacc
    from concourse import mybir as _mybir
    from concourse.bass_utils import run_bass_kernel_spmd as _run

    nc = _bacc.Bacc("TRN2", target_bir_lowering=False, num_devices=1)
    arrays, args = {}, []
    for name in _INS:
        a = _np.ascontiguousarray(inputs[name])
        arrays[f"in_{name}_dram"] = a
        args.append(nc.dram_tensor(f"in_{name}_dram", a.shape, _mybir.dt.from_np(a.dtype), kind="ExternalInput").ap())
    for i, shape in enumerate(_OUTS):
        args.append(nc.dram_tensor(f"out_{i}_dram", shape, _mybir.dt.float32, kind="ExternalOutput").ap())
    build(nc, *args)
    r = _run(nc, [arrays], core_ids=[0])
    return tuple(r.results[0][f"out_{i}_dram"] for i in range(len(_OUTS)))
```

```python
from collections import namedtuple
from contextlib import ExitStack, contextmanager

import concourse.bass as bass
from concourse import mybir

F32 = mybir.dt.float32
F32R = mybir.dt.float32r
ALU = mybir.AluOpType
ACT = mybir.ActivationFunctionType

P = 128
D = 1024
KD = D // P
SEQ = 2048
DEC = 32
TOK = SEQ + DEC
PT = SEQ // P
PAST = 1024
CT = PAST // P
SBW = 512
HEADS = 8
HD = 64
HC = SBW // P
WINDOWS = (2, 4, 8, 16)
HIST = 15
FF = 2816
FC = FF // P
ALPHA = 2.0 ** 0.25
EPS = 1e-5
PRIME = 96
NEG = -(2.0 ** 100)
TB = 416
NB = TOK // TB

Item = namedtuple("Item", "head tile key0 width first last group starts_group ends_group")
ITEMS = [Item(u, q, 512 * c, 512 if c < q // 4 else (q % 4 + 1) * P, c == q // 4, c == 0,
              PT // 4 * u + q // 4, q % 4 == 0 and c == q // 4, q % 4 == 3 and c == 0)
         for u in range(2) for q in range(PT) for c in range(q // 4, -1, -1)]
NI = len(ITEMS) // 2
ITEMS += [Item(2, 0, k0, w, k0 == PAST, k0 == 0, PT // 2, k0 == PAST, k0 == 0)
          for k0, w in ((PAST, P), (5 * P, 3 * P), (2 * P, 3 * P), (0, 2 * P))]


def r32(ap):
    return ap.bitcast(F32)


def build(nc, x_prompt, x_sample, cache_k, cache_v, state_pool, w_in, pool_w, pool_scale, w_out,
          ln1_g, ln1_b, w_gate, w_up, w_down, ln2_g, ln2_b,
          y_prompt, y_sample, k_prompt, v_prompt, pool_prompt, k_sample, v_sample, pool_sample):
    xp = x_prompt.rearrange("a t d -> (a t) d")
    xs = x_sample.rearrange("a t d -> (a t) d")
    ck = cache_k.rearrange("a t h d -> (a t) (h d)")
    cv = cache_v.rearrange("a t h d -> (a t) (h d)")
    sp = state_pool.rearrange("a t c -> (a t) c")
    yp = y_prompt.rearrange("a t d -> (a t) d")
    ys = y_sample.rearrange("a t d -> (a t) d")
    kp_out = k_prompt.rearrange("a t h d -> (a t) (h d)")
    vp_out = v_prompt.rearrange("a t h d -> (a t) (h d)")
    ks_out = k_sample.rearrange("a t h d -> (a t) (h d)")
    vs_out = v_sample.rearrange("a t h d -> (a t) (h d)")
    pp_out = pool_prompt.rearrange("a t c -> (a t) c")
    ps_out = pool_sample.rearrange("a t c -> (a t) c")

    qT_d = nc.dram_tensor("qT_scratch", [2, SBW, TOK], F32R).ap()
    kT_d = nc.dram_tensor("kT_scratch", [2, SBW, TOK], F32R).ap()
    kcT_d = nc.dram_tensor("kcT_scratch", [2, SBW, PAST], F32R).ap()
    mixT_d = nc.dram_tensor("mixT_scratch", [2, D, TOK], F32R).ap()
    x1_d = nc.dram_tensor("x1_scratch", [TOK, D], F32).ap()

    top = ExitStack()
    used = []

    def sem(n):
        used.append(nc.alloc_semaphore(name=n))
        return used[-1]

    @contextmanager
    def phase():
        with ExitStack() as ctx:
            yield ctx
            with nc.Block() as block:
                @block.sync
                def _(sp):
                    for x in used:
                        sp.sem_clear(x)
            for x in used:
                nc.release_semaphore(x)
            used.clear()

    def sb(ctx, n, shape, dt=F32):
        return ctx.enter_context(nc.sbuf_tensor(n, shape, dt))

    with top:
        passed = nc.alloc_semaphore(name="passed")
        bank = [top.enter_context(nc.psum_tensor(f"bank{i}", [P, 512], F32)) for i in range(8)]
        ident = sb(top, "ident", [P, P])
        ident_r = sb(top, "ident_r", [P, P], F32R)
        mask = sb(top, "mask", [P, P])
        mask_r = sb(top, "mask_r", [P, P], F32R)
        maskd_r = sb(top, "maskd_r", [P, P], F32R)
        eps_t = sb(top, "eps_t", [P, 1])

        constants(nc, sem, ident, ident_r, mask, mask_r, maskd_r, eps_t)
        with phase() as ctx:
            xT = [sb(ctx, f"xT{j}", [P, KD, TOK], F32R) for j in range(2)]
            transpose_inputs(nc, sem, sb, passed, bank, ident, xp, xs, ck, xT, kcT_d)
            project(nc, ctx, sem, sb, passed, bank, ident, xT, w_in, sp, pool_w, pool_scale,
                    qT_d, kT_d, mixT_d, kp_out, vp_out, ks_out, vs_out, pp_out, ps_out)
        with ExitStack() as both:
            wo = [sb(both, f"wo{j}", [P, KD, D], F32R) for j in range(2)]
            with phase() as ctx:
                attend(nc, ctx, sem, sb, passed, bank, ident, ident_r, mask_r, maskd_r, cv, qT_d, kT_d, kcT_d,
                       vp_out, vs_out, mixT_d, w_out, wo)
            with phase() as ctx:
                mix_norm(nc, ctx, sem, sb, passed, bank, eps_t, xp, xs, mixT_d, wo, ln1_g, ln1_b, x1_d)
        with phase() as ctx:
            ffn(nc, ctx, sem, sb, passed, bank, ident, eps_t, x1_d, w_gate, w_up, w_down, ln2_g, ln2_b, yp, ys)


def constants(nc, sem, ident, ident_r, mask, mask_r, maskd_r, eps_t):
    filled, made, cast = sem("c_filled"), sem("c_made"), sem("c_cast")
    with nc.Block() as block:
        @block.gpsimd
        def _(pool):
            pool.memset(ident[:], 0.0).then_inc(filled, 1)
            pool.memset(mask[:], 0.0).then_inc(filled, 1)
            pool.wait_ge(filled, 2)
            pool.affine_select(out=ident[:], in_=ident[:], compare_op=ALU.not_equal, fill=1.0, base=0,
                               pattern=[[-1, P]], channel_multiplier=1).then_inc(made, 1)
            pool.affine_select(out=mask[:], in_=mask[:], compare_op=ALU.is_gt, fill=NEG, base=0,
                               pattern=[[-1, P]], channel_multiplier=1).then_inc(made, 1)

        @block.vector
        def _(dve):
            dve.memset(eps_t[:], EPS)
            dve.memset(r32(maskd_r[:]), NEG).then_inc(cast, 1)
            dve.wait_ge(made, 2)
            dve.wait_ge(cast, 1)
            dve.tensor_copy(ident_r[:], ident[:])
            dve.tensor_copy(mask_r[:], mask[:])
            for h in range(4):
                s = slice(DEC * h, DEC * h + DEC)
                dve.tensor_copy(maskd_r[s, 0:DEC], mask[s, s])


def transpose_inputs(nc, sem, sb, passed, bank, ident, xp, xs, ck, xT, kcT_d):
    NX, NK = 4, 2
    with ExitStack() as mem:
        xin = [sb(mem, f"xin{u}", [P, D]) for u in range(NX)]
        kin = [sb(mem, f"kin{u}", [P, SBW]) for u in range(NK)]
        kparts = [sb(mem, f"kparts{u}", [P, 2, HC, P], F32R) for u in range(NK)]
        x_loaded = [sem(f"x_loaded{u}") for u in range(NX)]
        k_loaded = [sem(f"kc_loaded{u}") for u in range(NK)]
        stored = [sem(f"kc_stored{u}") for u in range(NK)]
        turned, hi_done, lo_done = sem("x_turned"), sem("x_hi"), sem("x_lo")
        k_turned, k_hi, k_lo = sem("kc_turned"), sem("kc_hi"), sem("kc_lo")
        assert PT // NX == CT // NK

        def tiles(eng, x_tile, k_tile):
            with eng.Fori(0, PT // NX) as i:
                for u in range(NX):
                    x_tile(NX * i + u, u, i, P)
                    if u % 2:
                        k_tile(NK * i + u // 2, u // 2, i)
            x_tile(PT, 0, PT // NX, DEC)

        with nc.Block() as block:
            @block.sync
            def _(sp):
                def load_x(t, u, times, rows):
                    sp.wait_ge(turned, t - NX + 1 + PRIME)
                    sp.sem_inc(passed, 1)
                    if rows == P:
                        sp.dma_start(xin[u][:], xp[bass.ds(t * P, P), :]).then_inc(x_loaded[u], 16)
                    else:
                        sp.dma_start(xin[u][0:DEC, :], xs).then_inc(x_loaded[u], 16)

                def load_k(t, u, times):
                    sp.wait_ge(k_turned, t - NK + 1 + PRIME)
                    sp.sem_inc(passed, 1)
                    sp.dma_start(kin[u][:], ck[bass.ds(t * P, P), :]).then_inc(k_loaded[u], 16)

                tiles(sp, load_x, load_k)

            @block.tensor
            def _(pe):
                pe.sem_inc(turned, PRIME)
                pe.sem_inc(k_turned, PRIME)

                def turn_x(t, u, times, rows):
                    pe.wait_ge(x_loaded[u], 16 * times + 16)
                    pe.wait_ge(lo_done, t - 1 + PRIME)
                    for k in range(KD):
                        m = pe.transpose(bank[2 * (u % 2) + k // 4][:, (k % 4) * P:(k % 4) * P + rows],
                                         xin[u][0:rows, k * P:(k + 1) * P], ident[0:rows, 0:rows])
                    m.then_inc(turned, 1)

                def turn_k(t, u, times):
                    pe.wait_ge(k_loaded[u], 16 * times + 16)
                    pe.wait_ge(k_lo, t - NK + 1 + PRIME)
                    for c in range(HC):
                        m = pe.transpose(bank[4 + u][:, c * P:(c + 1) * P], kin[u][:, c * P:(c + 1) * P], ident[:, :])
                    m.then_inc(k_turned, 1)

                tiles(pe, turn_x, turn_k)

            def halves(t, u, rows):
                for b in range(2):
                    yield bank[2 * (u % 2) + b][:, :].rearrange("p (k n) -> p k n", k=4)[:, :, 0:rows], \
                        (slice(None), slice(4 * b, 4 * b + 4), bass.ds(t * P, rows))

            def of_keys(u, j):
                return kparts[u][:, j, :, :].rearrange("p c n -> p (c n)")

            @block.scalar
            def _(act):
                act.sem_inc(hi_done, PRIME)
                act.sem_inc(k_hi, PRIME)

                def hi_x(t, u, times, rows):
                    act.wait_ge(turned, t + 1 + PRIME)
                    for src, at in halves(t, u, rows):
                        m = act.activation(xT[0][at], src, ACT.Copy)
                    m.then_inc(hi_done, 1)

                def hi_k(t, u, times):
                    act.wait_ge(k_turned, t + 1 + PRIME)
                    act.wait_ge(stored[u], 32 * times)
                    act.activation(of_keys(u, 0), bank[4 + u][:], ACT.Copy).then_inc(k_hi, 1)

                tiles(act, hi_x, hi_k)

            @block.vector
            def _(dve):
                dve.sem_inc(lo_done, PRIME)
                dve.sem_inc(k_lo, PRIME)

                def lo_x(t, u, times, rows):
                    dve.wait_ge(hi_done, t + 1 + PRIME)
                    for src, at in halves(t, u, rows):
                        m = dve.tensor_tensor(xT[1][at], src, r32(xT[0][at]), ALU.subtract)
                    m.then_inc(lo_done, 1)

                def lo_k(t, u, times):
                    dve.wait_ge(k_hi, t + 1 + PRIME)
                    dve.tensor_tensor(of_keys(u, 1), bank[4 + u][:], r32(of_keys(u, 0)), ALU.subtract)\
                       .then_inc(k_lo, 1)

                tiles(dve, lo_x, lo_k)

            @block.gpsimd
            def _(pool):
                with pool.Fori(0, CT // NK) as i:
                    for u in range(NK):
                        pool.wait_ge(k_lo, NK * i + u + 1 + PRIME)
                        pool.sem_inc(passed, 1)
                        for j in range(2):
                            pool.dma_start(r32(kcT_d[j].rearrange("(c p) t -> p c t", p=P)
                                               [:, :, bass.ds((NK * i + u) * P, P)]),
                                           r32(kparts[u][:, j, :, :])).then_inc(stored[u], 16)
                for u in range(NK):
                    pool.wait_ge(stored[u], 32 * CT // NK)


def project(nc, ctx, sem, sb, passed, bank, ident, xT, w_in, sp_in, pool_w, pool_scale,
            qT_d, kT_d, mixT_d, kp_out, vp_out, ks_out, vs_out, pp_out, ps_out):
    PAD = 16
    UW = PAD + SEQ + PAD + DEC
    S0 = PAD + SEQ + PAD
    wraw = sb(ctx, "wraw", [P, KD, P])
    whi = [sb(ctx, f"whi{u}", [P, KD, P], F32R) for u in range(2)]
    wlo = [sb(ctx, f"wlo{u}", [P, KD, P], F32R) for u in range(2)]
    col = [sb(ctx, f"col{u}", [P, UW]) for u in range(2)]
    parts = sb(ctx, "parts", [P, 2, TOK], F32R)
    nat = sb(ctx, "nat", [P, 17 * P])
    nat3 = nat[:, :].rearrange("p (t c) -> p t c", c=P)
    pw_raw = nat3[:, 0:4, :]
    pw = [sb(ctx, f"pw_{n}", [P, 4, P], F32R) for n in ("hi", "lo")]
    tails = col[1][:, 0:2 * P].rearrange("p (a b) -> p a b", a=2)
    d_parts = [[sb(ctx, f"d_parts{k}{j}", [P, TB + PAD], F32R) for j in range(2)] for k in range(2)]
    pscale = sb(ctx, "pscale", [P, 4])
    hist_in = nat[0:DEC, SBW:2 * SBW]
    hist = sb(ctx, "hist", [P, 4, PAD])
    rcount = sb(ctx, "rcount", [P, PAD])

    w_loaded = sem("w_loaded")
    w_hi, w_lo = sem("w_hi"), sem("w_lo")
    mm_done, col_done = sem("mm_done"), sem("col_done")
    parts_hi, parts_lo = sem("parts_hi"), sem("parts_lo")
    nat_turned, nat_done = sem("nat_turned"), sem("nat_done")
    stored = sem("p_stored")
    pre_loaded, pre_done = sem("pre_loaded"), sem("pre_done")
    hist_turned, hist_done = sem("hist_turned"), sem("hist_done")
    d_done, d_hi, d_lo, pooled_done, pooled_out, pooled_hi, pooled_lo = (
        sem(n) for n in ("d_done", "d_hi", "d_lo", "pooled_done", "pooled_out", "pooled_hi", "pooled_lo"))
    dve_chain = sem("p_dve_chain")

    wv = w_in.rearrange("(k p) n -> p k n", p=P)
    N_ST = {"q": 2, "k": 4, "v": 2, "u": 4}

    def st_before(kind, c):
        return 16 * (sum(N_ST[k] * 4 for k in "qkvu"[:"qkvu".index(kind)]) + N_ST[kind] * c)

    NBT = 5

    LW = PAD + TB + PAD
    ladder = [nat[:, LW * k:LW * (k + 1)] for k in range(2)]
    d_t = nat[:, 2 * LW:3 * LW - PAD]
    pooled = [nat[:, 3 * LW + TB * k:3 * LW + TB * (k + 1)] for k in range(2)]
    U = 4 * NB

    def span(b):
        return PAD + TB * b, TB if b < NB - 1 else TB + PAD

    def tok_cols(b):
        lo, hi = b * TB, (b + 1) * TB
        if hi <= SEQ:
            return [(0, TB, PAD + lo)]
        return [(0, SEQ - lo, PAD + lo), (SEQ - lo, hi - SEQ, S0)]

    with nc.Block() as block:
        @block.sync
        def _(sp):
            def load(n):
                sp.wait_ge(w_lo, n + PRIME)
                sp.sem_inc(passed, 1)
                sp.dma_start(wraw[:], wv[:, :, bass.ds(n * P, P)]).then_inc(w_loaded, 16)

            sp.wait_ge(pre_done, 1)
            sp.dma_start(hist_in[1:1 + HIST, :], sp_in).then_inc(pre_loaded, 16)
            sp.dma_start(pw_raw[:], pool_w.rearrange("g c d -> c g d")).then_inc(pre_loaded, 16)
            with nc.allow_non_contiguous_dma(reason="512 scales, one a partition"):
                sp.dma_start(pscale[:], pool_scale.rearrange("(g p) -> p g", p=P)).then_inc(pre_loaded, 16)
            load(0)
            load(1)

            def store_parts(n, dst, row):
                sp.wait_ge(parts_lo, n + 1 + PRIME)
                sp.sem_inc(passed, 1)
                for j in range(2):
                    sp.dma_start(r32(dst[j, bass.ds(row, P), :]), r32(parts[:, j, :])).then_inc(stored, 16)

            with sp.Fori(0, 2) as i:
                for u in range(2):
                    load(2 * i + u + 2)
                    store_parts(2 * i + u, qT_d, (2 * i + u) * P)
            with sp.Fori(0, 2) as i:
                for u in range(2):
                    c = 2 * i + u
                    load(c + 6)
                    store_parts(c + 4, kT_d, c * P)
                    sp.wait_ge(nat_done, NBT * (c + 1) + PRIME)
                    sp.sem_inc(passed, 1)
                    sp.dma_start(kp_out.rearrange("(t p) c -> p t c", p=P)[:, :, bass.ds(c * P, P)],
                                 nat3[:, 0:PT, :]).then_inc(stored, 16)
                    sp.dma_start(ks_out[:, bass.ds(c * P, P)], nat3[0:DEC, PT, :]).then_inc(stored, 16)
            with sp.Fori(0, 2) as i:
                for u in range(2):
                    c = 2 * i + u
                    load(c + 10)
                    sp.wait_ge(nat_done, NBT * (c + 5) + PRIME)
                    sp.sem_inc(passed, 1)
                    sp.dma_start(vp_out.rearrange("(t p) c -> p t c", p=P)[:, :, bass.ds(c * P, P)],
                                 nat3[:, 0:PT, :]).then_inc(stored, 16)
                    sp.dma_start(vs_out[:, bass.ds(c * P, P)], nat3[0:DEC, PT, :]).then_inc(stored, 16)
            for c in range(4):
                if c < 2:
                    load(c + 14)
                sp.wait_ge(hist_done, 2 + 2 * (c + 1))
                sp.dma_start(pp_out[:, c * P:(c + 1) * P], tails[P - HIST:P, 0, :]).then_inc(stored, 16)
                sp.dma_start(ps_out[:, c * P:(c + 1) * P], tails[DEC - HIST:DEC, 1, :]).then_inc(stored, 16)
                sp.wait_ge(pooled_lo, NB * (c + 1))
                for j in range(2):
                    sp.dma_start(r32(mixT_d[j, SBW + c * P:SBW + (c + 1) * P, :]), r32(parts[:, j, :]))\
                      .then_inc(stored, 16)
            sp.wait_ge(stored, st_before("u", 4))
            sp.sem_inc(passed, 1)

        @block.scalar
        def _(act):
            for x in (w_hi, col_done):
                act.sem_inc(x, PRIME)

            def split_w(n, u):
                act.wait_ge(w_loaded, 16 * (n + 1))
                act.wait_ge(mm_done, NB * (n - 1) + PRIME)
                act.activation(whi[u][:], wraw[:], ACT.Copy).then_inc(w_hi, 1)

            def columns(n, u, scale):
                for b in range(NB):
                    act.wait_ge(mm_done, NB * n + b + 1 + PRIME)
                    act.activation(col[u][:, b * TB:(b + 1) * TB], bank[(NB * u + b) % 2][:, 0:TB],
                                   ACT.Copy, scale=scale).then_inc(col_done, 1)

            split_w(0, 0)
            with act.Fori(0, 2) as i:
                for u in range(2):
                    n = 2 * i + u
                    split_w(n + 1, 1 - u)
                    act.wait_ge(parts_lo, n - 1 + PRIME)
                    columns(n, u, HD ** -0.5)
            with act.Fori(0, 2) as i:
                for u in range(2):
                    n = 2 * i + u + 4
                    split_w(n + 1, 1 - u)
                    act.wait_ge(parts_lo, n - 1 + PRIME)
                    act.wait_ge(nat_turned, NBT * (n - 5) + PRIME)
                    columns(n, u, 1.0)
            with act.Fori(0, 2) as i:
                for u in range(2):
                    n = 2 * i + u + 8
                    split_w(n + 1, 1 - u)
                    if u == 0:
                        act.wait_ge(parts_lo, 8 + PRIME)
                    act.wait_ge(nat_turned, NBT * (n - 5) + PRIME)
                    columns(n, u, 1.0)
            act.wait_ge(pre_loaded, 48)
            act.wait_ge(nat_turned, NBT * 8 + PRIME)
            for j in range(U + 3):
                c, b = divmod(j, NB)
                n = 12 + c
                if j < U:
                    act.wait_ge(mm_done, NB * n + b + 1 + PRIME)
                    if c > 0:
                        act.wait_ge(d_done, NB * (c - 1) + min(b + 2, NB))
                    if c > 0 and b == NB - 1:
                        act.wait_ge(hist_turned, c + 1)
                    for at0, w, at in tok_cols(b):
                        m = act.activation(col[0][:, at:at + w], bank[(NB * n + b) % 2][:, at0:at0 + w], ACT.Copy)
                    m.then_inc(col_done, 1)
                if 0 <= j - 1 < U:
                    k = j - 1
                    w = span(k % NB)[1]
                    act.wait_ge(d_done, k + 1)
                    if k >= 2:
                        act.wait_ge(pooled_done, k - 1)
                    act.activation(d_parts[k % 2][0][:, 0:w], d_t[:, 0:w], ACT.Copy).then_inc(d_hi, 1)
                if 0 <= j - 3 < U:
                    k = j - 3
                    act.wait_ge(pooled_done, k + 1)
                    if k >= 2:
                        act.wait_ge(pooled_lo, k - 1)
                    out = 0
                    for at0, w, at in tok_cols(k % NB):
                        src = at - span(k % NB)[0]
                        m = act.activation(pooled[k % 2][:, out:out + w], bank[4 + k % 2][:, src:src + w], ACT.Copy,
                                           scale=pscale[:, k // NB:k // NB + 1])
                        out += w
                    m.then_inc(pooled_out, 1)
                if b == 1 and c < 3:
                    split_w(n + 1, (n + 1) % 2)

        @block.tensor
        def _(pe):
            pe.sem_inc(mm_done, PRIME)
            pe.sem_inc(nat_turned, PRIME)
            pe.wait_ge(pre_loaded, 48)
            for g in range(4):
                m = pe.transpose(bank[6][:, g * DEC:(g + 1) * DEC], hist_in[:, g * P:(g + 1) * P],
                                 ident[0:DEC, 0:DEC])
            m.then_inc(hist_turned, 1)

            def product(n, u, par, b):
                if b == 0:
                    pe.wait_ge(w_lo, n + 1 + PRIME)
                pe.wait_ge(col_done, NB * n + b - 1 + PRIME)
                ps = bank[(par + b) % 2][:, 0:TB]
                for k in range(KD):
                    for j, (w, x) in enumerate(((whi, 0), (whi, 1), (wlo, 0))):
                        m = pe.matmul(ps, w[u][:, k, :], xT[x][:, k, b * TB:(b + 1) * TB],
                                      start=(k == 0 and j == 0), stop=(k == KD - 1 and j == 2))
                m.then_inc(mm_done, 1)

            def products(n, u, par):
                for b in range(NB):
                    product(n, u, par, b)

            def to_natural(m0, n, u, par):
                for b in range(NBT):
                    last_tile = min(4 * b + 4, 17)
                    pe.wait_ge(col_done, NB * n + min(NB, last_tile * P // TB + 1) + PRIME)
                    pe.wait_ge(nat_done, m0 + b - 1 + PRIME)
                    for t in range(4 * b, last_tile):
                        w = P if t < PT else DEC
                        m = pe.transpose(bank[2 + (par + b) % 2][0:w, (t % 4) * P:(t % 4 + 1) * P],
                                         col[u][:, t * P:t * P + w], ident[:, :])
                    m.then_inc(nat_turned, 1)

            with pe.Fori(0, 2) as i:
                for u in range(2):
                    products(2 * i + u, u, NB * u)
            for base in (4, 8):
                with pe.Fori(0, 2) as i:
                    for u in range(2):
                        n = 2 * i + u + base
                        products(n, u, NB * u)
                        to_natural(NBT * (n - 4), n, u, NBT * u)
            for j in range(U + 2):
                c, b = divmod(j, NB)
                if j < U:
                    product(12 + c, c % 2, NB * (12 + c), b)
                if b == 0 and c > 0:
                    pe.wait_ge(col_done, NB * (12 + c) + PRIME)
                    pe.wait_ge(hist_done, 2 * c)
                    pe.transpose(bank[6][:, 0:P], col[0][:, PAD + SEQ - P:PAD + SEQ], ident[:, :])
                    pe.transpose(bank[6][0:DEC, P:2 * P], col[0][:, S0:S0 + DEC], ident[:, :]).then_inc(hist_turned, 1)
                if j >= 2:
                    k = j - 2
                    w = span(k % NB)[1]
                    pe.wait_ge(d_lo, k + 1)
                    if k >= 2:
                        pe.wait_ge(pooled_out, k - 1)
                    for t, (a, d) in enumerate(((0, 0), (0, 1), (1, 0))):
                        m = pe.matmul(bank[4 + k % 2][:, 0:w], pw[a][:, k // NB, :], d_parts[k % 2][d][:, 0:w],
                                      start=t == 0, stop=t == 2)
                    m.then_inc(pooled_done, 1)

        @block.gpsimd
        def _(pool):
            pool.sem_inc(parts_hi, PRIME)
            pool.memset(hist_in, 0.0).then_inc(pre_done, 1)

            def hi_parts(n, u, base_st, c):
                pool.wait_ge(col_done, NB * (n + 1) + PRIME)
                pool.sem_inc(passed, 1)
                pool.wait_ge(stored, base_st)
                pool.sem_inc(passed, 1)
                pool.tensor_copy(parts[:, 0, 0:TOK], col[u][:, 0:TOK]).then_inc(parts_hi, 1)

            with pool.Fori(0, 2) as i:
                for u in range(2):
                    c = 2 * i + u
                    hi_parts(c, u, 32 * c, c)
            with pool.Fori(0, 2) as i:
                for u in range(2):
                    c = 2 * i + u
                    hi_parts(c + 4, u, 64 * c + st_before("k", 0), c)
            for k in range(U):
                c, b = divmod(k, NB)
                pool.wait_ge(pooled_out, k + 1)
                if b == 0:
                    pool.wait_ge(stored, st_before("u", c))
                at = slice(b * TB, (b + 1) * TB)
                pool.tensor_copy(parts[:, 0, at], pooled[k % 2]).then_inc(pooled_hi, 1)
                pool.wait_ge(pooled_hi, k + 1)
                pool.tensor_tensor(parts[:, 1, at], pooled[k % 2], r32(parts[:, 0, at]), ALU.subtract)\
                    .then_inc(pooled_lo, 1)

        @block.vector
        def _(dve):
            for x in (w_lo, parts_lo, nat_done):
                dve.sem_inc(x, PRIME)
            chain = [0]

            def link(m):
                chain[0] += 1
                m.then_inc(dve_chain, 1)
                dve.wait_ge(dve_chain, chain[0])

            def split_w(n, u):
                dve.wait_ge(w_hi, n + 1 + PRIME)
                dve.tensor_tensor(wlo[u][:], wraw[:], r32(whi[u][:]), ALU.subtract).then_inc(w_lo, 1)

            def lo_parts(n, u):
                dve.wait_ge(parts_hi, n + 1 + PRIME)
                dve.tensor_tensor(parts[:, 1, 0:TOK], col[u][:, 0:TOK], r32(parts[:, 0, 0:TOK]),
                                  ALU.subtract).then_inc(parts_lo, 1)

            def natural(m0, par, base_st):
                dve.wait_ge(stored, base_st)
                for b in range(NBT):
                    dve.wait_ge(nat_turned, m0 + b + 1 + PRIME)
                    if b < 4:
                        m = dve.tensor_copy(nat[:, 512 * b:512 * b + 512], bank[2 + (par + b) % 2][:])
                    else:
                        m = dve.tensor_copy(nat[0:DEC, PT * P:17 * P], bank[2 + (par + b) % 2][0:DEC, 0:P])
                    m.then_inc(nat_done, 1)

            for t in range(PAD):
                dve.memset(rcount[:, t:t + 1], 1.0 / (t + 1))
            dve.wait_ge(pre_loaded, 48)
            link(dve.tensor_copy(pw[0][:], pw_raw))
            dve.tensor_tensor(pw[1][:], pw_raw, r32(pw[0][:]), ALU.subtract)
            dve.wait_ge(hist_turned, 1)
            dve.tensor_copy(hist[:], bank[6][:, 0:4 * DEC].rearrange("p (g n) -> p g n", g=4)[:, :, 0:PAD])\
               .then_inc(hist_done, 2)
            split_w(0, 0)
            with dve.Fori(0, 2) as i:
                for u in range(2):
                    n = 2 * i + u
                    split_w(n + 1, 1 - u)
                    lo_parts(n, u)
            with dve.Fori(0, 2) as i:
                for u in range(2):
                    c = 2 * i + u
                    split_w(c + 5, 1 - u)
                    natural(NBT * c, NBT * u, 64 * c + st_before("k", 0))
                    lo_parts(c + 4, u)
            with dve.Fori(0, 2) as i:
                for u in range(2):
                    c = 2 * i + u
                    split_w(c + 9, 1 - u)
                    natural(NBT * (c + 4), NBT * u, 32 * c + st_before("v", 0))
            dve.wait_ge(stored, st_before("u", 0))
            dve.wait_ge(nat_turned, NBT * 8 + PRIME)
            dve.memset(col[0][:, 0:PAD], 0.0)
            for j in range(U + 1):
                c, b = divmod(j, NB)
                n = 12 + c
                if j >= 1:
                    k = j - 1
                    w = span(k % NB)[1]
                    dve.wait_ge(d_hi, k + 1)
                    dve.tensor_tensor(d_parts[k % 2][1][:, 0:w], d_t[:, 0:w], r32(d_parts[k % 2][0][:, 0:w]),
                                      ALU.subtract).then_inc(d_lo, 1)
                if j < U:
                    if b == 0:
                        link(dve.tensor_copy(col[0][:, S0 - PAD:S0], hist[:, c, :]))
                    dve.wait_ge(col_done, NB * n + b + 1 + PRIME)
                    start, w = span(b)
                    here = col[0][:, start - PAD:start + w]
                    src = here
                    for lv in range(c + 1):
                        back, dst = 1 << lv, ladder[lv % 2]
                        link(dve.tensor_tensor(dst[:, 2 * back - 1:PAD + w], src[:, 2 * back - 1:PAD + w],
                                               src[:, back - 1:PAD + w - back], ALU.add))
                        src = dst
                    m = dve.scalar_tensor_tensor(d_t[:, 0:w], src[:, PAD:PAD + w], 1.0 / WINDOWS[c], here[:, PAD:PAD + w],
                                                 ALU.mult, ALU.subtract)
                    if b == 0:
                        few = WINDOWS[c] - 1
                        link(m)
                        link(dve.tensor_tensor(d_t[:, 0:few], src[:, PAD:PAD + few], rcount[:, 0:few], ALU.mult))
                        m = dve.tensor_tensor(d_t[:, 0:few], d_t[:, 0:few], here[:, PAD:PAD + few], ALU.subtract)
                    m.then_inc(d_done, 1)
                if b == 1 and c < 3:
                    split_w(n + 1, (n + 1) % 2)
                if b == 1 and c > 0 or j == U:
                    done = c if j < U else 4
                    dve.wait_ge(hist_turned, done + 1)
                    if done > 1:
                        dve.wait_ge(stored, st_before("u", done - 1))
                    dve.tensor_copy(tails[:, 0, :], bank[6][:, 0:P]).then_inc(hist_done, 1)
                    dve.tensor_copy(tails[0:DEC, 1, :], bank[6][0:DEC, P:2 * P]).then_inc(hist_done, 1)


def attend(nc, ctx, sem, sb, passed, bank, ident, ident_r, mask_r, maskd_r, cv, qT_d, kT_d, kcT_d, vp_out, vs_out,
           mixT_d, w_out, wo):
    N = len(ITEMS)
    G = 2 * PT // 4 + 1
    OB = 3
    assert N % 12 == 0 and G % OB == 0
    KW = PAST + P
    k_st = [[sb(ctx, f"k_st{u}{j}", [P, SEQ], F32R) for j in range(2)] for u in range(2)]
    q_st = [sb(ctx, f"q_st{u}", [P, SEQ], F32R) for u in range(2)]
    v_st = [sb(ctx, f"v_st{u}", [P, PT, HD]) for u in range(2)]
    ks = [sb(ctx, f"ks{j}", [P, 2, KW], F32R) for j in range(2)]
    qs = sb(ctx, "qs", [P, 2, P], F32R)
    vs = sb(ctx, "vs", [P, 2, KW // P, HD])
    beta = [sb(ctx, f"beta{b}", [P, 512]) for b in range(3)]
    rest, a_t, aT = ([sb(ctx, f"{n}{b}", [P, 512]) for b in range(2)] for n in ("rest", "a_t", "aT"))
    left = [sb(ctx, f"left{b}", [P, SEQ + 1]) for b in range(2)] + [sb(ctx, "left_sample", [P, KW + 1])]
    o_t = [sb(ctx, f"o_t{b}", [HD, 512]) for b in range(OB)]
    oparts = [sb(ctx, f"oparts{b}", [HD, 2, 512], F32R) for b in range(OB)]
    wraw = sb(ctx, "wo_raw", [P, D])

    wo_loaded, wo_hi, wo_lo = sem("wo_loaded"), sem("wo_hi"), sem("wo_lo")
    loaded = [sem(f"a_loaded{u}") for u in range(2)]
    sample_loaded, zeroed, strips_filled = sem("a_sample_loaded"), sem("a_zeroed"), sem("a_strips_filled")
    z_done, beta_done, rest_done, left_done, turn_done, aT_done, av_done = (
        sem(f"a_{n}") for n in ("z", "beta", "rest", "left", "turn", "aT", "av"))
    a_done = [sem("a_even"), sem("a_odd")]
    o_done, opart_done = sem("a_o"), sem("a_opart")
    stored = [sem(f"a_stored{b}") for b in range(OB)]
    Z_BANK, T_BANK, O_BANK = 0, 4, 6
    NZ = 4

    AT_BETA, AT_LEFT, AT_A, AT_TURN, AT_OUT, AT_V, AT_O = 1, 2, 3, 4, 5, 6, 7
    STEPS = N + AT_O

    def z_bank(n):
        return bank[Z_BANK + n % NZ][:, 0:ITEMS[n].width]

    def half_count(n, i):
        return N // 2 * i + n // 2 + 1

    def strip(n):
        return left[2 if ITEMS[n].head == 2 else ITEMS[n].tile % 2]

    def group_end(n):
        return 0 <= n < N and ITEMS[n].ends_group

    with nc.Block() as block:
        @block.sync
        def _(sp):
            with sp.Fori(0, HEADS // 2) as i:
                for u in range(2):
                    sp.wait_ge(av_done, N * (i - 1) + NI * (u + 1) + PRIME)
                    sp.sem_inc(passed, 1)
                    row = (2 * i + u) * HD
                    for half in range(2):
                        s = slice(half * HD, half * HD + HD)
                        for j in range(2):
                            sp.dma_start(r32(k_st[u][j][s, :]), r32(kT_d[j, bass.ds(row, HD), 0:SEQ]))\
                              .then_inc(loaded[u], 16)
                        sp.dma_start(r32(q_st[u][s, :]), r32(qT_d[half, bass.ds(row, HD), 0:SEQ]))\
                          .then_inc(loaded[u], 16)
                    sp.dma_start(v_st[u][:], vp_out.rearrange("(t p) c -> p t c", p=P)[:, :, bass.ds(row, HD)])\
                      .then_inc(loaded[u], 16)
                sp.wait_ge(zeroed, 4)
                sp.wait_ge(av_done, N * i + PRIME)
                sp.sem_inc(passed, 1)
                for h in range(2):
                    row = (2 * i + h) * HD
                    for half in range(2):
                        s = slice(half * HD, half * HD + HD)
                        for j in range(2):
                            sp.dma_start(r32(ks[j][s, h, 0:PAST]), r32(kcT_d[j, bass.ds(row, HD), :]))\
                              .then_inc(sample_loaded, 16)
                            sp.dma_start(r32(ks[j][s, h, PAST:PAST + DEC]), r32(kT_d[j, bass.ds(row, HD), SEQ:TOK]))\
                              .then_inc(sample_loaded, 16)
                        sp.dma_start(r32(qs[s, h, h * DEC:(h + 1) * DEC]), r32(qT_d[half, bass.ds(row, HD), SEQ:TOK]))\
                          .then_inc(sample_loaded, 16)
                    sp.dma_start(vs[:, h, 0:CT, :], cv.rearrange("(t p) c -> p t c", p=P)[:, :, bass.ds(row, HD)])\
                      .then_inc(sample_loaded, 16)
                    sp.dma_start(vs[0:DEC, h, CT, :], vs_out[:, bass.ds(row, HD)]).then_inc(sample_loaded, 16)

        @block.tensor
        def _(pe):
            for x in (z_done, turn_done, av_done):
                pe.sem_inc(x, PRIME)
            with pe.Fori(0, HEADS // 2) as i:
                def scores(n):
                    it, z = ITEMS[n], z_bank(n)
                    if n % NI == 0 and it.head < 2:
                        pe.wait_ge(loaded[it.head], 16 * 7 * (i + 1))
                    if it.head == 2 and it.first:
                        pe.wait_ge(sample_loaded, 16 * 24 * (i + 1))
                    pe.wait_ge(rest_done, N * i + n - NZ + 1 + PRIME)
                    keys = slice(it.key0, it.key0 + it.width)
                    if it.head < 2:
                        queries = q_st[it.head][:, it.tile * P:(it.tile + 1) * P]
                        terms = [(queries, k_st[it.head][j][:, keys]) for j in range(2)]
                    else:
                        terms = [(qs[:, h, :], ks[j][:, h, keys]) for h in range(2) for j in range(2)]
                    for k, (queries, right) in enumerate(terms):
                        if it.first and k == len(terms) - 1:
                            pe.matmul(z[:, it.width - P:it.width], ident_r[:], (mask_r if it.head < 2 else maskd_r)[:],
                                      start=False, stop=False, skip_group_check=True)
                        m = pe.matmul(z, queries, right, start=k == 0, stop=k == len(terms) - 1)
                    m.then_inc(z_done, 1)

                def turn(n):
                    pe.wait_ge(a_done[n % 2], half_count(n, i) + PRIME)
                    pe.wait_ge(aT_done, N * i + n - 1 + PRIME)
                    for b in range(ITEMS[n].width // P):
                        m = pe.transpose(bank[T_BANK + n % 2][:, b * P:(b + 1) * P],
                                         a_t[n % 2][:, b * P:(b + 1) * P], ident[:, :])
                    m.then_inc(turn_done, 1)

                def values(n):
                    it = ITEMS[n]
                    pe.wait_ge(aT_done, N * i + n + 1 + PRIME)
                    g = it.group
                    if it.starts_group:
                        pe.wait_ge(o_done, G * i + (g if g in (0, G - 1) else g - 1) + PRIME)
                    for b in range(it.width // P):
                        start, stop = it.first and b == 0, it.last and b == it.width // P - 1
                        t = it.key0 // P + b
                        if it.head < 2:
                            m = pe.matmul(bank[O_BANK + g % 2][0:HD, (it.tile % 4) * P:(it.tile % 4 + 1) * P],
                                          v_st[it.head][:, t, :], aT[n % 2][:, b * P:(b + 1) * P],
                                          start=start, stop=stop)
                        else:
                            for h in range(2):
                                m = pe.matmul(bank[O_BANK + h][0:HD, 0:DEC], vs[:, h, t, :],
                                              aT[n % 2][:, b * P + h * DEC:b * P + (h + 1) * DEC],
                                              start=start, stop=stop)
                    m.then_inc(av_done, 1)

                for s in range(STEPS):
                    if 0 <= s - AT_V < N:
                        values(s - AT_V)
                    if 0 <= s - AT_TURN < N:
                        turn(s - AT_TURN)
                    if s < N:
                        scores(s)

        @block.scalar
        def _(act):
            for x in (beta_done, rest_done, o_done):
                act.sem_inc(x, PRIME)
            with act.Fori(0, HEADS // 2) as i:
                for s in range(STEPS + 1):
                    n = s - AT_BETA
                    if 0 <= n < N:
                        w = ITEMS[n].width
                        act.wait_ge(z_done, N * i + n + 1 + PRIME)
                        act.wait_ge(a_done[(n - 3) % 2], half_count(n - 3, i) + PRIME)
                        act.activation(beta[n % 3][:, 0:w], z_bank(n), ACT.Sigmoid).then_inc(beta_done, 1)
                        act.wait_ge(left_done, N * i + n - 1 + PRIME)
                        act.activation(rest[n % 2][:, 0:w], z_bank(n), ACT.Sigmoid, scale=-1.0).then_inc(rest_done, 1)
                    n = s - AT_O
                    if group_end(n):
                        g = ITEMS[n].group
                        act.wait_ge(av_done, N * i + n + 1 + PRIME)
                        act.wait_ge(opart_done, 2 * (G * i + g - OB + 1) + PRIME)
                        if g < G - 1:
                            m = act.activation(o_t[g % OB][:], bank[O_BANK + g % 2][0:HD, :], ACT.Copy)
                        else:
                            for h in range(2):
                                m = act.activation(o_t[g % OB][:, h * DEC:(h + 1) * DEC],
                                                   bank[O_BANK + h][0:HD, 0:DEC], ACT.Copy)
                        m.then_inc(o_done, 1)

        @block.vector
        def _(dve):
            for x in (left_done, aT_done, a_done[1]):
                dve.sem_inc(x, PRIME)
            dve.memset(r32(qs[:]), 0.0).then_inc(zeroed, 1)
            dve.memset(vs[:, :, CT, :], 0.0).then_inc(zeroed, 1)
            for j in range(2):
                dve.memset(r32(ks[j][:, :, PAST:KW]), 0.0).then_inc(zeroed, 1)
            for x in left:
                dve.memset(x[:], 1.0).then_inc(strips_filled, 1)
            dve.wait_ge(strips_filled, len(left))
            with dve.Fori(0, HEADS // 2) as i:
                for s in range(STEPS):
                    n = s - AT_LEFT
                    if 0 <= n < N:
                        w, at = ITEMS[n].width, ITEMS[n].key0
                        dve.wait_ge(rest_done, N * i + n + 1 + PRIME)
                        if ITEMS[n].first:
                            for m in (n - 2, n - 3):
                                dve.wait_ge(a_done[m % 2], half_count(m, i) + PRIME)
                        else:
                            dve.wait_ge(left_done, N * i + n + PRIME)
                        back = rest[n % 2][:, 0:w][:, ::-1]
                        dve.tensor_tensor_scan(strip(n)[:, at:at + w][:, ::-1], back, back,
                                               1.0 if ITEMS[n].first else strip(n)[:, at + w:at + w + 1],
                                               ALU.mult, ALU.min).then_inc(left_done, 1)
                    n = s - AT_A
                    if 0 <= n < N and n % 2 == 1:
                        w, at = ITEMS[n].width, ITEMS[n].key0
                        dve.wait_ge(left_done, N * i + n + 1 + PRIME)
                        dve.wait_ge(turn_done, N * i + n - 1 + PRIME)
                        dve.tensor_tensor(a_t[1][:, 0:w], beta[n % 3][:, 0:w], strip(n)[:, at + 1:at + w + 1],
                                          ALU.mult).then_inc(a_done[1], 1)
                    n = s - AT_OUT
                    if 0 <= n < N:
                        w = ITEMS[n].width
                        dve.wait_ge(turn_done, N * i + n + 1 + PRIME)
                        dve.wait_ge(av_done, N * i + n - 1 + PRIME)
                        dve.tensor_copy(aT[n % 2][:, 0:w], bank[T_BANK + n % 2][:, 0:w]).then_inc(aT_done, 1)

        @block.gpsimd
        def _(pool):
            for x in (a_done[0], opart_done, wo_hi, wo_lo):
                pool.sem_inc(x, PRIME)
            with pool.Fori(0, HEADS // 2) as i:
                def outputs(g, stage):
                    w = 512 if g < G - 1 else 2 * DEC
                    out, parts = o_t[g % OB], oparts[g % OB]
                    if stage == 0:
                        pool.wait_ge(o_done, G * i + g + 1 + PRIME)
                        pool.sem_inc(passed, 1)
                        pool.wait_ge(stored[g % OB], 32 * (G // OB * i + g // OB))
                        pool.sem_inc(passed, 1)
                        pool.tensor_copy(parts[:, 0, 0:w], out[:, 0:w]).then_inc(opart_done, 1)
                    elif stage == 1:
                        pool.wait_ge(opart_done, 2 * (G * i + g) + 1 + PRIME)
                        pool.sem_inc(passed, 1)
                        pool.tensor_tensor(parts[:, 1, 0:w], out[:, 0:w], r32(parts[:, 0, 0:w]), ALU.subtract)\
                            .then_inc(opart_done, 1)
                    else:
                        pool.wait_ge(opart_done, 2 * (G * i + g) + 2 + PRIME)
                        pool.sem_inc(passed, 1)
                        if g < G - 1:
                            for j in range(2):
                                pool.dma_start(r32(mixT_d[j, bass.ds((2 * i + g // 4) * HD, HD),
                                                          (g % 4) * 512:(g % 4 + 1) * 512]),
                                               r32(parts[:, j, :])).then_inc(stored[g % OB], 16)
                        else:
                            for j in range(2):
                                pool.dma_start(r32(mixT_d[j, bass.ds(2 * i * HD, 2 * HD), SEQ:TOK]
                                                   .rearrange("(h d) t -> d h t", h=2)),
                                               r32(parts[:, j, 0:w].rearrange("d (h t) -> d h t", h=2)))\
                                    .then_inc(stored[g % OB], 16)

                def split_w_out(k, stage):
                    c = 2 * i + k
                    if stage == 0:
                        pool.wait_ge(wo_lo, c + PRIME)
                        pool.sem_inc(passed, 1)
                        pool.dma_start(wraw[:], w_out[bass.ds(c * P, P), :]).then_inc(wo_loaded, 16)
                    elif stage == 1:
                        pool.wait_ge(wo_loaded, 16 * c + 16)
                        pool.sem_inc(passed, 1)
                        pool.tensor_copy(wo[0][:, bass.ds(c, 1), :].rearrange("p a n -> p (a n)"), wraw[:])\
                            .then_inc(wo_hi, 1)
                    else:
                        pool.wait_ge(wo_hi, c + 1 + PRIME)
                        pool.sem_inc(passed, 1)
                        pool.tensor_tensor(wo[1][:, bass.ds(c, 1), :].rearrange("p a n -> p (a n)"), wraw[:],
                                           r32(wo[0][:, bass.ds(c, 1), :]).rearrange("p a n -> p (a n)"), ALU.subtract)\
                            .then_inc(wo_lo, 1)

                W_OUT_STEPS = {20: (0, 0), 28: (0, 1), 32: (0, 2), 50: (1, 0), 60: (1, 1), 64: (1, 2)}
                for s in range(STEPS + 6):
                    n = s - AT_A
                    if 0 <= n < N and n % 2 == 0:
                        w, at = ITEMS[n].width, ITEMS[n].key0
                        pool.wait_ge(left_done, N * i + n + 1 + PRIME)
                        pool.sem_inc(passed, 1)
                        pool.wait_ge(turn_done, N * i + n - 1 + PRIME)
                        pool.sem_inc(passed, 1)
                        pool.tensor_tensor(a_t[0][:, 0:w], beta[n % 3][:, 0:w], strip(n)[:, at + 1:at + w + 1],
                                           ALU.mult).then_inc(a_done[0], 1)
                    for stage in range(3):
                        n = s - AT_O - 1 - stage
                        if group_end(n):
                            outputs(ITEMS[n].group, stage)
                    if s in W_OUT_STEPS:
                        split_w_out(*W_OUT_STEPS[s])
            for b in range(OB):
                pool.wait_ge(stored[b], 32 * G // OB * HEADS // 2)


def mix_norm(nc, ctx, sem, sb, passed, bank, eps_t, xp, xs, mixT_d, wo, ln_g, ln_b, x1_d):
    NX = 4
    xin = [sb(ctx, f"m_x{u}", [P, D]) for u in range(NX)]
    mixT = [sb(ctx, f"m_mixT{u}", [P, 2, KD, P], F32R) for u in range(2)]
    gain, bias = sb(ctx, "m_gain", [P, D]), sb(ctx, "m_bias", [P, D])
    stats = [sb(ctx, f"m_stats{u}", [P, 2, 6]) for u in range(2)]
    mv = [sb(ctx, f"m_mv{u}", [P, 2]) for u in range(2)]
    lnv = [sb(ctx, f"m_lnv{u}", [P, 1]) for u in range(2)]
    rstd = [sb(ctx, f"m_rstd{u}", [P, 1]) for u in range(2)]

    x_loaded = [sem(f"m_x_loaded{u}") for u in range(NX)]
    stored = [sem(f"m_stored{u}") for u in range(NX)]
    mixT_loaded = [sem(f"m_mixT_loaded{u}") for u in range(2)]
    par_loaded = sem("m_par_loaded")
    sums, added, bn, var, lnd, rs, normed, scaled, shifted = (
        sem(f"m_{n}") for n in ("sums", "added", "bn", "var", "ln", "rs", "normed", "scaled", "shifted"))
    LAST = PT

    def slots(eng, f, lag):
        for o in range(2):
            f(0, o)
        with eng.Fori(0, (PT - 4) // NX) as i:
            for o in range(2, 2 + NX):
                f(i, o)
        for o in range(PT - 2, LAST + 1 + lag):
            f(0, o)

    def rows_of(o):
        return DEC if o == LAST else P

    with nc.Block() as block:
        @block.sync
        def _(sp):
            sp.dma_start(gain[:], ln_g.rearrange("(a n) -> a n", a=1).broadcast_to([P, D])).then_inc(par_loaded, 16)
            sp.dma_start(bias[:], ln_b.rearrange("(a n) -> a n", a=1).broadcast_to([P, D])).then_inc(par_loaded, 16)

            def load(i, o):
                t, rows = NX * i + o, rows_of(o)
                sp.wait_ge(sums, 2 * (t - 1) + PRIME)
                sp.sem_inc(passed, 1)
                for j in range(2):
                    sp.dma_start(r32(mixT[o % 2][:, j, :, 0:rows]),
                                 r32(mixT_d[j].rearrange("(k p) t -> p k t", p=P)[:, :, bass.ds(t * P, rows)]))\
                      .then_inc(mixT_loaded[o % 2], 16)
                sp.wait_ge(stored[o % NX], 16 * (i + o // NX))
                sp.sem_inc(passed, 1)
                src = xs if o == LAST else xp[bass.ds(t * P, P), :]
                sp.dma_start(xin[o % NX][0:rows, :], src).then_inc(x_loaded[o % NX], 16)

            slots(sp, load, 0)
            for u in range(NX):
                sp.wait_ge(stored[u], 16 * (PT // NX + (u == LAST % NX)))

        @block.tensor
        def _(pe):
            pe.sem_inc(sums, PRIME)

            def project(i, o):
                t = NX * i + o
                pe.wait_ge(mixT_loaded[o % 2], 32 * (2 * i + o // 2 + 1))
                for half in range(2):
                    pe.wait_ge(added, 2 * (t - 1) + half - 1 + PRIME)
                    for k in range(KD):
                        for n, (a, w) in enumerate(((0, 0), (0, 1), (1, 0))):
                            m = pe.matmul(bank[2 * (o % 2) + half][:], mixT[o % 2][:, a, k, :],
                                          wo[w][:, k, half * 512:half * 512 + 512],
                                          start=k == 0 and n == 0, stop=k == KD - 1 and n == 2)
                    m.then_inc(sums, 1)

            slots(pe, project, 0)

        @block.scalar
        def _(act):
            act.preload_act_table_set("natural_log_exp_and_others")
            act.sem_inc(lnd, PRIME)
            act.sem_inc(rs, PRIME)

            def deviation(i, o):
                t, u = NX * i + o, o % 2
                act.wait_ge(var, t + 1 + PRIME)
                act.activation(lnv[u][:], mv[u][:, 1:2], ACT.Ln, bias=eps_t[:]).then_inc(lnd, 1)
                act.wait_ge(lnd, t + 1 + PRIME)
                act.wait_ge(normed, t - 1 + PRIME)
                act.activation(rstd[u][:], lnv[u][:], ACT.Exp, scale=-0.5).then_inc(rs, 1)

            slots(act, deviation, 0)

        @block.vector
        def _(dve):
            for x in (added, bn, var, normed):
                dve.sem_inc(x, PRIME)

            def statistics(i, o):
                t, u, x = NX * i + o, o % 2, xin[o % NX]
                dve.wait_ge(x_loaded[o % NX], 16 * (i + o // NX + 1))
                for half in range(2):
                    dve.wait_ge(sums, 2 * t + half + 1 + PRIME)
                    at = slice(half * 512, half * 512 + 512)
                    dve.scalar_tensor_tensor(x[:, at], x[:, at], ALPHA, bank[2 * u + half][:], ALU.mult, ALU.add)\
                       .then_inc(added, 1)
                for half in range(2):
                    dve.wait_ge(added, 2 * t + half + 1 + PRIME)
                    dve.bn_stats(stats[u][:, half, :], x[:, half * 512:half * 512 + 512]).then_inc(bn, 1)
                dve.wait_ge(bn, 2 * t + 2 + PRIME)
                dve.sem_inc(passed, 1)
                dve.bn_aggr(mv[u][:], stats[u][:].rearrange("p a b -> p (a b)")).then_inc(var, 1)

            def norm(i, o):
                t, u, x = NX * i + o, o % 2, xin[o % NX]
                dve.wait_ge(rs, t + 1 + PRIME)
                dve.tensor_scalar(x[:], x[:], mv[u][:, 0:1], rstd[u][:, 0:1], ALU.subtract, ALU.mult)\
                   .then_inc(normed, 1)

            def slot(i, o):
                if o <= LAST:
                    statistics(i, o)
                if o >= 1:
                    norm(i, o - 1)

            slots(dve, slot, 1)

        @block.gpsimd
        def _(pool):
            pool.sem_inc(scaled, PRIME)
            pool.sem_inc(shifted, PRIME)
            pool.wait_ge(par_loaded, 32)

            def affine(i, o):
                t, x, rows = NX * i + o, xin[o % NX], rows_of(o)
                pool.wait_ge(normed, t + 1 + PRIME)
                pool.sem_inc(passed, 1)
                pool.tensor_tensor(x[:], x[:], gain[:], ALU.mult).then_inc(scaled, 1)
                pool.wait_ge(scaled, t + 1 + PRIME)
                pool.sem_inc(passed, 1)
                pool.tensor_tensor(x[:], x[:], bias[:], ALU.add).then_inc(shifted, 1)
                pool.wait_ge(shifted, t + 1 + PRIME)
                pool.sem_inc(passed, 1)
                pool.dma_start(x1_d[bass.ds(t * P, rows), :], x[0:rows, :]).then_inc(stored[o % NX], 16)

            slots(pool, affine, 0)


def ffn(nc, ctx, sem, sb, passed, bank, ident, eps_t, x1_d, w_gate, w_up, w_down, ln_g, ln_b, yp, ys):
    NT, TW = 3, 352
    TPB = 3
    TILES = (8, 9)
    XB = 9
    WIDTH = (8 * P, 8 * P + DEC)
    assert NT * TW == WIDTH[1] and TPB * P >= TW and (NT * TPB) == TILES[1]
    x1T = [sb(ctx, f"x1T{j}", [P, KD, WIDTH[1]], F32R) for j in range(2)]
    acc = sb(ctx, "acc", [P, XB, D])
    graw = [sb(ctx, f"graw{j}", [P, KD, P]) for j in range(2)]
    gw = [[[sb(ctx, f"gw{u}{g}{j}", [P, KD, P], F32R) for j in range(2)] for g in range(2)] for u in range(2)]
    draw = sb(ctx, "draw", [P, D])
    dw = [[sb(ctx, f"dw{u}{j}", [P, D], F32R) for j in range(2)] for u in range(2)]
    hT = [[sb(ctx, f"hT{u}{j}", [P, XB * P], F32R) for j in range(2)] for u in range(2)]
    e_t = [sb(ctx, f"fe{b}", [P, TW]) for b in range(2)]
    h_t = [sb(ctx, f"fh{b}", [P, TW]) for b in range(2)]
    y = [sb(ctx, f"y{u}", [P, D]) for u in range(2)]
    gain, bias = sb(ctx, "f_gain", [P, D]), sb(ctx, "f_bias", [P, D])
    stats = [sb(ctx, f"f_stats{u}", [P, 2, 6]) for u in range(2)]
    mv = [sb(ctx, f"f_mv{u}", [P, 2]) for u in range(2)]
    lnv = [sb(ctx, f"f_lnv{u}", [P, 1]) for u in range(2)]
    rstd = [sb(ctx, f"f_rstd{u}", [P, 1]) for u in range(2)]

    def each(n):
        return [sem(f"f{blk}_{n}") for blk in range(2)]

    x_turned, x_hi, x_scaled, x_lo = (each(n) for n in ("x_turned", "x_hi", "x_scaled", "x_lo"))
    x_loaded = [[sem(f"f{blk}_x_loaded{t}") for t in range(TILES[blk])] for blk in range(2)]
    g_loaded, g_hi, g_lo, d_loaded, d_hi, d_lo = (
        each(n) for n in ("g_loaded", "g_hi", "g_lo", "d_loaded", "d_hi", "d_lo"))
    gate_up, sig, silu, prod, h_hi, h_lo = (each(n) for n in ("gate_up", "sig", "silu", "prod", "h_hi", "h_lo"))
    down, summed = each("down"), each("summed")
    bn, var, lnd, rs, normed, scaled, shifted = (
        each(n) for n in ("bn", "var", "ln", "rs", "normed", "scaled", "shifted"))
    y_stored = [sem(f"y_stored{u}") for u in range(2)]
    par_loaded, pad = sem("f_par_loaded"), sem("f_pad")

    def cols(blk, n):
        return slice(n * TW, min((n + 1) * TW, WIDTH[blk]))

    def tiles_of(blk, n):
        return range(TPB * n, min(TPB * (n + 1), TILES[blk]))

    def rows_of(blk, t):
        return DEC if blk and t == XB - 1 else P

    LOOP = FC // 2 - 1
    BEHIND = 3

    with nc.Block() as block:
        @block.sync
        def _(sp):
            def load_gate(blk, f):
                sp.wait_ge(g_lo[blk], f + PRIME)
                sp.sem_inc(passed, 1)
                for j, w in enumerate((w_gate, w_up)):
                    sp.dma_start(graw[j][:], w.rearrange("(k p) f -> p k f", p=P)[:, :, bass.ds(f * P, P)])\
                      .then_inc(g_loaded[blk], 16)

            def load_down(blk, f):
                sp.wait_ge(d_lo[blk], f + PRIME)
                sp.sem_inc(passed, 1)
                sp.dma_start(draw[:], w_down[bass.ds(f * P, P), :]).then_inc(d_loaded[blk], 16)

            def load_x(blk, t):
                rows = rows_of(blk, t)
                if blk and t < TILES[0]:
                    sp.wait_ge(scaled[0], t + 1 + PRIME)
                sp.dma_start(acc[0:rows, t, :], x1_d[(8 * blk + t) * P:(8 * blk + t) * P + rows, :])\
                  .then_inc(x_loaded[blk][t], 16)

            def store(blk, t):
                rows = rows_of(blk, t)
                sp.wait_ge(shifted[blk], t + 1 + PRIME)
                dst = yp[(8 * blk + t) * P:(8 * blk + t + 1) * P, :] if rows == P else ys
                sp.dma_start(dst, y[t % 2][0:rows, :]).then_inc(y_stored[t % 2], 16)

            for blk in range(2):
                if blk:
                    sp.wait_ge(g_lo[0], FC + PRIME)
                    sp.wait_ge(d_lo[0], FC + PRIME)
                load_gate(blk, 0)
                for t in range(TILES[blk] + 1):
                    if t < TILES[blk]:
                        load_x(blk, t)
                    if t == 0:
                        load_gate(blk, 1)
                        load_down(blk, 0)
                    if blk and 1 <= t <= TILES[0]:
                        store(0, t - 1)
                if blk == 0:
                    sp.dma_start(gain[:], ln_g.rearrange("(a n) -> a n", a=1).broadcast_to([P, D])).then_inc(par_loaded, 16)
                    sp.dma_start(bias[:], ln_b.rearrange("(a n) -> a n", a=1).broadcast_to([P, D])).then_inc(par_loaded, 16)
                with sp.Fori(2, FC) as f:
                    load_down(blk, f - 1)
                    load_gate(blk, f)
                load_down(blk, FC - 1)
            for t in range(TILES[1]):
                store(1, t)
            sp.wait_ge(y_stored[0], 16 * (4 + 5))
            sp.wait_ge(y_stored[1], 16 * (4 + 4))

        @block.tensor
        def _(pe):
            def turn(blk, n):
                for t in tiles_of(blk, n):
                    rows = rows_of(blk, t)
                    pe.wait_ge(x_loaded[blk][t], 16)
                    pe.wait_ge(x_lo[blk], t - 1 + PRIME)
                    for k in range(KD):
                        m = pe.transpose(bank[4 + 2 * (t % 2) + k // 4][:, (k % 4) * P:(k % 4) * P + rows],
                                         acc[0:rows, t, k * P:(k + 1) * P], ident[0:rows, 0:rows])
                    m.then_inc(x_turned[blk], 1)

            def gates(blk, f, u, n):
                if n == 0:
                    pe.wait_ge(g_lo[blk], f + 1 + PRIME)
                pe.wait_ge(prod[blk], NT * f + n - 1 + PRIME)
                b, at = (NT * u + n) % 2, cols(blk, n)
                for g in range(2):
                    for k in range(KD):
                        for s, (w, x) in enumerate(((0, 0), (0, 1), (1, 0))):
                            m = pe.matmul(bank[2 * b + g][:, 0:at.stop - at.start], gw[u][g][w][:, k, :],
                                          x1T[x][:, k, at], start=k == 0 and s == 0, stop=k == KD - 1 and s == 2)
                m.then_inc(gate_up[blk], 1)

            def downs(blk, f, u, n):
                ND = 2 * TILES[blk]
                if n == 0:
                    pe.wait_ge(d_lo[blk], f + 1 + PRIME)
                    pe.wait_ge(h_lo[blk], NT * (f + 1) + PRIME)
                for t in tiles_of(blk, n):
                    for half in range(2):
                        d = 2 * t + half
                        pe.wait_ge(summed[blk], ND * f + d - 3 + PRIME)
                        for s, (a, w) in enumerate(((0, 0), (0, 1), (1, 0))):
                            m = pe.matmul(bank[4 + (ND * u + d) % 4][:], hT[u][a][:, t * P:(t + 1) * P],
                                          dw[u][w][:, half * 512:half * 512 + 512], start=s == 0, stop=s == 2)
                        m.then_inc(down[blk], 1)

            for x in (*x_turned, *gate_up, *down):
                pe.sem_inc(x, PRIME)
            pe.wait_ge(pad, 4)
            for blk in range(2):
                if blk:
                    pe.wait_ge(prod[0], NT * FC + PRIME)
                    pe.wait_ge(summed[0], 2 * TILES[0] * FC + PRIME)
                for n in range(NT):
                    turn(blk, n)
                    pe.wait_ge(x_lo[blk], tiles_of(blk, n).stop + PRIME)
                    gates(blk, 0, 0, n)
                with pe.Fori(0, LOOP) as i:
                    for v in range(2):
                        for n in range(NT):
                            gates(blk, 2 * i + v + 1, 1 - v, n)
                            downs(blk, 2 * i + v, v, n)
                for n in range(NT):
                    gates(blk, FC - 1, 1, n)
                    downs(blk, FC - 2, 0, n)
                for n in range(NT):
                    downs(blk, FC - 1, 1, n)

        def turned_tile(blk, t):
            rows = rows_of(blk, t)
            return [(bank[4 + 2 * (t % 2) + b][:, :].rearrange("p (k n) -> p k n", k=4)[:, :, 0:rows],
                     (slice(None), slice(4 * b, 4 * b + 4), slice(t * P, t * P + rows))) for b in range(2)]

        @block.scalar
        def _(act):
            for x in (*x_hi, *x_scaled, *g_hi, *d_hi, *sig, *h_hi, *lnd, *rs, *normed):
                act.sem_inc(x, PRIME)

            def split_gate(blk, f, u):
                act.wait_ge(g_loaded[blk], 32 * f + 32)
                act.wait_ge(gate_up[blk], NT * (f - 1) + PRIME)
                act.activation(gw[u][0][0][:], graw[0][:], ACT.Copy)
                act.activation(gw[u][1][0][:], graw[1][:], ACT.Copy).then_inc(g_hi[blk], 1)

            def split_down(blk, f, u):
                act.wait_ge(d_loaded[blk], 16 * f + 16)
                act.wait_ge(down[blk], 2 * TILES[blk] * (f - 1) + PRIME)
                act.activation(dw[u][0][:], draw[:], ACT.Copy).then_inc(d_hi[blk], 1)

            def sigmoid(blk, f, u, n):
                b, at = (NT * u + n) % 2, cols(blk, n)
                w = at.stop - at.start
                act.wait_ge(gate_up[blk], NT * f + n + 1 + PRIME)
                act.wait_ge(silu[blk], NT * f + n - 1 + PRIME)
                act.activation(e_t[b][:, 0:w], bank[2 * b][:, 0:w], ACT.Sigmoid).then_inc(sig[blk], 1)

            def hidden(blk, f, u, n):
                b, at = (NT * u + n) % 2, cols(blk, n)
                act.wait_ge(prod[blk], NT * f + n + 1 + PRIME)
                act.wait_ge(down[blk], 2 * TILES[blk] * (f - 1) + PRIME)
                act.activation(hT[u][0][:, at], h_t[b][:, 0:at.stop - at.start], ACT.Copy).then_inc(h_hi[blk], 1)

            def chunk(blk, f, u, more=True):
                for n in range(NT):
                    sigmoid(blk, f, u, n)
                    if n == 0:
                        split_down(blk, f, u)
                    hidden(blk, f, u, n)
                if more:
                    split_gate(blk, f + 2, u)

            def deviation(blk, t):
                act.wait_ge(var[blk], t + 1 + PRIME)
                act.activation(lnv[t % 2][:], mv[t % 2][:, 1:2], ACT.Ln, bias=eps_t[:]).then_inc(lnd[blk], 1)
                act.wait_ge(lnd[blk], t + 1 + PRIME)
                act.activation(rstd[t % 2][:], lnv[t % 2][:], ACT.Exp, scale=-0.5).then_inc(rs[blk], 1)
                act.wait_ge(rs[blk], t + 1 + PRIME)
                act.wait_ge(scaled[blk], t + 1 + PRIME)
                r = slice(0, rows_of(blk, t))
                act.activation(y[t % 2][r, :], y[t % 2][r, :], ACT.Copy, scale=rstd[t % 2][r, 0:1])\
                   .then_inc(normed[blk], 1)

            def hi_of_x(blk, t):
                act.wait_ge(x_turned[blk], t + 1 + PRIME)
                for src, at in turned_tile(blk, t):
                    m = act.activation(x1T[0][at], src, ACT.Copy)
                m.then_inc(x_hi[blk], 1)
                x = acc[0:rows_of(blk, t), t, :]
                act.activation(x, x, ACT.Copy, scale=ALPHA).then_inc(x_scaled[blk], 1)

            for blk in range(2):
                if blk:
                    act.preload_act_table_set("natural_log_exp_and_others")
                    act.wait_ge(gate_up[0], NT * FC + PRIME)
                split_gate(blk, 0, 0)
                for t in range(TILES[blk] + BEHIND * blk):
                    if t == 2:
                        split_gate(blk, 1, 1)
                    if blk and t < TILES[0]:
                        deviation(0, t)
                    if t - BEHIND * blk >= 0:
                        hi_of_x(blk, t - BEHIND * blk)
                if blk:
                    act.wait_ge(silu[0], NT * FC + PRIME)
                    act.wait_ge(down[0], 2 * TILES[0] * FC + PRIME)
                with act.Fori(0, LOOP) as i:
                    chunk(blk, 2 * i, 0)
                    chunk(blk, 2 * i + 1, 1)
                chunk(blk, FC - 2, 0, False)
                chunk(blk, FC - 1, 1, False)
            act.preload_act_table_set("natural_log_exp_and_others")
            for t in range(TILES[1]):
                deviation(1, t)

        @block.vector
        def _(dve):
            for x in (*x_lo, *g_lo, *d_lo, *silu, *prod, *h_lo, *summed, *bn, *var, *scaled):
                dve.sem_inc(x, PRIME)
            for u in range(2):
                for j in range(2):
                    dve.memset(r32(hT[u][j][:, WIDTH[1]:XB * P]), 0.0).then_inc(pad, 1)

            def split_gate(blk, f, u):
                dve.wait_ge(g_hi[blk], f + 1 + PRIME)
                dve.tensor_tensor(gw[u][0][1][:], graw[0][:], r32(gw[u][0][0][:]), ALU.subtract)
                dve.tensor_tensor(gw[u][1][1][:], graw[1][:], r32(gw[u][1][0][:]), ALU.subtract)\
                   .then_inc(g_lo[blk], 1)

            def split_down(blk, f, u):
                dve.wait_ge(d_hi[blk], f + 1 + PRIME)
                dve.tensor_tensor(dw[u][1][:], draw[:], r32(dw[u][0][:]), ALU.subtract).then_inc(d_lo[blk], 1)

            def hidden(blk, f, u, n):
                b, at = (NT * u + n) % 2, cols(blk, n)
                w = at.stop - at.start
                e, h = e_t[b][:, 0:w], h_t[b][:, 0:w]
                if n == 0:
                    split_down(blk, f, u)
                dve.wait_ge(sig[blk], NT * f + n + 1 + PRIME)
                dve.wait_ge(h_hi[blk], NT * f + n - 1 + PRIME)
                dve.wait_ge(h_lo[blk], NT * f + n - 1 + PRIME)
                dve.tensor_tensor(h, bank[2 * b][:, 0:w], e, ALU.mult).then_inc(silu[blk], 1)
                dve.wait_ge(silu[blk], NT * f + n + 1 + PRIME)
                dve.tensor_tensor(h, bank[2 * b + 1][:, 0:w], h, ALU.mult).then_inc(prod[blk], 1)
                dve.wait_ge(h_hi[blk], NT * f + n + 1 + PRIME)
                dve.tensor_tensor(hT[u][1][:, at], h, r32(hT[u][0][:, at]), ALU.subtract).then_inc(h_lo[blk], 1)

            def sums(blk, f, u, n):
                for t in tiles_of(blk, n):
                    sum_of_tile(blk, f, u, t)

            def sum_of_tile(blk, f, u, t):
                ND = 2 * TILES[blk]
                for half in range(2):
                    d = 2 * t + half
                    dve.wait_ge(down[blk], ND * f + d + 1 + PRIME)
                    dve.wait_ge(summed[blk], ND * (f - 1) + d + 1 + PRIME)
                    rows = rows_of(blk, t)
                    s = acc[0:rows, t, half * 512:half * 512 + 512]
                    dve.tensor_tensor(s, bank[4 + (ND * u + d) % 4][0:rows, :], s, ALU.add).then_inc(summed[blk], 1)

            def norm(blk, t):
                u, rows = t % 2, rows_of(blk, t)
                dve.wait_ge(summed[blk], 2 * TILES[blk] * (FC - 1) + 2 * t + 2 + PRIME)
                for half in range(2):
                    m = dve.bn_stats(stats[u][0:rows, half, :], acc[0:rows, t, half * 512:half * 512 + 512])
                m.then_inc(bn[blk], 1)
                dve.wait_ge(bn[blk], t + 1 + PRIME)
                if t >= 2:
                    dve.wait_ge(normed[blk], t - 1 + PRIME)
                dve.sem_inc(passed, 1)
                dve.bn_aggr(mv[u][0:rows], stats[u][0:rows].rearrange("p a b -> p (a b)")).then_inc(var[blk], 1)
                dve.wait_ge(var[blk], t + 1 + PRIME)
                uses = t // 2 + (0 if blk == 0 else 4)
                if uses:
                    dve.wait_ge(y_stored[u], 16 * uses)
                r = slice(0, rows)
                dve.scalar_tensor_tensor(y[u][r, :], acc[r, t, :], mv[u][r, 0:1], gain[r, :], ALU.subtract, ALU.mult)\
                   .then_inc(scaled[blk], 1)

            def lo_of_x(blk, t):
                dve.wait_ge(x_hi[blk], t + 1 + PRIME)
                for src, at in turned_tile(blk, t):
                    m = dve.tensor_tensor(x1T[1][at], src, r32(x1T[0][at]), ALU.subtract)
                m.then_inc(x_lo[blk], 1)

            for blk in range(2):
                split_gate(blk, 0, 0)
                for t in range(TILES[blk] + BEHIND * blk):
                    if t == 2:
                        split_gate(blk, 1, 1)
                    if blk and t < TILES[0]:
                        norm(0, t)
                    if t - BEHIND * blk >= 0:
                        lo_of_x(blk, t - BEHIND * blk)
                for n in range(NT):
                    hidden(blk, 0, 0, n)
                if blk == 0:
                    dve.wait_ge(par_loaded, 32)
                dve.wait_ge(x_scaled[blk], TILES[blk] + PRIME)
                with dve.Fori(0, LOOP) as i:
                    for v in range(2):
                        split_gate(blk, 2 * i + v + 2, v)
                        for n in range(NT):
                            sums(blk, 2 * i + v, v, n)
                            hidden(blk, 2 * i + v + 1, 1 - v, n)
                for n in range(NT):
                    sums(blk, FC - 2, 0, n)
                    hidden(blk, FC - 1, 1, n)
                if blk == 0:
                    for n in range(NT):
                        sums(blk, FC - 1, 1, n)
            for t in range(TILES[1]):
                sum_of_tile(1, FC - 1, 1, t)
                norm(1, t)

        @block.gpsimd
        def _(pool):
            for x in shifted:
                pool.sem_inc(x, PRIME)
            pool.wait_ge(par_loaded, 32)
            for blk in range(2):
                for t in range(TILES[blk]):
                    u = t % 2
                    pool.wait_ge(normed[blk], t + 1 + PRIME)
                    r = slice(0, rows_of(blk, t))
                    pool.tensor_tensor(y[u][r, :], y[u][r, :], bias[r, :], ALU.add).then_inc(shifted[blk], 1)


_INS = ["x_prompt", "x_sample", "cache_k", "cache_v", "state_pool", "w_in", "pool_w", "pool_scale", "w_out",
        "ln1_g", "ln1_b", "w_gate", "w_up", "w_down", "ln2_g", "ln2_b"]
_OUTS = [(1, SEQ, D), (1, DEC, D), (1, SEQ, HEADS, HD), (1, SEQ, HEADS, HD), (1, HIST, SBW),
         (1, DEC, HEADS, HD), (1, DEC, HEADS, HD), (1, HIST, SBW)]


def kernel(**inputs):
    import numpy as _np
    import concourse.bacc as _bacc
    from concourse import mybir as _mybir
    from concourse.bass_utils import run_bass_kernel_spmd as _run

    nc = _bacc.Bacc("TRN2", target_bir_lowering=False, num_devices=1)
    arrays, args = {}, []
    for name in _INS:
        a = _np.ascontiguousarray(inputs[name])
        arrays[f"in_{name}_dram"] = a
        args.append(nc.dram_tensor(f"in_{name}_dram", a.shape, _mybir.dt.from_np(a.dtype), kind="ExternalInput").ap())
    for i, shape in enumerate(_OUTS):
        args.append(nc.dram_tensor(f"out_{i}_dram", shape, _mybir.dt.float32, kind="ExternalOutput").ap())
    build(nc, *args)
    r = _run(nc, [arrays], core_ids=[0])
    return tuple(r.results[0][f"out_{i}_dram"] for i in range(len(_OUTS)))
```
